# Optimizing a Trainium2 kernel written in Bass

```python
import math
import jax, jax.numpy as jnp
from jax import lax
import numpy as np
import jax
import jax.numpy as jnp

D_MODEL = 1024
BATCH = 1
SEQ = 256
DEPTH = 2

GRID_W = 64
N_Q_HEADS = 8
N_KV_HEADS = 2
HEAD_DIM = 64
Q_BLOCK = 128
ROPE_THETA = 10000.0
ATTN_WIDTH = N_Q_HEADS * HEAD_DIM
KV_WIDTH = N_KV_HEADS * HEAD_DIM
SGU_GROUPS = 8
SGU_WIDTH = 512
SGU_GROUP_DIM = SGU_WIDTH // SGU_GROUPS
SGU_CHUNK = 128
Q_END = ATTN_WIDTH
K_END = Q_END + KV_WIDTH
V_END = K_END + KV_WIDTH
Z_END = V_END + 2 * SGU_WIDTH
GA_END = Z_END + D_MODEL
IN_COLS = GA_END + D_MODEL
N_EXPERTS = 64
TOP_K = 8
N_GROUPS = 8
TOPK_GROUPS = 4
EXPERT_FF = 256
SHARED_FF = 256
ROUTED_SCALE = 2.5
MOE_BLOCK = 128
ALPHA = (2 * DEPTH) ** 0.25
BETA = (8 * DEPTH) ** -0.25


def layer_norm(x, g, b, eps=1e-5):
    xf = x.astype(jnp.float32)
    mu = jnp.mean(xf, -1, keepdims=True)
    var = jnp.mean(jnp.square(xf - mu), -1, keepdims=True)
    return ((xf - mu) * lax.rsqrt(var + eps)).astype(x.dtype) * g + b

def rms_norm(x, g, eps=1e-6):
    xf = x.astype(jnp.float32)
    return (xf * lax.rsqrt(jnp.mean(jnp.square(xf), -1, keepdims=True) + eps)).astype(x.dtype) * g

def axial_rope_tables(seq_len, rows):
    t = jnp.arange(seq_len)
    row = (t // GRID_W - rows // 2).astype(jnp.float32)
    col = (t % GRID_W - GRID_W // 2).astype(jnp.float32)
    n_pairs = HEAD_DIM // 4
    inv_freq = ROPE_THETA ** (-jnp.arange(n_pairs, dtype=jnp.float32) / n_pairs)
    ang = jnp.concatenate([row[:, None] * inv_freq, col[:, None] * inv_freq], -1)
    return jnp.cos(ang), jnp.sin(ang)

def apply_rope(x, cos, sin):
    xf = x.astype(jnp.float32).reshape(*x.shape[:-1], HEAD_DIM // 2, 2)
    x0, x1 = xf[..., 0], xf[..., 1]
    c = cos[None, :, None, :]
    s = sin[None, :, None, :]
    out = jnp.stack([x0 * c - x1 * s, x0 * s + x1 * c], -1)
    return out.reshape(x.shape).astype(x.dtype)

def attention_branch(q, k, v, q_scale, k_scale, cos, sin):
    B, S = q.shape[:2]
    grp = N_Q_HEADS // N_KV_HEADS
    q = apply_rope(rms_norm(q, q_scale), cos, sin)
    k = apply_rope(rms_norm(k, k_scale), cos, sin)
    nqb = S // Q_BLOCK
    qb = q.reshape(B, nqb, Q_BLOCK, N_KV_HEADS, grp, HEAD_DIM).transpose(1, 0, 3, 4, 2, 5)
    kt = k.transpose(0, 2, 1, 3)
    vt = v.transpose(0, 2, 1, 3)
    scale = HEAD_DIM ** -0.5

    def attend(q_blk):
        s = jnp.einsum('bkgqd,bksd->bkgqs', q_blk, kt).astype(jnp.float32) * scale
        p = jax.nn.softmax(s, axis=-1).astype(vt.dtype)
        return jnp.einsum('bkgqs,bksd->bkgqd', p, vt)

    o = lax.map(attend, qb)
    return o.transpose(1, 0, 4, 2, 3, 5).reshape(B, S, ATTN_WIDTH)

def spatial_gating_branch(z, ln_g, ln_b, w_s, b_s):
    B, S, _ = z.shape
    z = jax.nn.gelu(z, approximate=False)
    u, v = z[..., :SGU_WIDTH], z[..., SGU_WIDTH:]
    v = layer_norm(v, ln_g, ln_b)
    vc = v.reshape(B, S // SGU_CHUNK, SGU_CHUNK, SGU_GROUPS, SGU_GROUP_DIM)
    sv = jnp.einsum('gij,bnjgd->bnigd', w_s, vc) + b_s.T[:, :, None]
    return u * sv.reshape(B, S, SGU_WIDTH)

def token_mixer(h, w_in, q_scale, k_scale, sgu_ln_g, sgu_ln_b, w_s, b_s, w_branch_a, w_branch_b, w_out, cos, sin):
    B, S, _ = h.shape
    p = h @ w_in
    q = p[..., :Q_END].reshape(B, S, N_Q_HEADS, HEAD_DIM)
    k = p[..., Q_END:K_END].reshape(B, S, N_KV_HEADS, HEAD_DIM)
    v = p[..., K_END:V_END].reshape(B, S, N_KV_HEADS, HEAD_DIM)
    z = p[..., V_END:Z_END]
    gate_a = p[..., Z_END:GA_END]
    gate_b = p[..., GA_END:]
    o_a = attention_branch(q, k, v, q_scale, k_scale, cos, sin)
    o_b = spatial_gating_branch(z, sgu_ln_g, sgu_ln_b, w_s, b_s)
    y = jax.nn.sigmoid(gate_a) * (o_a @ w_branch_a) + jax.nn.sigmoid(gate_b) * (o_b @ w_branch_b)
    return y @ w_out

def moe_ffn(h, router_w, router_bias, w_gate, w_up, w_down, ws_gate, ws_up, ws_down):
    B, S, D = h.shape
    T = B * S
    xt = h.reshape(T, D)
    scores = jax.nn.sigmoid((xt @ router_w).astype(jnp.float32))
    sel = scores + router_bias.astype(jnp.float32)
    per_group = N_EXPERTS // N_GROUPS
    group_score = lax.top_k(sel.reshape(T, N_GROUPS, per_group), 2)[0].sum(-1)
    _, gidx = lax.top_k(group_score, TOPK_GROUPS)
    gmask = jnp.any(gidx[..., None] == jnp.arange(N_GROUPS), axis=-2)
    emask = jnp.repeat(gmask, per_group, axis=-1)
    _, eidx = lax.top_k(jnp.where(emask, sel, -jnp.inf), TOP_K)
    wts = jnp.take_along_axis(scores, eidx, -1)
    wts = wts / jnp.sum(wts, -1, keepdims=True) * ROUTED_SCALE
    A = T * TOP_K
    e_flat = eidx.reshape(A)
    t_flat = jnp.repeat(jnp.arange(T, dtype=jnp.int32), TOP_K)
    w_flat = wts.reshape(A)
    order = jnp.argsort(e_flat)
    e_s, t_s, w_s = e_flat[order], t_flat[order], w_flat[order]
    counts = jnp.bincount(e_flat, length=N_EXPERTS)
    starts = jnp.cumsum(counts) - counts
    padded = (counts + MOE_BLOCK - 1) // MOE_BLOCK * MOE_BLOCK
    pends = jnp.cumsum(padded)
    pstarts = pends - padded
    dest = pstarts[e_s] + (jnp.arange(A) - starts[e_s])
    n_blocks = A // MOE_BLOCK + N_EXPERTS
    P = n_blocks * MOE_BLOCK
    tok_buf = jnp.full((P,), T, jnp.int32).at[dest].set(t_s.astype(jnp.int32))
    w_buf = jnp.zeros((P,), xt.dtype).at[dest].set(w_s.astype(xt.dtype))
    blk_expert = jnp.minimum(jnp.searchsorted(pends, jnp.arange(n_blocks) * MOE_BLOCK, side='right'), N_EXPERTS - 1)
    x_pad = jnp.concatenate([xt, jnp.zeros((1, D), xt.dtype)], 0)

    def run_block(args):
        e, toks, ws = args
        xb = x_pad[toks]
        hb = jax.nn.silu(xb @ w_gate[e]) * (xb @ w_up[e])
        return (hb @ w_down[e]) * ws[:, None]

    yb = lax.map(run_block, (blk_expert, tok_buf.reshape(n_blocks, MOE_BLOCK), w_buf.reshape(n_blocks, MOE_BLOCK)))
    routed = jax.ops.segment_sum(yb.reshape(P, D), tok_buf, num_segments=T + 1)[:T]
    shared = (jax.nn.silu(xt @ ws_gate) * (xt @ ws_up)) @ ws_down
    return (routed + shared).reshape(B, S, D)

def first_inputs(seed: int = 0) -> dict:
    key = jax.random.key(seed)
    ks = jax.random.split(key, 26)
    L, D, E = DEPTH, D_MODEL, N_EXPERTS
    f32 = jnp.float32

    def nrm(k, shape, s):
        return jax.random.normal(k, shape, f32) * s

    def gain(k, shape):
        return 1.0 + 0.02 * jax.random.normal(k, shape, f32)

    w_in = nrm(ks[4], (L, D, IN_COLS), D ** -0.5)
    w_in = w_in.at[:, :, K_END:V_END].multiply(BETA)
    return {
        'x': nrm(ks[0], (BATCH, SEQ, D), 1.0),
        'c': nrm(ks[1], (BATCH, D), 1.0),
        'w_ada': nrm(ks[2], (L, D, 6 * D), 0.5 * D ** -0.5),
        'b_ada': nrm(ks[3], (L, 6 * D), 0.02),
        'w_in': w_in,
        'q_scale': gain(ks[5], (L, HEAD_DIM)),
        'k_scale': gain(ks[6], (L, HEAD_DIM)),
        'sgu_ln_g': gain(ks[7], (L, SGU_WIDTH)),
        'sgu_ln_b': nrm(ks[8], (L, SGU_WIDTH), 0.02),
        'w_spatial': nrm(ks[9], (L, SGU_GROUPS, SGU_CHUNK, SGU_CHUNK), SGU_CHUNK ** -0.5),
        'b_spatial': nrm(ks[10], (L, SGU_GROUPS, SGU_CHUNK), 0.02),
        'w_branch_a': nrm(ks[11], (L, ATTN_WIDTH, D), ATTN_WIDTH ** -0.5),
        'w_branch_b': nrm(ks[12], (L, SGU_WIDTH, D), SGU_WIDTH ** -0.5),
        'w_out': nrm(ks[13], (L, D, D), BETA * D ** -0.5),
        'ln1_g': gain(ks[14], (L, D)),
        'ln1_b': nrm(ks[15], (L, D), 0.02),
        'router_w': nrm(ks[16], (L, D, E), D ** -0.5),
        'router_bias': nrm(ks[17], (L, E), 0.01),
        'w_gate': nrm(ks[18], (L, E, D, EXPERT_FF), D ** -0.5),
        'w_up': nrm(ks[19], (L, E, D, EXPERT_FF), D ** -0.5),
        'w_down': nrm(ks[20], (L, E, EXPERT_FF, D), BETA * EXPERT_FF ** -0.5),
        'ws_gate': nrm(ks[21], (L, D, SHARED_FF), D ** -0.5),
        'ws_up': nrm(ks[22], (L, D, SHARED_FF), D ** -0.5),
        'ws_down': nrm(ks[23], (L, SHARED_FF, D), BETA * SHARED_FF ** -0.5),
        'ln2_g': gain(ks[24], (L, D)),
        'ln2_b': nrm(ks[25], (L, D), 0.02),
    }

def first_block(x, c, w_ada, b_ada, w_in, q_scale, k_scale, sgu_ln_g, sgu_ln_b, w_spatial, b_spatial,
              w_branch_a, w_branch_b, w_out, ln1_g, ln1_b, router_w, router_bias, w_gate, w_up, w_down,
              ws_gate, ws_up, ws_down, ln2_g, ln2_b):
    B, S, D = x.shape
    rows = S // GRID_W
    cos, sin = axial_rope_tables(S, rows)
    cond = jax.nn.silu(c)
    for l in range(DEPTH):
        mod = cond @ w_ada[l] + b_ada[l]
        shift1, scale1, gate1, shift2, scale2, gate2 = jnp.split(mod[:, None, :], 6, axis=-1)
        h = x * (1 + scale1) + shift1
        y = token_mixer(h, w_in[l], q_scale[l], k_scale[l], sgu_ln_g[l], sgu_ln_b[l], w_spatial[l], b_spatial[l],
                        w_branch_a[l], w_branch_b[l], w_out[l], cos, sin)
        x = layer_norm(ALPHA * x + gate1 * y, ln1_g[l], ln1_b[l])
        h = x * (1 + scale2) + shift2
        y = moe_ffn(h, router_w[l], router_bias[l], w_gate[l], w_up[l], w_down[l], ws_gate[l], ws_up[l], ws_down[l])
        x = layer_norm(ALPHA * x + gate2 * y, ln2_g[l], ln2_b[l])
    return x


CTX_LEN = 256
N_MIXERS = 2
N_ATT = (DEPTH + 1) // 2
N_RWKV = DEPTH // 2
ATT_Q_HEADS = D_MODEL // HEAD_DIM
ATT_KV_HEADS = ATT_Q_HEADS // 4
ATT_GROUP = ATT_Q_HEADS // ATT_KV_HEADS
WINDOW = 128
BLOCK = 128
ROPE_BASE = 10000.0
RWKV_HEADS = D_MODEL // HEAD_DIM
DECAY_LORA = 64
ICLR_LORA = 64
GATE_LORA = 128
D_FF = 4 * D_MODEL
NORM_EPS = 1e-6
GN_EPS = 64e-5
NEG_INF = -1e30
F32 = jnp.float32


def rmsnorm(x, g):
    x32 = x.astype(F32)
    y = x32 * lax.rsqrt(jnp.mean(x32 * x32, axis=-1, keepdims=True) + NORM_EPS)
    return (y * g.astype(F32)).astype(x.dtype)

def rope_1d(t, pos):
    half = t.shape[-1] // 2
    freqs = ROPE_BASE ** (-jnp.arange(half, dtype=F32) / half)
    ang = pos.astype(F32)[:, None, None] * freqs
    cos, sin = jnp.cos(ang), jnp.sin(ang)
    t1, t2 = t[..., :half].astype(F32), t[..., half:].astype(F32)
    return jnp.concatenate([t1 * cos - t2 * sin, t1 * sin + t2 * cos], axis=-1).astype(t.dtype)

def rope_2d(t, rows, cols):
    r = HEAD_DIM // 2
    return jnp.concatenate([rope_1d(t[..., :r], rows), rope_1d(t[..., r:], cols)], axis=-1)

def sq_relu_mlp(h, w1, w2):
    return jnp.square(jax.nn.relu(h @ w1)) @ w2

def attention_mixer(h, hc, w_qkv, q_gain, k_gain, sink, w_o, rows, cols, ctx_out):
    B, S, _ = h.shape
    L = hc.shape[1]
    nq, nk = ATT_Q_HEADS * HEAD_DIM, ATT_KV_HEADS * HEAD_DIM

    def project(t):
        T = t.shape[1]
        qkv = t @ w_qkv
        q = rmsnorm(qkv[..., :nq].reshape(B, T, ATT_Q_HEADS, HEAD_DIM), q_gain)
        k = rmsnorm(qkv[..., nq:nq + nk].reshape(B, T, ATT_KV_HEADS, HEAD_DIM), k_gain)
        v = qkv[..., nq + nk:].reshape(B, T, ATT_KV_HEADS, HEAD_DIM)
        return q, k, v

    q, k, v = project(h)
    q, k = rope_2d(q, rows, cols), rope_2d(k, rows, cols)
    qc, kc, vc = project(hc)
    scale = HEAD_DIM ** -0.5
    sink_logit = sink.astype(F32).reshape(ATT_KV_HEADS, ATT_GROUP, 1, 1)

    nb = S // BLOCK
    qb = q.reshape(B, nb, BLOCK, ATT_KV_HEADS, ATT_GROUP, HEAD_DIM)

    def band(t):
        tp = jnp.pad(t, ((0, 0), (BLOCK, BLOCK), (0, 0), (0, 0))).reshape(B, nb + 2, BLOCK, ATT_KV_HEADS, HEAD_DIM)
        return jnp.concatenate([tp[:, :-2], tp[:, 1:-1], tp[:, 2:]], axis=2)

    kw, vw = band(k), band(v)
    s_win = jnp.einsum('bnqhgd,bnkhd->bnhgqk', qb, kw).astype(F32) * scale
    s_ctx = jnp.einsum('bnqhgd,blhd->bnhgql', qb, kc).astype(F32) * scale
    blk = jnp.arange(nb)[:, None, None] * BLOCK
    qpos = blk + jnp.arange(BLOCK)[None, :, None]
    kpos = blk - BLOCK + jnp.arange(3 * BLOCK)[None, None, :]
    mask = (jnp.abs(kpos - qpos) <= WINDOW) & (kpos >= 0) & (kpos < S)
    s_win = jnp.where(mask[None, :, None, None], s_win, NEG_INF)
    sinks = jnp.broadcast_to(sink_logit, s_win.shape[:-1] + (1,))
    p = jax.nn.softmax(jnp.concatenate([s_win, s_ctx, sinks], axis=-1), axis=-1)
    p_win = p[..., :3 * BLOCK].astype(v.dtype)
    p_ctx = p[..., 3 * BLOCK:3 * BLOCK + L].astype(v.dtype)
    o = jnp.einsum('bnhgqk,bnkhd->bnqhgd', p_win, vw) + jnp.einsum('bnhgql,blhd->bnqhgd', p_ctx, vc)
    y = o.reshape(B, S, D_MODEL) @ w_o
    if not ctx_out:
        return y, None

    qcg = qc.reshape(B, L, ATT_KV_HEADS, ATT_GROUP, HEAD_DIM)
    s_cc = jnp.einsum('blhgd,bmhd->bhglm', qcg, kc).astype(F32) * scale
    sinks_c = jnp.broadcast_to(sink_logit, s_cc.shape[:-1] + (1,))
    pc = jax.nn.softmax(jnp.concatenate([s_cc, sinks_c], axis=-1), axis=-1)[..., :L].astype(vc.dtype)
    yc = jnp.einsum('bhglm,bmhd->blhgd', pc, vc).reshape(B, L, D_MODEL) @ w_o
    return y, yc

def wkv_scan(r, w, k, v, a, b, s0, reverse):
    def step(s, inp):
        r_t, w_t, k_t, v_t, a_t, b_t = inp
        sa = jnp.einsum('bhvk,bhk->bhv', s, a_t)
        s = s * w_t[:, :, None, :] + sa[..., None] * b_t[:, :, None, :] + v_t[..., None] * k_t[:, :, None, :]
        return s, jnp.einsum('bhvk,bhk->bhv', s, r_t)

    xs = tuple(jnp.moveaxis(t, 1, 0) for t in (r, w, k, v, a, b))
    s_final, ys = lax.scan(step, s0, xs, reverse=reverse)
    return s_final, jnp.moveaxis(ys, 0, 1)

def rwkv_features(h, mu, w_rkv, w0, w1, w2, a0, a1, a2, k_k, k_a):
    B, T, _ = h.shape
    hn = (RWKV_HEADS, HEAD_DIM)
    hp = jnp.pad(h, ((0, 0), (1, 1), (0, 0)))
    xx = 0.5 * (hp[:, :-2] + hp[:, 2:]) - h
    xr, xw, xk, xv, xa, xg = [h + xx * mu[m] for m in range(6)]

    def heads(t):
        return t.astype(F32).reshape(B, T, *hn)

    r = heads(xr @ w_rkv[0])
    k = heads(xk @ w_rkv[1])
    v = heads(xv @ w_rkv[2])
    decay = tuple(
        heads(jnp.exp(-jnp.exp(-jax.nn.softplus(-(w0[d] + jnp.tanh(xw @ w1[d]) @ w2[d]).astype(F32)) - 0.5)))
        for d in range(2))
    a = heads(jax.nn.sigmoid((a0 + (xa @ a1) @ a2).astype(F32)))
    kk = k * k_k.astype(F32).reshape(hn)
    kk = kk / jnp.maximum(jnp.sqrt(jnp.sum(kk * kk, axis=-1, keepdims=True)), 1e-12)
    k = k * (1.0 + (a - 1.0) * k_a.astype(F32).reshape(hn))
    return r, k, v, -kk, kk * a, decay, xg

def group_norm(y, g, b):
    hn = (RWKV_HEADS, HEAD_DIM)
    mean = jnp.mean(y, axis=-1, keepdims=True)
    var = jnp.mean(jnp.square(y - mean), axis=-1, keepdims=True)
    return (y - mean) * lax.rsqrt(var + GN_EPS) * g.astype(F32).reshape(hn) + b.astype(F32).reshape(hn)

def rwkv_readout(y_fwd, y_bwd, r, k, v, xg, g1, g2, r_k, gn_g, gn_b, w_o):
    B, T = xg.shape[:2]
    bonus = jnp.sum(r * k * r_k.astype(F32), axis=-1, keepdims=True) * v

    def gate(d):
        return (jax.nn.sigmoid(xg @ g1[d]) @ g2[d]).astype(F32).reshape(B, T, RWKV_HEADS, HEAD_DIM)

    o = (group_norm(y_fwd, gn_g, gn_b) + bonus) * gate(0) + (group_norm(y_bwd, gn_g, gn_b) + bonus) * gate(1)
    return o.reshape(B, T, D_MODEL).astype(xg.dtype) @ w_o

def rwkv_mixer(h, hc, mu, w_rkv, w0, w1, w2, a0, a1, a2, g1, g2, k_k, k_a, r_k, gn_g, gn_b, w_o, ctx_out):
    feat = (mu, w_rkv, w0, w1, w2, a0, a1, a2, k_k, k_a)
    rc, kc, vc, nac, bc, decc, xgc = rwkv_features(hc, *feat)
    r, k, v, na, b, dec, xg = rwkv_features(h, *feat)
    zero = jnp.zeros((h.shape[0], RWKV_HEADS, HEAD_DIM, HEAD_DIM), F32)
    s_fwd, yc_fwd = wkv_scan(rc, decc[0], kc, vc, nac, bc, zero, False)
    s_bwd, yc_bwd = wkv_scan(rc, decc[1], kc, vc, nac, bc, zero, True)
    _, y_fwd = wkv_scan(r, dec[0], k, v, na, b, s_fwd, False)
    _, y_bwd = wkv_scan(r, dec[1], k, v, na, b, s_bwd, True)
    ro = (g1, g2, r_k, gn_g, gn_b, w_o)
    y = rwkv_readout(y_fwd, y_bwd, r, k, v, xg, *ro)
    if not ctx_out:
        return y, None
    return y, rwkv_readout(yc_fwd, yc_bwd, rc, kc, vc, xgc, *ro)

def second_inputs(seed: int = 0) -> dict:
    key = jax.random.key(seed)
    ks = iter(jax.random.split(key, 40))
    D = D_MODEL

    def nrm(shape, s):
        return jax.random.normal(next(ks), shape, F32) * s

    def unif(shape, lo, hi):
        return jax.random.uniform(next(ks), shape, F32, lo, hi)

    qkv_cols = (ATT_Q_HEADS + 2 * ATT_KV_HEADS) * HEAD_DIM
    return {
        'x': nrm((BATCH, SEQ, D), 1.0),
        'c': nrm((BATCH, D), 1.0),
        'ctx': nrm((BATCH, CTX_LEN, D), 1.0),
        'c_ctx': nrm((D,), 1.0),
        'ada_w': nrm((DEPTH, D, 6 * D), 0.5 * D ** -0.5),
        'ada_b': nrm((DEPTH, 6 * D), 0.01),
        'norm1_g': 1.0 + nrm((DEPTH, D), 0.1),
        'norm2_g': 1.0 + nrm((DEPTH, D), 0.1),
        'mlp_w1': nrm((DEPTH, D, D_FF), D ** -0.5),
        'mlp_w2': nrm((DEPTH, D_FF, D), D_FF ** -0.5),
        'att_w_qkv': nrm((N_ATT, D, qkv_cols), D ** -0.5),
        'att_q_gain': 1.0 + nrm((N_ATT, HEAD_DIM), 0.1),
        'att_k_gain': 1.0 + nrm((N_ATT, HEAD_DIM), 0.1),
        'att_sink': nrm((N_ATT, ATT_Q_HEADS), 1.0),
        'att_w_o': nrm((N_ATT, D, D), D ** -0.5),
        'rwkv_mu': unif((N_RWKV, 6, D), 0.0, 1.0),
        'rwkv_w_rkv': nrm((N_RWKV, 3, D, D), D ** -0.5),
        'rwkv_w0': unif((N_RWKV, 2, D), -6.0, 1.0),
        'rwkv_w1': nrm((N_RWKV, 2, D, DECAY_LORA), D ** -0.5),
        'rwkv_w2': nrm((N_RWKV, 2, DECAY_LORA, D), 0.5 * DECAY_LORA ** -0.5),
        'rwkv_a0': nrm((N_RWKV, D), 0.5),
        'rwkv_a1': nrm((N_RWKV, D, ICLR_LORA), D ** -0.5),
        'rwkv_a2': nrm((N_RWKV, ICLR_LORA, D), ICLR_LORA ** -0.5),
        'rwkv_g1': nrm((N_RWKV, 2, D, GATE_LORA), D ** -0.5),
        'rwkv_g2': nrm((N_RWKV, 2, GATE_LORA, D), GATE_LORA ** -0.5),
        'rwkv_k_k': 0.85 + nrm((N_RWKV, D), 0.05),
        'rwkv_k_a': 1.0 + nrm((N_RWKV, D), 0.05),
        'rwkv_r_k': nrm((N_RWKV, RWKV_HEADS, HEAD_DIM), 0.1),
        'rwkv_gn_g': 1.0 + nrm((N_RWKV, D), 0.1),
        'rwkv_gn_b': nrm((N_RWKV, D), 0.01),
        'rwkv_w_o': nrm((N_RWKV, D, D), D ** -0.5),
    }

def second_block(x, c, ctx, c_ctx, ada_w, ada_b, norm1_g, norm2_g, mlp_w1, mlp_w2,
              att_w_qkv, att_q_gain, att_k_gain, att_sink, att_w_o,
              rwkv_mu, rwkv_w_rkv, rwkv_w0, rwkv_w1, rwkv_w2, rwkv_a0, rwkv_a1, rwkv_a2,
              rwkv_g1, rwkv_g2, rwkv_k_k, rwkv_k_a, rwkv_r_k, rwkv_gn_g, rwkv_gn_b, rwkv_w_o):
    S = x.shape[1]
    n_rows = S // GRID_W
    rows = jnp.repeat(jnp.arange(n_rows), GRID_W)
    cols = jnp.tile(jnp.arange(GRID_W), n_rows)
    silu_c = jax.nn.silu(c)[:, None, :]
    silu_cc = jax.nn.silu(c_ctx)[None, None, :]
    xc = ctx
    for i in range(DEPTH):
        ctx_out = i < DEPTH - 1
        j = i // N_MIXERS
        sh1, sc1, gt1, sh2, sc2, gt2 = jnp.split(silu_c @ ada_w[i] + ada_b[i], 6, axis=-1)
        csh1, csc1, cgt1, csh2, csc2, cgt2 = jnp.split(silu_cc @ ada_w[i] + ada_b[i], 6, axis=-1)
        h = rmsnorm(x, norm1_g[i]) * (1.0 + sc1) + sh1
        hc = rmsnorm(xc, norm1_g[i]) * (1.0 + csc1) + csh1
        if i % N_MIXERS == 0:
            y, yc = attention_mixer(h, hc, att_w_qkv[j], att_q_gain[j], att_k_gain[j], att_sink[j],
                                    att_w_o[j], rows, cols, ctx_out)
        else:
            y, yc = rwkv_mixer(h, hc, rwkv_mu[j], rwkv_w_rkv[j], rwkv_w0[j], rwkv_w1[j], rwkv_w2[j],
                               rwkv_a0[j], rwkv_a1[j], rwkv_a2[j], rwkv_g1[j], rwkv_g2[j],
                               rwkv_k_k[j], rwkv_k_a[j], rwkv_r_k[j], rwkv_gn_g[j], rwkv_gn_b[j],
                               rwkv_w_o[j], ctx_out)
        x = x + gt1 * y
        x = x + gt2 * sq_relu_mlp(rmsnorm(x, norm2_g[i]) * (1.0 + sc2) + sh2, mlp_w1[i], mlp_w2[i])
        if ctx_out:
            xc = xc + cgt1 * yc
            xc = xc + cgt2 * sq_relu_mlp(rmsnorm(xc, norm2_g[i]) * (1.0 + csc2) + csh2, mlp_w1[i], mlp_w2[i])
    return x


def setup_inputs(seed=0):
    out = dict(first_inputs(seed))
    for name, value in second_inputs(seed + 1).items():
        if name != "x":
            out[name + "_2"] = value
    return out


def reference(
    x, c, w_ada, b_ada, w_in, q_scale, k_scale, sgu_ln_g, sgu_ln_b, w_spatial, b_spatial,
    w_branch_a, w_branch_b, w_out, ln1_g, ln1_b, router_w, router_bias, w_gate, w_up, w_down,
    ws_gate, ws_up, ws_down, ln2_g, ln2_b, c_2, ctx_2, c_ctx_2, ada_w_2, ada_b_2, norm1_g_2,
    norm2_g_2, mlp_w1_2, mlp_w2_2, att_w_qkv_2, att_q_gain_2, att_k_gain_2, att_sink_2,
    att_w_o_2, rwkv_mu_2, rwkv_w_rkv_2, rwkv_w0_2, rwkv_w1_2, rwkv_w2_2, rwkv_a0_2, rwkv_a1_2,
    rwkv_a2_2, rwkv_g1_2, rwkv_g2_2, rwkv_k_k_2, rwkv_k_a_2, rwkv_r_k_2, rwkv_gn_g_2,
    rwkv_gn_b_2, rwkv_w_o_2,
):
    x = first_block(
        x, c, w_ada, b_ada, w_in, q_scale, k_scale, sgu_ln_g, sgu_ln_b, w_spatial, b_spatial,
        w_branch_a, w_branch_b, w_out, ln1_g, ln1_b, router_w, router_bias, w_gate, w_up,
        w_down, ws_gate, ws_up, ws_down, ln2_g, ln2_b,
    )
    return second_block(
        x, c_2, ctx_2, c_ctx_2, ada_w_2, ada_b_2, norm1_g_2, norm2_g_2, mlp_w1_2, mlp_w2_2,
        att_w_qkv_2, att_q_gain_2, att_k_gain_2, att_sink_2, att_w_o_2, rwkv_mu_2, rwkv_w_rkv_2,
        rwkv_w0_2, rwkv_w1_2, rwkv_w2_2, rwkv_a0_2, rwkv_a1_2, rwkv_a2_2, rwkv_g1_2, rwkv_g2_2,
        rwkv_k_k_2, rwkv_k_a_2, rwkv_r_k_2, rwkv_gn_g_2, rwkv_gn_b_2, rwkv_w_o_2,
    )


_drawn_inputs = setup_inputs


def setup_inputs(seed=0):
    import zlib

    import numpy as np

    out = dict(_drawn_inputs(seed))
    spreads = {}
    factors = {'q_scale': 8.0,
     'k_scale': 8.0,
     'sgu_ln_g': 8.0,
     'sgu_ln_b': 8.0,
     'b_spatial': 8.0,
     'w_branch_a': 2.785,
     'att_q_gain_2': 8.0,
     'att_k_gain_2': 8.0,
     'att_sink_2': 8.0,
     'rwkv_w1_2': 5.009,
     'rwkv_w2_2': 4.826,
     'rwkv_gn_g_2': 2.769,
     'rwkv_gn_b_2': 28.036}
    for name, (base, spread) in spreads.items():
        noise = np.random.default_rng([zlib.crc32(name.encode()), seed]).standard_normal(out[name].shape)
        drawn = base * np.exp(spread * noise) if base else spread * noise
        out[name] = jnp.asarray(drawn.astype(out[name].dtype))
    for name, factor in factors.items():
        out[name] = (out[name] * factor).astype(out[name].dtype)
    return out
```

```python
import math
from contextlib import ExitStack

import numpy as np

import concourse.bass as bass
from concourse import mybir
from concourse.alu_op_type import AluOpType as ALU

ACT = mybir.ActivationFunctionType
F32 = mybir.dt.float32
AX = mybir.AxisListType.X

ALPHA = 4.0 ** 0.25
NRING = 5
ARENA = 35300
EXPM05 = math.exp(-0.5)


class Mark:

    def __init__(self, queue, index):
        self.queue, self.index, self.needed = queue, index, False

    def where(self):
        return self.queue.sem, self.queue.count[self.index]


class Landed:

    def __init__(self, sem, value):
        self.sem, self.value, self.needed = sem, value, False

    def where(self):
        return self.sem, self.value


def flat(xs):
    for x in xs:
        if isinstance(x, (list, tuple)):
            yield from flat(x)
        elif x is not None:
            yield x


class Queue:

    def __init__(self, sem, linked):
        self.sem, self.linked, self.ops, self.count, self.last = sem, linked, [], [], None

    def add(self, fn, after):
        after = list(flat(after))
        if self.linked and self.last is not None:
            after.append(self.last)
        for m in after:
            m.needed = True
        mark = Mark(self, len(self.ops))
        self.ops.append((fn, after, mark))
        self.last = mark
        return mark

    def number(self):
        n = 0
        for _, _, mark in self.ops:
            n += mark.needed
            self.count.append(n)

    def play(self, eng):
        seen = {}
        for fn, after, mark in self.ops:
            for m in after:
                sem, value = m.where()
                if seen.get(sem.num, 0) < value:
                    eng.wait_ge(sem, value)
                    seen[sem.num] = value
            ins = fn()
            if mark.needed and ins is not None:
                ins.then_inc(self.sem, 1)


class Tensor(Queue):
    def __init__(self, nc, sem):
        super().__init__(sem, False)
        self.e = nc.tensor

    def mm(self, out, lhsT, rhs, start, stop, *after):
        return self.add(lambda: self.e.matmul(out, lhsT, rhs, start=start, stop=stop), after)

    def tr(self, out, in_, ident, *after):
        return self.add(lambda: self.e.transpose(out, in_, ident), after)

    def group(self, out, pairs, *after):
        n = len(pairs)
        m = None
        for i, p in enumerate(pairs):
            m = self.mm(out, p[0], p[1], i == 0, i == n - 1, after if i == 0 else (), *p[2:])
        return m


class Scalar(Queue):
    def __init__(self, nc, sem):
        super().__init__(sem, True)
        self.e = nc.scalar

    def act(self, out, in_, func, *after, bias=0.0, scale=1.0, accum=None):
        if accum is None:
            return self.add(lambda: self.e.activation(out, in_, func, bias=bias, scale=scale), after)
        return self.add(lambda: self.e.activation(out, in_, func, bias=bias, scale=scale, accum_out=accum), after)

    def cp(self, out, in_, *after):
        return self.act(out, in_, ACT.Copy, *after)

    def fma(self, out, in_, scale, bias, *after):
        return self.act(out, in_, ACT.Identity, *after, bias=bias, scale=scale)


class Vector(Queue):
    def __init__(self, nc, sem, e):
        super().__init__(sem, True)
        self.e = e

    def tt(self, out, a, b, op, *after):
        return self.add(lambda: self.e.tensor_tensor(out, a, b, op), after)

    def stt(self, out, a, s, b, op0, op1, *after):
        return self.add(lambda: self.e.scalar_tensor_tensor(out, a, s, b, op0, op1), after)

    def ts(self, out, a, s1, s2, op0, op1, *after):
        if op1 is None:
            return self.add(lambda: self.e.tensor_scalar(out, a, s1, None, op0), after)
        return self.add(lambda: self.e.tensor_scalar(out, a, s1, s2, op0, op1), after)

    def fma(self, out, in_, scale, bias, *after):
        return self.ts(out, in_, scale, bias, ALU.mult, ALU.add, *after)

    def red(self, out, a, op, *after, negate=False):
        if negate:
            return self.add(lambda: self.e.tensor_reduce(out, a, AX, op, negate=True), after)
        return self.add(lambda: self.e.tensor_reduce(out, a, AX, op), after)

    def rcp(self, out, a, *after):
        return self.add(lambda: self.e.reciprocal(out, a), after)

    def cp(self, out, a, *after):
        return self.add(lambda: self.e.tensor_copy(out, a), after)

    def ms(self, out, v, *after):
        return self.add(lambda: self.e.memset(out, v), after)

    def top8(self, out, a, *after):
        return self.add(lambda: self.e.max(out, a), after)

    def drop8(self, out, vals, a, imm, *after):
        return self.add(lambda: self.e.match_replace(out, vals, a, imm), after)

    def bns(self, out, a, *after):
        return self.add(lambda: self.e.bn_stats(out, a), after)

    def bna(self, out, a, *after):
        return self.add(lambda: self.e.bn_aggr(out, a), after)

    def scan(self, out, a, b, *after):
        return self.add(lambda: self.e.tensor_tensor_scan(out, a, b, 0.0, ALU.mult, ALU.add), after)

    def sel(self, out, pattern, op, fill, base, cm, *after):
        return self.add(lambda: self.e.affine_select(out=out, in_=out, compare_op=op, fill=fill, base=base,
                                                     pattern=pattern, channel_multiplier=cm), after)


def bc(a, dim, n):
    dims = [list(d) for d in a.ap]
    dims.insert(dim, [0, n])
    return bass.AP(a.tensor, a.offset, dims)


class Bank:
    def __init__(self, t):
        self.t, self.free = t, []


class Piece:
    def __init__(self, ap, landed):
        self.ap, self.h, self.rel = ap, landed, None


def program(nc, D, out, opts=None):
    opts = opts or {}
    parts = opts.get("parts", "m0 e0 m1 e1 a b")
    ctx = ExitStack()
    with ctx:
        def sb(name, n):
            return ctx.enter_context(nc.sbuf_tensor(name, [128, n], F32))

        def sem(name):
            return ctx.enter_context(nc.semaphore(name))

        ring = sb("ring", NRING * 2048)
        arena = sb("arena", ARENA)
        XS = sb("XS", 2048)
        ident = sb("ident", 128)
        ones = sb("ones", 128)
        eps5 = sb("eps5", 1)
        eps6 = sb("eps6", 1)
        epsg = sb("epsg", 1)
        cond = sb("cond", 8 * 4)
        condr = sb("condr", 8 * 64)
        mod1 = sb("mod1", 2 * 32)
        mod2 = sb("mod2", 2 * 96)
        vecs = sb("vecs", D["vecs"].shape[1])
        stage = sb("stage", 2 * 256)
        small = sb("small", 512)
        banks = [Bank(ctx.enter_context(nc.psum_tensor(f"ps{i}", [128, 512], F32))) for i in range(8)]

        T = Tensor(nc, sem("s_pe"))
        A = Scalar(nc, sem("s_act"))
        V = Vector(nc, sem("s_dve"), nc.vector)
        G = Vector(nc, sem("s_pool"), nc.gpsimd)
        S = Queue(sem("s_sp"), False)
        engines = [T, A, V, G]

        def everyone():
            return [q.last for q in engines if q.last is not None]

        def barrier():
            return everyone()

        ring_sems = [sem(f"s_ring{i}") for i in range(NRING)]
        pieces = []

        def load(src, shape=None):
            n = len(pieces)
            slot = n % NRING
            flat_ap = ring[:, slot * 2048:slot * 2048 + 2048]
            if shape is None:
                width = src.shape[1]
                dst = flat_ap[:, 0:width]
            else:
                dst = flat_ap.rearrange("p (a b) -> p a b", a=shape)
            prev = pieces[n - NRING] if n >= NRING else None
            s = ring_sems[slot]
            S.add(lambda: nc.sync.dma_start(dst, src).then_inc(s, 16) and None,
                  [prev.rel, prev.h] if prev else [])
            p = Piece(flat_ap, Landed(s, 16 * (n // NRING + 1)))
            pieces.append(p)
            return p

        side = {}

        def fetch(name, dst, src, *after):
            if name not in side:
                side[name] = [sem("s_" + name), 0]
            s = side[name]
            s[1] += 16
            sm = s[0]
            S.add(lambda: nc.sync.dma_start(dst, src).then_inc(sm, 16) and None, after)
            return Landed(sm, s[1])

        turn = [0]

        def bank():
            b = banks[turn[0] % 8]
            turn[0] += 1
            return b

        flip = [0]

        def va():
            flip[0] += 1
            return V if flip[0] % 2 else A

        h_vec = fetch("c0", vecs[:, :], D["vecs"])
        h_cond = fetch("c1", cond[:, :], D["cond"])
        G.ms(ident[:, :], 0.0)
        h_id = G.sel(ident[:, :], [[-1, 128]], ALU.not_equal, 1.0, 0, 1)
        V.ms(ones[:, :], 1.0)
        V.ms(eps5[:, :], 1e-5)
        V.ms(eps6[:, :], 1e-6)
        h_one = V.ms(epsg[:, :], 64e-5)
        h = A.act(cond[:, :], cond[:, :], ACT.Silu, h_cond)
        cr = condr[:, :].rearrange("p (b k c) -> p b k c", b=2, k=8)
        V.cp(cr[:, 0, :, :], bc(cond[:, 0:8], 2, 32), h)
        V.cp(cr[:, 1, :, 0:16], bc(cond[:, 8:16], 2, 16))
        h_cr = V.cp(cr[:, 1, :, 16:32], bc(cond[:, 16:24], 2, 16))
        const = [h_vec, h_id, h_one]

        VO = D["voff"]

        def vec(name, n=8):
            o = VO[name]
            return vecs[:, o:o + n]

        stage_free = [None, None]
        stage_n = [0]

        def ada_rows(src, blk, waits=()):
            p = load(src)
            w = p.ap.rearrange("p (k c) -> p k c", k=8)
            b = bank()
            m = None
            for k in range(8):
                j = k % 4
                m = T.mm(b.t[32 * j:32 * j + 32, 0:256], cr[:, blk, k, :], w[:, k, :], k < 4, k >= 4,
                         p.h, h_cr, b.free, waits)
            p.rel = m
            n = stage_n[0] % 2
            stage_n[0] += 1
            st = stage[:, n * 256:n * 256 + 256]
            h = V.cp(st, b.t[:, 0:256], m, stage_free[n])
            b.free = [h]
            return st, n, h

        ones32 = sb("ones32", 128)
        h_o32 = V.ms(ones32[:, :], 1.0 / 32)

        def ada_cols(src, blk, dst, bias, after=()):
            st, n, h = ada_rows(src, blk)
            b = bank()
            m = None
            for c in range(2):
                m = T.tr(b.t[:, c * 128:c * 128 + 128], st[:, c * 128:c * 128 + 128], ident[:, :], h, b.free, h_id)
            stage_free[n] = m
            if blk == 0:
                view = b.t[:, 0:256].rearrange("p (c j r) -> p c j r", c=2, j=4)[:, :, :, 0]
                tmp = small[:, 0:2]
                V.red(tmp, view, ALU.add, m)
                b.free = [V.last]
                return V.tt(dst, tmp, bias, ALU.add, after, h_vec)
            view = b.t[:, 0:256].rearrange("p (c j s r) -> p c s j r", c=2, j=4, s=2)[:, :, :, :, 0]
            tmp = small[:, 0:4].rearrange("p (c s) -> p c s", c=2)
            V.red(tmp, view, ALU.add, m)
            b.free = [V.last]
            return V.tt(dst, tmp, bc(bias, 2, 2), ALU.add, after, h_vec)

        def ada_gate(src, dst, after=()):
            st, n, h = ada_rows(src, 0)
            b = bank()
            m = T.mm(b.t[:, 0:256], ones32[:, :], st, True, True, h, b.free, h_o32)
            stage_free[n] = m
            b.free = [V.tt(dst, b.t[:, 0:256], dst, ALU.add, m, after)]
            return b.free[0]

        gates = sb("gates", 2 * 1024)
        gate = [gates[:, 0:1024], gates[:, 1024:2048]]

        def ada1(l, after):
            hb = fetch("gb", gates[:, :], D["b_gate"][l].partition_broadcast(128), after)
            for v in range(6):
                for q in range(4):
                    src = D["w_ada"][l, v * 4 + q]
                    if v in (2, 5):
                        ada_gate(src, gate[v // 3][:, q * 256:q * 256 + 256], hb)
                    else:
                        vi = {0: 0, 1: 1, 3: 2, 4: 3}[v]
                        o = l * 32 + vi * 8 + 2 * q
                        bo = VO[f"b_ada{l}"] + vi * 8 + 2 * q
                        ada_cols(src, 0, mod1[:, o:o + 2], vecs[:, bo:bo + 2], after)
            for vi in (1, 3):
                o = l * 32 + vi * 8
                V.ts(mod1[:, o:o + 8], mod1[:, o:o + 8], 1.0, None, ALU.add, None)
            return V.last

        def transposed(dst, l, which, after):
            hs = []
            o = l * 32 + which * 16
            xk = XS[:, :].rearrange("p (t d k) -> p t k d", t=2, k=8)
            for k2 in range(4):
                b = bank()
                m = None
                for kk in range(2):
                    for t in range(2):
                        c = kk * 256 + t * 128
                        m = T.tr(b.t[:, c:c + 128], xk[:, t, 2 * k2 + kk, :], ident[:, :], b.free, h_id, after)
                fr = []
                for kk in range(2):
                    k = 2 * k2 + kk
                    e = A if k2 % 2 else V
                    fr.append(e.fma(dst[:, k * 256:k * 256 + 256], b.t[:, kk * 256:kk * 256 + 256],
                                    mod1[:, o + 8 + k:o + 9 + k], mod1[:, o + k:o + k + 1], m, after))
                b.free = fr
                hs += fr
            return hs

        def ln_tok(t, g, bvec, hv, dst, after):
            st = small[:, 16:16 + 24].rearrange("p (t s c) -> p t s c", t=2, s=2)
            mv = small[:, 48:52].rearrange("p (t c) -> p t c", t=2)
            tv = t.rearrange("p (t n) -> p t n", t=2)
            dv = dst.rearrange("p (t n) -> p t n", t=2)
            for i in range(2):
                for s in range(2):
                    V.bns(st[:, i, s, :], tv[:, i, s * 512:s * 512 + 512], after)
                V.bna(mv[:, i, :], st[:, i, :, :])
            h = V.last
            rs = small[:, 52:54]
            A.act(rs, mv[:, :, 1], ACT.Sqrt, h, h_one, bias=eps5[:, 0:1])
            V.rcp(rs, rs, A.last)
            for i in range(2):
                V.ts(tv[:, i, :], tv[:, i, :], mv[:, i, 0:1], rs[:, i:i + 1], ALU.subtract, ALU.mult)
            V.tt(tv, tv, bc(g, 1, 2), ALU.mult, hv)
            return V.tt(dv, tv, bc(bvec, 1, 2), ALU.add, after)

        def rms_rope(src, tmp, nt, nh, gain, hg, cs, sn, swap, hr, nrope):
            ss = small[:, 64:64 + nt * nh].rearrange("p (t h) -> p t h", t=nt)
            V.tt(tmp, src, src, ALU.mult, hg, hr)
            V.red(ss, tmp, ALU.add)
            h = A.act(ss, ss, ACT.Sqrt, V.last, h_one, bias=eps6[:, 0:1], scale=1.0 / 64)
            V.rcp(ss, ss, h)
            V.tt(src, src, bc(ss, 3, 64), ALU.mult)
            V.tt(src, src, bc(gain, 1, nt), ALU.mult)
            for t in range(nrope):
                s_, t_ = src[:, t], tmp[:, t]
                a0, a1 = swap(s_)
                b0, b1 = swap(t_)
                for dst_, x_, n_ in ((b0, a1, 0), (b1, a0, 1)):
                    tab = swap(sn[:, t])[n_]
                    V.tt(dst_, x_, bc(tab, 1, nh), ALU.mult)
                V.tt(s_, s_, bc(cs[:, t], 1, nh), ALU.mult)
                V.tt(s_, s_, t_, ALU.add)
            return V.last

        def softmax_pv(jobs):
            return None

        def mixer(l, x_ready, first):
            a0 = [0]

            def take(n):
                v = arena[:, a0[0]:a0[0] + n]
                a0[0] += n
                assert a0[0] <= ARENA, a0
                return v

            start = barrier() + [x_ready]
            hT, PQ, PQt, Z = take(2048), take(1536), take(1280), take(2048)
            GS, qT, kT, oaT, obT, yT = take(4096), take(1024), take(512), take(1024), take(1024), take(2048)
            PP, PT = take(4 * 256), take(2 * 512)
            gain, tabs = take(640), take(256)
            sg, sbv, lg, lb = take(512), take(512), take(1024), take(1024)
            ws = take(1024)
            TM = take(1536)
            hm = first
            hL = fetch("mx", gain, D["qk_gain"][l].partition_broadcast(128), start)
            hL = fetch("mx", tabs, D["rope1"], start)
            hL = fetch("mx", sg, D["sgu_g"][l].partition_broadcast(128), start)
            hL = fetch("mx", sbv, D["sgu_b"][l].partition_broadcast(128), start)
            hL = fetch("mx", lg, D["ln1_g"][l].partition_broadcast(128), start)
            hL = fetch("mx", lb, D["ln1_b"][l].partition_broadcast(128), start)
            hL = fetch("mx", ws, D["w_sp"][l], start)
            hh = transposed(hT, l, 0, start + [hm])
            hv = hT.rearrange("p (k t) -> p k t", k=8)
            PQv = PQ.rearrange("p (t n) -> p t n", t=2)
            Zv = Z.rearrange("p (t n) -> p t n", t=2)
            GSv = GS.rearrange("p (m t) -> p m t", m=16)
            hq, hz, hg = [], [], []
            for i in range(7):
                p = load(D["w_in"][l, i])
                w = p.ap.rearrange("p (k c) -> p k c", k=8)
                for t in range(2):
                    b = bank()
                    m = T.group(b.t[:, 0:256], [(hv[:, k, t * 128:t * 128 + 128], w[:, k, :]) for k in range(8)],
                                p.h, b.free, hh)
                    if i < 3:
                        b.free = [V.cp(PQv[:, t, i * 256:i * 256 + 256], b.t[:, 0:256], m, start)]
                        hq += b.free
                    else:
                        b.free = [A.act(Zv[:, t, (i - 3) * 256:(i - 3) * 256 + 256], b.t[:, 0:256], ACT.Gelu, m, start)]
                        hz += b.free
                p.rel = m
            q4 = PQv[:, :, 0:640].rearrange("p t (h d) -> p t h d", h=10)
            t4 = PQt.rearrange("p (t h d) -> p t h d", t=2, h=10)
            tb = tabs.rearrange("p (c t d) -> p c t d", c=2, t=2)

            def pairs(v):
                if len(v.shape) == 3:
                    w_ = v.rearrange("p h (j e) -> p h j e", e=2)
                    return w_[:, :, :, 0], w_[:, :, :, 1]
                w_ = v.rearrange("p (j e) -> p j e", e=2)
                return w_[:, :, 0], w_[:, :, 1]

            g3 = gain.rearrange("p (h d) -> p h d", h=10)
            hr = rms_rope(q4, t4, 2, 10, g3, hL, tb[:, 0], tb[:, 1], pairs, hq, 2)
            hk = V.cp(TM[:, 0:512].rearrange("p (t g r d) -> p t g r d", t=2, g=2, r=2),
                      bc(q4[:, :, 8:10, :], 3, 2), start)
            zs = small[:, 100:124].rearrange("p (t c) -> p t c", t=2)
            zm = small[:, 124:128].rearrange("p (t c) -> p t c", t=2)
            for t in range(2):
                V.bns(zs[:, t, 0:6], Zv[:, t, 512:1024], hz)
                V.bna(zm[:, t, :], zs[:, t, 0:6])
            rz = small[:, 128:130]
            h = A.act(rz, zm[:, :, 1], ACT.Sqrt, V.last, h_one, bias=eps5[:, 0:1])
            V.rcp(rz, rz, h)
            for t in range(2):
                V.ts(Zv[:, t, 512:1024], Zv[:, t, 512:1024], zm[:, t, 0:1], rz[:, t:t + 1], ALU.subtract, ALU.mult)
            V.tt(Zv[:, :, 512:1024], Zv[:, :, 512:1024], bc(sg, 1, 2), ALU.mult, hL)
            hvn = V.tt(Zv[:, :, 512:1024], Zv[:, :, 512:1024], bc(sbv, 1, 2), ALU.add, hL)
            for i in range(7, 15):
                p = load(D["w_in"][l, i])
                w = p.ap.rearrange("p (k c) -> p k c", k=8)
                for c in range(2):
                    b = bank()
                    m = T.group(b.t[:, 0:256], [(w[:, k, c * 128:c * 128 + 128], hv[:, k, :]) for k in range(8)],
                                p.h, b.free)
                    b.free = [A.act(GSv[:, 2 * (i - 7) + c, :], b.t[:, 0:256], ACT.Sigmoid, m, start)]
                    hg += b.free
                p.rel = m
            hqT = []
            qv = qT.rearrange("p (a t) -> p a t", a=4)
            kv = kT.rearrange("p (a t) -> p a t", a=2)
            for a in range(3):
                b = bank()
                m = None
                for s in range(2):
                    for t in range(2):
                        if a < 2:
                            src = q4[:, t, 4 * a + 2 * s:4 * a + 2 * s + 2, :]
                        else:
                            src = TM[:, t * 256 + s * 128:t * 256 + s * 128 + 128]
                        m = T.tr(b.t[:, s * 256 + t * 128:s * 256 + t * 128 + 128],
                                 src if a == 2 else src.rearrange("p h d -> p (h d)"), ident[:, :],
                                 b.free, hr, hk)
                dst = qT[:, a * 512:a * 512 + 512] if a < 2 else kT[:, 0:512]
                b.free = [va().cp(dst, b.t[:, 0:512], m, start)]
                hqT += b.free
            ho = attend(8, 2, lambda h_, t: qv[64 * (h_ % 2):64 * (h_ % 2) + 64, h_ // 2, t * 128:t * 128 + 128],
                        lambda h_: [(kv[64 * (h_ % 2):64 * (h_ % 2) + 64, h_ // 4, :], 0)],
                        lambda h_, c: PQv[:, c, 640 + 64 * (h_ // 4):704 + 64 * (h_ // 4)],
                        256, None, None, PP, PT, oaT.rearrange("p (a t) -> p a t", a=4), 0, hqT, start)
            wsv = ws.rearrange("p (g i) -> p g i", g=8)
            b = [bank(), bank()]
            m = None
            for g in range(8):
                bb = b[g // 4]
                o = (g % 4) * 128
                m = T.mm(bb.t[:, o:o + 128].rearrange("p (t d) -> p t d", t=2), wsv[:, g, :],
                         Zv[:, :, 512 + g * 64:576 + g * 64], True, True, bb.free, hvn, hL)
                if g % 4 == 3:
                    gg = g // 4
                    bs = vec(f"b_sp{l}")[:, 4 * gg:4 * gg + 4]
                    tmp = TM[:, 512 + gg * 512:1024 + gg * 512].rearrange("p (t g d) -> p t g d", t=2, g=4)
                    V.tt(tmp, bb.t[:, 0:512].rearrange("p (g t d) -> p t g d", g=4, t=2),
                         bc(bc(bs, 1, 2), 3, 64), ALU.add, m, start)
                    bb.free = [V.last]
                    uz = Zv[:, :, gg * 256:gg * 256 + 256].rearrange("p t (g d) -> p t g d", g=4)
                    V.tt(uz, uz, tmp, ALU.mult)
            hub = V.last
            obv = obT.rearrange("p (c t) -> p c t", c=4)
            hob = []
            for a in range(2):
                b = bank()
                for s in range(2):
                    for t in range(2):
                        m = T.tr(b.t[:, s * 256 + t * 128:s * 256 + t * 128 + 128],
                                 Zv[:, t, (2 * a + s) * 128:(2 * a + s) * 128 + 128], ident[:, :], b.free, hub)
                b.free = [va().cp(obT[:, a * 512:a * 512 + 512], b.t[:, 0:512], m, start)]
                hob += b.free
            yv = yT.rearrange("p (c t) -> p c t", c=8)
            oav = oaT.rearrange("p (a t) -> p a t", a=4)
            hy = []
            for hf in range(2):
                pa = load(D["w_ba"][l, hf])
                pb = load(D["w_bb"][l, hf])
                wa = pa.ap.rearrange("p (c n) -> p c n", c=4)
                wb = pb.ap.rearrange("p (c n) -> p c n", c=4)
                for c in range(4):
                    mt = hf * 4 + c
                    b = bank()
                    T.group(b.t[:, 0:256], [(wa[:, k, c * 128:c * 128 + 128], oav[:, k, :]) for k in range(4)],
                            pa.h, b.free, ho)
                    m = T.group(b.t[:, 256:512], [(wb[:, k, c * 128:c * 128 + 128], obv[:, k, :]) for k in range(4)],
                                pb.h, hob)
                    V.tt(yv[:, mt, :], GSv[:, mt, :], b.t[:, 0:256], ALU.mult, m, hg, start)
                    V.tt(GSv[:, 8 + mt, :], GSv[:, 8 + mt, :], b.t[:, 256:512], ALU.mult, hg)
                    b.free = [V.last]
                    V.tt(yv[:, mt, :], yv[:, mt, :], GSv[:, 8 + mt, :], ALU.add)
                pa.rel = pb.rel = m
            hy = V.last
            Tm = Z
            Tv = Zv
            for i in range(4):
                p = load(D["w_out"][l, i])
                w = p.ap.rearrange("p (k c) -> p k c", k=8)
                for t in range(2):
                    b = bank()
                    m = T.group(b.t[:, 0:256], [(yv[:, k, t * 128:t * 128 + 128], w[:, k, :]) for k in range(8)],
                                p.h, b.free, hy)
                    V.tt(Tv[:, t, i * 256:i * 256 + 256], b.t[:, 0:256], gate[0][:, i * 256:i * 256 + 256], ALU.mult, m, hob)
                    b.free = [V.last]
                p.rel = m
            V.stt(Tm, XS[:, :], ALPHA, Tm, ALU.mult, ALU.add)
            return ln_tok(Tm, lg, lb, hL, XS[:, :], hh)

        def attend(nh, nt, qf, kf, vf, nk, mask, sinks, PP, PT, oT, ocol, ready, start):
            nc_ = nk // 128
            done = []
            pfree = [None] * 4
            tfree = [None] * 2
            n = 0
            prev = None
            pv_open = {}
            st = small[:, 200:232]

            def scores(h_, t):
                nonlocal n
                i = n % 4
                n += 1
                b = bank()
                m = None
                for kk, off in kf(h_):
                    w_ = kk.shape[1]
                    m = T.mm(b.t[:, off:off + w_], qf(h_, t), kk, True, True, ready, b.free)
                P = PP[:, i * nk:i * nk + nk]
                s4 = st[:, i * 8:i * 8 + 8]
                waits = [m, pfree[i], start]
                if mask is None:
                    hm = V.red(s4[:, 0:1], b.t[:, 0:nk], ALU.max, waits)
                    src = b.t[:, 0:nk]
                else:
                    V.stt(P[:, 0:256], b.t[:, 0:256], 0.125, mask[:, t], ALU.mult, ALU.add, waits)
                    V.ts(P[:, 256:512], b.t[:, 256:512], 0.125, None, ALU.mult, None)
                    b.free = [V.last]
                    hm = V.red(s4[:, 0:1], P, ALU.max)
                    src = P
                sc = 0.125 if mask is None else 1.0
                if sinks is not None:
                    V.stt(s4[:, 1:2], s4[:, 0:1], sc, sinks[:, h_:h_ + 1], ALU.mult, ALU.max)
                    V.ts(s4[:, 1:2], s4[:, 1:2], -1.0, None, ALU.mult, None)
                else:
                    V.ts(s4[:, 1:2], s4[:, 0:1], -sc, None, ALU.mult, None)
                he = A.act(P, src, ACT.Exp, V.last, bias=s4[:, 1:2], scale=sc, accum=s4[:, 2:3])
                if mask is None:
                    b.free = [he]
                if sinks is not None:
                    he = A.act(s4[:, 3:4], sinks[:, h_:h_ + 1], ACT.Exp, bias=s4[:, 1:2])
                    V.tt(s4[:, 2:3], s4[:, 2:3], s4[:, 3:4], ALU.add, he)
                V.rcp(s4[:, 2:3], s4[:, 2:3], he)
                hp = V.ts(P, P, s4[:, 2:3], None, ALU.mult, None)
                return P, i, hp

            def finish(h_, parts_):
                for g in range(nc_ // 2):
                    ti = (h_ * (nc_ // 2) + g) % 2
                    b = bank()
                    m = None
                    for c in range(2):
                        for t, (P, i, hp) in enumerate(parts_):
                            o = c * nt * 128 + t * 128
                            m = T.tr(b.t[:, o:o + 128], P[:, (2 * g + c) * 128:(2 * g + c) * 128 + 128], ident[:, :],
                                     hp, b.free)
                    if g == nc_ // 2 - 1:
                        for P, i, hp in parts_:
                            pfree[i] = m
                    dst = PT[:, ti * 512:ti * 512 + 512]
                    he = va().cp(dst, b.t[:, 0:512], m, tfree[ti], start)
                    b.free = [he]
                    if g == 0:
                        if h_ % 2 == 0:
                            pv_open["b"] = bank()
                        ob = pv_open["b"]
                    for c in range(2):
                        first_, last_ = g == 0 and c == 0, g == nc_ // 2 - 1 and c == 1
                        m = T.mm(ob.t[64 * (h_ % 2):64 * (h_ % 2) + 64, 0:nt * 128], vf(h_, 2 * g + c),
                                 dst[:, c * nt * 128:c * nt * 128 + nt * 128], first_, last_, he, ob.free)
                    tfree[ti] = m
                if h_ % 2 == 1:
                    ob.free = [va().cp(oT[:, h_ // 2, ocol:ocol + nt * 128], ob.t[:, 0:nt * 128], m, start)]
                    done.append(ob.free[0])

            pend = None
            for h_ in range(nh):
                cur = [scores(h_, t) for t in range(nt)]
                if pend is not None:
                    finish(*pend)
                pend = (h_, cur)
            if pend is not None:
                finish(*pend)
            return done

        def moe(l, x_ready):
            a0 = [0]

            def take(n):
                v = arena[:, a0[0]:a0[0] + n]
                a0[0] += n
                return v

            start = barrier() + [x_ready]
            hT, acc, lg, lb = take(2048), take(2048), take(1024), take(1024)
            rw, HA, HX = take(512), take(1024), take(1024)
            Gt = take(130)
            rb, sc, sl, mk = take(64), take(128), take(128), take(128)
            gt, gm, gs = take(256), take(16), take(128)
            ltri = take(64)
            hL = fetch("mo", lg, D["ln2_g"][l].partition_broadcast(128), start)
            hL = fetch("mo", lb, D["ln2_b"][l].partition_broadcast(128), start)
            hL = fetch("mo", rw, D["router_w"][l], start)
            hL = fetch("mo", rb, D["router_b"][l].partition_broadcast(128), start)
            hL = fetch("mo", ltri, D["ltri"].partition_broadcast(128), start)
            hh = transposed(hT, l, 1, start)
            hv = hT.rearrange("p (k t) -> p k t", k=8)
            rv = rw.rearrange("p (k e) -> p k e", k=8)
            b = bank()
            for t in range(2):
                m = T.group(b.t[:, t * 64:t * 64 + 64], [(hv[:, k, t * 128:t * 128 + 128], rv[:, k, :]) for k in range(8)],
                            b.free, hh, hL)
            b.free = [A.act(sc, b.t[:, 0:128], ACT.Sigmoid, m, start)]
            V.tt(sl.rearrange("p (t e) -> p t e", t=2), sc.rearrange("p (t e) -> p t e", t=2), bc(rb, 1, 2), ALU.add,
                 b.free, start, hL)
            for t in range(2):
                for g in range(8):
                    V.top8(gs[:, t * 64 + g * 8:t * 64 + g * 8 + 8], sl[:, t * 64 + g * 8:t * 64 + g * 8 + 8])
            gv = gs.rearrange("p (t g c) -> p t g c", t=2, g=8)
            V.tt(gm.rearrange("p (t g) -> p t g", t=2), gv[:, :, :, 0], gv[:, :, :, 1], ALU.add)
            for t in range(2):
                me = gm[:, t * 8:t * 8 + 8]
                g1 = gt[:, 0:64].rearrange("p (i j) -> p i j", i=8)
                g2 = gt[:, 64:128].rearrange("p (i j) -> p i j", i=8)
                oth, own = bc(me, 1, 8), bc(me, 2, 8)
                V.tt(g1, oth, own, ALU.is_gt)
                V.tt(g2, oth, own, ALU.is_equal)
                V.tt(g2, g2, ltri.rearrange("p (i j) -> p i j", i=8), ALU.mult)
                V.tt(g1, g1, g2, ALU.add)
                V.red(gt[:, 128:136], g1, ALU.add)
                V.ts(gt[:, 136:144], gt[:, 128:136], 3.5, None, ALU.is_lt, None)
                V.ts(gt[:, 144:152], gt[:, 136:144], -1.0, 3e38, ALU.add, ALU.mult)
                st = sl[:, t * 64:t * 64 + 64].rearrange("p (g c) -> p g c", g=8)
                mt = mk[:, t * 64:t * 64 + 64].rearrange("p (g c) -> p g c", g=8)
                V.tt(mt, st, bc(gt[:, 136:144], 2, 8), ALU.mult)
                V.tt(mt, mt, bc(gt[:, 144:152], 2, 8), ALU.add)
                V.top8(gt[:, 160:168], mk[:, t * 64:t * 64 + 64])
                V.drop8(gs[:, t * 64:t * 64 + 64], gt[:, 160:168], mk[:, t * 64:t * 64 + 64], -3.3e38)
                V.tt(mk[:, t * 64:t * 64 + 64], mk[:, t * 64:t * 64 + 64], gs[:, t * 64:t * 64 + 64], ALU.not_equal)
                V.tt(sc[:, t * 64:t * 64 + 64], sc[:, t * 64:t * 64 + 64], mk[:, t * 64:t * 64 + 64], ALU.mult)
                V.red(gt[:, 170:171], sc[:, t * 64:t * 64 + 64], ALU.add)
                V.rcp(gt[:, 171:172], gt[:, 170:171])
                V.ts(Gt[:, t * 65:t * 65 + 64], sc[:, t * 64:t * 64 + 64], gt[:, 171:172], 2.5, ALU.mult, ALU.mult)
                V.ms(Gt[:, t * 65 + 64:t * 65 + 65], 1.0)
            ne = opts.get("experts", 64)
            order = [64] + list(range(ne))
            gu = [banks[i] for i in range(4)]
            dn = [banks[i] for i in range(4, 8)]
            ha_free = [None] * 4
            hx_free = [None] * 4

            def weights(e):
                if e == 64:
                    return (load(D["ws_gate"][l]), load(D["ws_up"][l]), load(D["ws_down"][l], 2))
                return (load(D["w_gate"][l, e]), load(D["w_up"][l, e]), load(D["w_down"][l, e], 2))

            def gate_up(n, e, pw):
                wg, wu = (p_.ap.rearrange("p (k f) -> p k f", k=8) for p_ in pw[:2])
                hx = []
                for j in range(2):
                    i = (n % 2) * 2 + j
                    b = gu[i]
                    T.group(b.t[:, 0:256], [(wg[:, k, j * 128:j * 128 + 128], hv[:, k, :]) for k in range(8)],
                            pw[0].h, b.free, hh)
                    m = T.group(b.t[:, 256:512], [(wu[:, k, j * 128:j * 128 + 128], hv[:, k, :]) for k in range(8)],
                                pw[1].h)
                    h1 = A.act(HA[:, i * 256:i * 256 + 256], b.t[:, 0:256], ACT.Silu, m, ha_free[i], start)
                    h2 = V.tt(HX[:, i * 256:i * 256 + 256], HA[:, i * 256:i * 256 + 256], b.t[:, 256:512], ALU.mult,
                              h1, hx_free[i], start)
                    ha_free[i] = h2
                    b.free = [h2]
                    hx.append(h2)
                pw[0].rel = pw[1].rel = m
                return hx

            def down(n, e, pw, hx):
                wd = pw[2].ap.rearrange("p (j d) -> p j d", j=2)
                for t in range(2):
                    for nh in range(2):
                        b = dn[t * 2 + nh]
                        m = None
                        for j in range(2):
                            i = (n % 2) * 2 + j
                            m = T.mm(b.t[:, :], HX[:, i * 256 + t * 128:i * 256 + t * 128 + 128],
                                     wd[:, j, nh * 512:nh * 512 + 512], j == 0, j == 1, hx, pw[2].h, b.free)
                        dst = acc[:, t * 1024 + nh * 512:t * 1024 + nh * 512 + 512]
                        if n == 0:
                            h = V.cp(dst, b.t[:, :], m, start)
                        else:
                            h = V.stt(dst, b.t[:, :], Gt[:, t * 65 + e:t * 65 + e + 1], dst, ALU.mult, ALU.add, m)
                        b.free = [h]
                pw[2].rel = m
                for j in range(2):
                    hx_free[(n % 2) * 2 + j] = m

            prev = None
            for n, e in enumerate(order):
                pw = weights(e)
                hx = gate_up(n, e, pw)
                if prev is not None:
                    down(*prev)
                prev = (n, e, pw, hx)
            down(*prev)
            av = acc.rearrange("p (t n) -> p t n", t=2)
            V.tt(av, av, bc(gate[1], 1, 2), ALU.mult)
            V.stt(acc, XS[:, :], ALPHA, acc, ALU.mult, ALU.add)
            return ln_tok(acc, lg, lb, hL, XS[:, :], hh)

        def ada2(l, after):
            for v in range(6):
                for q in range(4):
                    o = l * 96 + v * 16 + 4 * q
                    bo = VO[f"b2_{l}"] + v * 8 + 2 * q
                    ada_cols(D["ada2"][l, v * 4 + q], 1, mod2[:, o:o + 4].rearrange("p (c s) -> p c s", c=2),
                             vecs[:, bo:bo + 2], after)
            return V.last

        def block2(x_ready):
            XC = gates
            X = [XS[:, :].rearrange("p (k t) -> p k t", k=8), XC[:, :].rearrange("p (k t) -> p k t", k=8)]
            h_ada = [ada2(0, everyone()), ada2(1, ())]
            mv2 = mod2[:, :].rearrange("p (l v k s) -> p l v k s", l=2, v=6, k=8)

            class Arena:
                def __init__(self):
                    self.o = 0

                def take(self, n):
                    v = arena[:, self.o:self.o + n]
                    self.o += n
                    assert self.o <= ARENA, self.o
                    return v

            def norm_t(l, which, Xs, dst_of, sq, R, AB, after):
                outs = []
                gv = vec(f"n{which + 1}g{l}")
                for s, x in Xs:
                    ab = AB[:, s * 8:s * 8 + 8]
                    V.stt(ab, mv2[:, l, 3 * which + 1, :, s], 1.0, gv, ALU.add, ALU.mult, after, h_ada)
                    hs = A.act(sq, x, ACT.Square, after, outs)
                    b = bank()
                    m = T.group(b.t[:, 0:256], [(ones[:, :], sq[:, k, :]) for k in range(8)], hs, b.free, h_one)
                    h = A.act(R, b.t[:, 0:256], ACT.Sqrt, m, after, bias=eps6[:, 0:1], scale=1.0 / 1024)
                    b.free = [h]
                    V.rcp(R, R, h)
                    V.tt(sq, x, bc(R, 1, 8), ALU.mult, m)
                    hx_ = V.last
                    fr = []
                    for k in range(8):
                        e = A if k % 2 else V
                        fr.append(e.fma(dst_of(s, k), sq[:, k, :], ab[:, k:k + 1], mv2[:, l, 3 * which, k, s:s + 1],
                                        hx_, after))
                    outs += fr
                return outs

            def add_gated(l, which, mt, b, m, nseg, after=()):
                for s in range(nseg):
                    x = X[s][:, mt, :]
                    V.stt(x, b.t[:, s * 256:s * 256 + 256], mv2[:, l, 3 * which + 2, mt, s:s + 1], x, ALU.mult, ALU.add,
                          m, after)
                b.free = [V.last]

            def mlp(l, nseg, hx_):
                ar = Arena()
                start = everyone() + [hx_]
                W = nseg * 256
                hT = ar.take(8 * W).rearrange("p (k t) -> p k t", k=8)
                h1 = ar.take(32 * W).rearrange("p (k t) -> p k t", k=32)
                sq = ar.take(2048).rearrange("p (k t) -> p k t", k=8)
                R, AB = ar.take(256), ar.take(16)
                hh = norm_t(l, 1, [(s, X[s]) for s in range(nseg)],
                            lambda s, k: hT[:, k, s * 256:s * 256 + 256], sq, R, AB, start)
                hs = []
                for i in range(16):
                    p = load(D["mlp1"][l, i])
                    w = p.ap.rearrange("p (k c) -> p k c", k=8)
                    for c in range(2):
                        b = bank()
                        m = T.group(b.t[:, 0:W], [(w[:, k, c * 128:c * 128 + 128], hT[:, k, :]) for k in range(8)],
                                    p.h, b.free, hh)
                        dst = h1[:, 2 * i + c, :]
                        ha = A.act(dst, b.t[:, 0:W], ACT.Relu, m, start)
                        b.free = [ha]
                        hs.append(V.tt(dst, dst, dst, ALU.mult, ha))
                    p.rel = m
                for mt in range(8):
                    b = bank()
                    for hf in range(2):
                        p = load(D["mlp2"][l, mt, hf])
                        w = p.ap.rearrange("p (k c) -> p k c", k=16)
                        m = None
                        for k in range(16):
                            kk = hf * 16 + k
                            m = T.mm(b.t[:, 0:W], w[:, k, :], h1[:, kk, :], kk == 0, kk == 31, p.h, b.free, hs[kk])
                        p.rel = m
                    add_gated(l, 1, mt, b, m, nseg)
                return V.last

            ar = Arena()
            start = everyone() + [x_ready, h_ada]
            tmp = ar.take(2048)
            ctx_t = ar.take(2048)
            hc = fetch("cx", ctx_t.rearrange("p (t n) -> p t n", t=2), D["ctx"].rearrange("(t p) n -> p t n", p=128), start)
            xs_done = []
            for src, dst, hw in ((ctx_t, XC[:, :], hc), (XS[:, :], tmp, start)):
                sv = src.rearrange("p (t n) -> p t n", t=2)
                for k2 in range(4):
                    b = bank()
                    m = None
                    for kk in range(2):
                        for t in range(2):
                            k = 2 * k2 + kk
                            m = T.tr(b.t[:, kk * 256 + t * 128:kk * 256 + t * 128 + 128], sv[:, t, k * 128:k * 128 + 128],
                                     ident[:, :], hw, b.free, start)
                    b.free = [va().cp(dst[:, k2 * 512:k2 * 512 + 512], b.t[:, :], m, start)]
                    xs_done += b.free
            hx_ = V.cp(XS[:, :], tmp, xs_done)
            ar = Arena()
            start = everyone()
            hT = ar.take(4096)
            PQ = ar.take(6144)
            tm_ = ar.take(5120)
            qT, kT = ar.take(4096), ar.take(2048)
            PP, PT = ar.take(2048), ar.take(1024)
            oT = ar.take(4096)
            gain, tabs, mask, sk = ar.take(1280), ar.take(256), ar.take(512), ar.take(16)
            R, AB = ar.take(256), ar.take(16)
            TM = ar.take(2048)
            hL = fetch("at", gain, D["gain2"].partition_broadcast(128), start)
            hL = fetch("at", tabs, D["rope2"], start)
            hL = fetch("at", mask, D["mask"], start)
            hL = fetch("at", sk, D["sink"].partition_broadcast(128), start)
            sq = TM.rearrange("p (k t) -> p k t", k=8)
            hv = hT.rearrange("p (k t) -> p k t", k=8)
            hh = norm_t(0, 0, [(0, X[0]), (1, X[1])], lambda s, k: hv[:, k, s * 256:s * 256 + 256], sq, R, AB,
                        [start, hx_])
            PQv = PQ.rearrange("p (t n) -> p t n", t=4)
            hq = []
            for i in range(6):
                p = load(D["wqkv"][i])
                w = p.ap.rearrange("p (k c) -> p k c", k=8)
                for t in range(4):
                    b = bank()
                    m = T.group(b.t[:, 0:256], [(hv[:, k, t * 128:t * 128 + 128], w[:, k, :]) for k in range(8)],
                                p.h, b.free, hh)
                    b.free = [va().cp(PQv[:, t, i * 256:i * 256 + 256], b.t[:, 0:256], m, start)]
                    hq += b.free
                p.rel = m
            q4 = PQv[:, :, 0:1280].rearrange("p t (h d) -> p t h d", h=20)
            t4 = tm_.rearrange("p (t h d) -> p t h d", t=4, h=20)
            tb = tabs.rearrange("p (c t d) -> p c t d", c=2, t=2)

            def halves(v):
                if len(v.shape) == 3:
                    w_ = v.rearrange("p h (g e j) -> p h g e j", g=2, e=2)
                    return w_[:, :, :, 0, :], w_[:, :, :, 1, :]
                w_ = v.rearrange("p (g e j) -> p g e j", g=2, e=2)
                return w_[:, :, 0, :], w_[:, :, 1, :]

            hr = rms_rope(q4, t4, 4, 20, gain.rearrange("p (h d) -> p h d", h=20), [hL, hq], tb[:, 0], tb[:, 1],
                          halves, hL, 2)
            for t in range(4):
                hk = V.cp(TM[:, t * 512:t * 512 + 512].rearrange("p (g r d) -> p g r d", g=4, r=2),
                          bc(q4[:, t, 16:20, :], 2, 2), hh)
            qv = qT.rearrange("p (a t) -> p a t", a=8)
            kv = kT.rearrange("p (a t) -> p a t", a=4)
            hqT = []
            for a in range(12):
                b = bank()
                m = None
                for t in range(4):
                    if a < 8:
                        src = q4[:, t, 2 * a:2 * a + 2, :].rearrange("p h d -> p (h d)")
                    else:
                        src = TM[:, t * 512 + (a - 8) * 128:t * 512 + (a - 8) * 128 + 128]
                    m = T.tr(b.t[:, t * 128:t * 128 + 128], src, ident[:, :], b.free, hr, hk)
                dst = qv[:, a, :] if a < 8 else kv[:, a - 8, :]
                b.free = [va().cp(dst, b.t[:, 0:512], m, start)]
                hqT += b.free
            ov = oT.rearrange("p (a t) -> p a t", a=8)
            mk = mask.rearrange("p (t n) -> p t n", t=2)
            ho = attend(16, 2, lambda h_, t: qv[64 * (h_ % 2):64 * (h_ % 2) + 64, h_ // 2, t * 128:t * 128 + 128],
                        lambda h_: [(kv[64 * (h_ % 2):64 * (h_ % 2) + 64, h_ // 4, :], 0)],
                        lambda h_, c: PQv[:, c, 1280 + 64 * (h_ // 4):1344 + 64 * (h_ // 4)],
                        512, mk, sk, PP, PT, ov, 0, [hqT, hL], start)
            ho2 = attend(16, 2, lambda h_, t: qv[64 * (h_ % 2):64 * (h_ % 2) + 64, h_ // 2, 256 + t * 128:384 + t * 128],
                         lambda h_: [(kv[64 * (h_ % 2):64 * (h_ % 2) + 64, h_ // 4, 256:512], 0)],
                         lambda h_, c: PQv[:, 2 + c, 1280 + 64 * (h_ // 4):1344 + 64 * (h_ // 4)],
                         256, None, sk, PP, PT, ov, 256, [hqT, ho], [start, everyone()])
            for i in range(4):
                p = load(D["w_o"][i])
                w = p.ap.rearrange("p (k c) -> p k c", k=8)
                for c in range(2):
                    b = bank()
                    m = T.group(b.t[:, :], [(w[:, k, c * 128:c * 128 + 128], ov[:, k, :]) for k in range(8)],
                                p.h, b.free, ho, ho2)
                    add_gated(0, 0, 2 * i + c, b, m, 2)
                p.rel = m
            hx_ = mlp(0, 2, V.last)
            if "b" in parts:
                hx_ = rwkv(hx_, X, mv2, norm_t, add_gated, Arena, h_ada)
                hx_ = mlp(1, 1, hx_)
            ar = Arena()
            start = everyone() + [hx_]
            tmp = ar.take(2048).rearrange("p (t n) -> p t n", t=2)
            outs = []
            for k2 in range(4):
                b = bank()
                m = None
                for t in range(2):
                    for kk in range(2):
                        k = 2 * k2 + kk
                        m = T.tr(b.t[:, t * 256 + kk * 128:t * 256 + kk * 128 + 128], X[0][:, k, t * 128:t * 128 + 128],
                                 ident[:, :], start, b.free)
                b.free = [va().cp(tmp[:, :, k2 * 256:k2 * 256 + 256], b.t[:, :].rearrange("p (t c) -> p t c", t=2), m, start)]
                outs += b.free
            return V.cp(XS[:, :].rearrange("p (t n) -> p t n", t=2), tmp, outs)

        def rwkv(x_ready, X, mv2, norm_t, add_gated, Arena, h_ada):
            ar = Arena()
            start = everyone() + [x_ready]
            v8 = lambda a: a.rearrange("p (k t) -> p k t", k=8)
            r, k_, kk, b_ = (v8(ar.take(2048)) for _ in range(4))
            sg = [v8(ar.take(2048)) for _ in range(2)]
            vT = v8(ar.take(2048))
            xg = X[1]
            Z = [ar.take(512).rearrange("p (a v) -> p a v", a=8) for _ in range(2)]
            cs = ar.take(672)
            bo = ar.take(128)
            kvec = ar.take(8)
            base = ar.o
            hL = fetch("rw", cs, D["scan_c"], start)
            hL = fetch("rw", bo, D["blockones"], start)
            V.ts(kvec, vec("k_a"), -1.0, 1.0, ALU.mult, ALU.add, start, h_vec)
            for d in range(2):
                V.ms(Z[d], 0.0, start)
            hz = V.last

            def features(s, after):
                ar.o = base
                W = 256
                hp = ar.take(8 * 258).rearrange("p (k t) -> p k t", k=8)
                xx, aT, mixa, mixb = (v8(ar.take(2048)) for _ in range(4))
                low = [ar.take(256) for _ in range(2)]
                R, AB = ar.take(256), ar.take(16)
                V.ms(hp[:, :, 0:1], 0.0, after)
                V.ms(hp[:, :, 257:258], 0.0)
                hh = norm_t(1, 0, [(s, X[s])], lambda s_, k: hp[:, k, 1:257], mixa, R, AB, after)
                V.tt(xx, hp[:, :, 0:256], hp[:, :, 2:258], ALU.add, hh)
                hxx = V.stt(xx, xx, 0.5, hp[:, :, 1:257], ALU.mult, ALU.subtract)
                bufs, bfree, nb = [mixa, mixb], [None, None], [0]

                def mix(m_, dst=None):
                    i = nb[0] % 2
                    if dst is None:
                        nb[0] += 1
                    o = dst if dst is not None else bufs[i]
                    mu = vec(f"mu{m_}")
                    for k in range(8):
                        h = V.stt(o[:, k, :], xx[:, k, :], mu[:, k:k + 1], hp[:, k, 1:257], ALU.mult, ALU.add,
                                  bfree[i] if dst is None else None, after)
                    return o, h, i

                def wide(src, h, i, w_, evac):
                    for q in range(4):
                        p = load(w_[q])
                        w = p.ap.rearrange("p (k c) -> p k c", k=8)
                        b = bank()
                        m = None
                        for c in range(2):
                            m = T.group(b.t[:, c * 256:c * 256 + 256],
                                        [(w[:, k, c * 128:c * 128 + 128], src[:, k, :]) for k in range(8)],
                                        p.h, b.free, h)
                        p.rel = m
                        b.free = [evac(q, b.t[:, :].rearrange("p (c t) -> p c t", c=2), m)]
                    bfree[i] = m
                    return b.free[0]

                def lora(src, h, i, w1, n, func, dst, bias_of, w2, outs_, func2):
                    p = load(w1)
                    w = p.ap[:, 0:8 * n].rearrange("p (k c) -> p k c", k=8)
                    b = bank()
                    m = T.group(b.t[0:n, 0:256], [(w[:, k, :], src[:, k, :]) for k in range(8)], p.h, b.free, h)
                    p.rel = m
                    bfree[i] = m
                    ht = A.act(dst[0:n, :], b.t[0:n, 0:256], func, m, after)
                    b.free = [ht]
                    p = load(w2)
                    hs = []
                    for d, out_ in enumerate(outs_):
                        for q in range(4):
                            b = bank()
                            for c in range(2):
                                mt = 2 * q + c
                                m = T.mm(b.t[:, c * 256:c * 256 + 256], p.ap[64 * d:64 * d + 64, mt * 128:mt * 128 + 128],
                                         dst[64 * d:64 * d + 64, :], True, True, p.h, b.free, ht)
                            for c in range(2):
                                mt = 2 * q + c
                                hs.append(A.act(out_[:, mt, :], b.t[:, c * 256:c * 256 + 256], func2, m, after,
                                                bias=bias_of(d)[:, mt:mt + 1]))
                            b.free = [hs[-1]]
                    p.rel = m
                    return hs

                if s == 0:
                    o, h, i = mix(0)
                    wide(o, h, i, D["w_rkv"][0], lambda q, t, m: V.cp(r[:, 2 * q:2 * q + 2, :], t, m, after))
                o, h, i = mix(1)
                h_sg = lora(o, h, i, D["w1"], 128, ACT.Tanh, low[0], lambda d: vec(f"w0_{d}"), D["w2"], sg, ACT.Sigmoid)
                o, h, i = mix(2)
                wide(o, h, i, D["w_rkv"][1], lambda q, t, m: V.cp(k_[:, 2 * q:2 * q + 2, :], t, m, after))
                o, h, i = mix(3)
                h_v = wide(o, h, i, D["w_rkv"][2], lambda q, t, m: A.cp(vT[:, 2 * q:2 * q + 2, :], t, m, after))
                o, h, i = mix(4)
                h_a = lora(o, h, i, D["a1"], 64, ACT.Copy, low[1], lambda d: vec("a0"), D["a2"], [aT], ACT.Sigmoid)
                if s == 0:
                    o, h_g, i = mix(5, xg)
                for k in range(8):
                    V.ts(kk[:, k, :], k_[:, k, :], vec("k_k")[:, k:k + 1], None, ALU.mult, None, after)
                sq = xx
                hs = V.tt(sq, kk, kk, ALU.mult)
                head_sums(sq, hs, lambda q, t, m: A.act(sq[:, 2 * q:2 * q + 2, :], t, ACT.Sqrt, m))
                V.ts(sq, sq, 1e-12, None, ALU.max, None, A.last)
                V.rcp(sq, sq)
                V.tt(kk, kk, sq, ALU.mult)
                V.tt(b_, kk, aT, ALU.mult, h_a, after)
                for k in range(8):
                    V.ts(aT[:, k, :], aT[:, k, :], vec("k_a")[:, k:k + 1], kvec[:, k:k + 1], ALU.mult, ALU.add)
                V.tt(k_, k_, aT, ALU.mult)
                return [V.last, A.last]

            def head_sums(src, h, evac):
                for q in range(4):
                    b = bank()
                    m = None
                    for c in range(2):
                        m = T.mm(b.t[:, c * 256:c * 256 + 256], bo, src[:, 2 * q + c, :], True, True, h, b.free, hL)
                    b.free = [evac(q, b.t[:, :].rearrange("p (c t) -> p c t", c=2), m)]

            def scan(s, d, ready, Y):
                ar.o = base + (4096 if s == 0 else 0)
                after = ready
                C = v8(ar.take(1024))
                BK, AR, GT = (ar.take(2048) for _ in range(3))
                E1, E2 = v8(ar.take(1024)), v8(ar.take(1024))
                U, L, Yi, YTi, T1, BL = (ar.take(512) for _ in range(6))
                BKt, VS = [ar.take(512) for _ in range(2)], [ar.take(512) for _ in range(2)]
                Ts = ar.take(256)
                PC = ar.take(32)
                c0 = d * 320
                mG, mU, mL, mU1 = (cs[:, c0 + o:c0 + o + n] for o, n in ((0, 64), (64, 32), (96, 32), (128, 32)))
                mBL = [cs[:, c0 + 160 + 32 * i:c0 + 192 + 32 * i] for i in range(5)]
                I32 = cs[:, 640:672]
                cc = C.rearrange("p k (c t) -> p k c t", c=4)
                Sc = sg[d].rearrange("p k (c t) -> p k c t", c=8)
                BKv = BK.rearrange("p (a c e t) -> p a c e t", a=8, c=4, e=2)
                ARv = AR.rearrange("p (a c e t) -> p a c e t", a=8, c=4, e=2)
                GTv = GT.rearrange("p (c a n) -> p c a n", c=4, a=8)
                E1v = E1.rearrange("p k (c t) -> p k c t", c=4)
                E2v = E2.rearrange("p k (c t) -> p k c t", c=4)

                def q4(x):
                    return x.rearrange("p (c g n) -> p c g n", c=4, g=4)

                batch_order = (0, 1) if d == 0 else (1, 0)
                rows = [None, None]
                h_prev_batch = after
                h_z = hz
                for bt in batch_order:
                    h_b = [V.last, T.last, A.last]
                    for k in range(8):
                        V.scan(C[:, k, :], scanm, sg[d][:, k, bt * 128:bt * 128 + 128], after, h_scanm, h_b)
                    ss = Sc[:, :, 4 * bt:4 * bt + 4, :]

                    def seg_(x, off=0):
                        return x[:, :, off + bt * 128:off + bt * 128 + 128].rearrange("p k (c t) -> p k c t", c=4)

                    tot = cc[:, :, :, 31]
                    h_b = [V.last, T.last, A.last]
                    pcv = PC.rearrange("p (a c) -> p a c", a=8)
                    A.act(pcv, tot, ACT.Exp, h_b, h_prev_batch, scale=-EXPM05)
                    if d == 0:
                        V.tt(E2v, cc, ss, ALU.subtract, h_b, h_prev_batch)
                        incl = cc
                    else:
                        V.tt(E2v, bc(tot, 3, 32), cc, ALU.subtract, h_b, h_prev_batch)
                        V.tt(E1v, E2v, ss, ALU.add)
                        incl = E1v
                    hE2 = V.last
                    hx3 = A.act(E2v, E2v, ACT.Exp, hE2, scale=-EXPM05)
                    V.stt(ARv[:, :, :, 0, :], seg_(kk), -1.0, E2v, ALU.mult, ALU.mult, hx3)
                    if s == 0:
                        ha = A.act(E2v, incl, ACT.Exp, V.last, scale=-EXPM05)
                        V.tt(ARv[:, :, :, 1, :], seg_(r), E2v, ALU.mult, ha)
                    ha = A.act(E2v, incl, ACT.Exp, V.last, scale=EXPM05)
                    V.tt(BKv[:, :, :, 0, :], seg_(b_), E2v, ALU.mult, ha)
                    hbk = V.tt(BKv[:, :, :, 1, :], seg_(k_), E2v, ALU.mult)
                    ne_ = 2 if s == 0 else 1
                    for c in range(4):
                        b = bank()
                        m = None
                        for h_ in range(16):
                            a, o = h_ // 2, 64 * (h_ % 2)
                            m = T.mm(b.t[o:o + 64, a * 32 * ne_:(a + 1) * 32 * ne_],
                                     BKv[o:o + 64, a, c, :, :].rearrange("p e t -> p (e t)"),
                                     ARv[o:o + 64, a, c, 0:ne_, :].rearrange("p e t -> p (e t)"), True, True,
                                     hbk, b.free)
                        b.free = [V.tt(GTv[:, c, :, 0:32 * ne_], b.t[:, 0:256 * ne_].rearrange("p (a n) -> p a n", a=8),
                                       bc(mG[:, 0:32 * ne_], 1, 8), ALU.mult, m, hL)]
                    for dst, mask_, up in ((U, mU, True), (L, mL, False)):
                        b = bank()
                        m = None
                        for c in range(4):
                            for h_ in range(16):
                                a, o, g = h_ // 2, 64 * (h_ % 2), 32 * (h_ % 4)
                                x_, y_ = BKv[o:o + 64, a, c, 0, :], ARv[o:o + 64, a, c, 0, :]
                                if not up:
                                    x_, y_ = y_, x_
                                m = T.mm(b.t[g:g + 32, c * 128 + (h_ // 4) * 32:c * 128 + (h_ // 4) * 32 + 32], x_, y_,
                                         True, True, hbk, b.free)
                        b.free = [V.tt(q4(dst), b.t[:, :].rearrange("p (c g n) -> p c g n", c=4, g=4),
                                       bc(bc(mask_, 1, 4), 1, 4), ALU.mult, m, hL)]
                    iden = bc(bc(I32, 1, 4), 1, 4)
                    V.tt(q4(Yi), q4(U), bc(bc(mU1, 1, 4), 1, 4), ALU.mult)
                    V.tt(q4(Yi), q4(Yi), iden, ALU.add)
                    V.tt(q4(YTi), q4(L), bc(bc(mBL[0], 1, 4), 1, 4), ALU.mult)
                    V.tt(q4(YTi), q4(YTi), iden, ALU.add)
                    hY = V.last

                    def prods(b, lhs, rhs, *w):
                        m = None
                        for c in range(4):
                            for gf in range(4):
                                for g in range(4):
                                    o, f = 32 * g, c * 128 + gf * 32
                                    m = T.mm(b.t[o:o + 32, f:f + 32], lhs[o:o + 32, f:f + 32], rhs[o:o + 32, f:f + 32],
                                             True, True, w, b.free)
                        return m

                    for lev in range(1, 5):
                        hB = V.tt(q4(BL), q4(L), bc(bc(mBL[lev], 1, 4), 1, 4), ALU.mult, T.last)
                        b = bank()
                        m = prods(b, BL, Yi, hB, hY)
                        h1 = A.cp(T1, b.t[:, :], m)
                        b.free = [h1]
                        b = bank()
                        m = prods(b, YTi, T1, h1)
                        b2 = None
                        if lev < 4:
                            b2 = bank()
                            m2 = prods(b2, T1, YTi, h1)
                            V.tt(Yi, Yi, b.t[:, :], ALU.add, m)
                            b.free = [V.last]
                            V.tt(YTi, YTi, b2.t[:, :], ALU.add, m2)
                            b2.free = [V.last]
                        else:
                            V.tt(Yi, Yi, b.t[:, :], ALU.add, m)
                            b.free = [V.last]
                        hY = V.last
                    order = range(4) if d == 0 else range(3, -1, -1)
                    for n_, c in enumerate(order):
                        i = n_ % 2
                        hb_ = []
                        b = bank()
                        m = None
                        for h_ in range(16):
                            a, o = h_ // 2, 64 * (h_ % 2)
                            m = T.mm(b.t[o:o + 64, a * 64:a * 64 + 64],
                                     BKv[o:o + 64, a, c, :, :].rearrange("p e t -> p (e t)"),
                                     ident[o:o + 64, o:o + 64], True, True, hbk, b.free)
                        b.free = [V.cp(BKt[i], b.t[:, :], m, rows[i], h_b)]
                        hb_.append(V.last)
                        b = bank()
                        t0 = bt * 128 + c * 32
                        for h_ in range(16):
                            a, o = h_ // 2, 64 * (h_ % 2)
                            m = T.mm(b.t[o + 32:o + 64, a * 64:a * 64 + 64], vT[o:o + 64, a, t0:t0 + 32],
                                     ident[o:o + 64, o:o + 64], True, True, ready, b.free)
                        e1 = V.cp(VS[i][32:64, :], b.t[32:64, :], m, rows[i], h_b)
                        e2 = A.cp(VS[i][96:128, :], b.t[96:128, :], m, rows[i], h_b)
                        b.free = [e1, e2]
                        hb_ += [e1, e2]
                        bkt = BKt[i].rearrange("p (a v) -> p a v", a=8)
                        vs_ = VS[i].rearrange("p (a v) -> p a v", a=8)
                        b = bank()
                        m = None
                        for h_ in range(16):
                            a, o, g = h_ // 2, 64 * (h_ % 2), 32 * (h_ % 4)
                            dst = b.t[g:g + 32, (h_ // 4) * 64:(h_ // 4) * 64 + 64]
                            T.mm(dst, ARv[o:o + 64, a, c, 0, :], Z[d][o:o + 64, a, :], True, False, h_z, b.free, hbk)
                            m = T.mm(dst, GTv[o + 32:o + 64, c, a, 0:32], vs_[o + 32:o + 64, a, :], False, True, hb_)
                        hT_ = A.cp(Ts, b.t[:, 0:256], m, h_b)
                        b.free = [hT_]
                        hs_ = []
                        vv = VS[i].rearrange("p (a e v) -> p a e v", a=4, e=2)
                        for e in range(2):
                            b = bank()
                            for a2 in range(4):
                                for par in range(2):
                                    h_ = 4 * a2 + 2 * e + par
                                    o, g = 64 * par, 32 * (h_ % 4)
                                    f = c * 128 + a2 * 32
                                    m = T.mm(b.t[o:o + 32, a2 * 64:a2 * 64 + 64], Yi[g:g + 32, f:f + 32],
                                             Ts[g:g + 32, a2 * 64:a2 * 64 + 64], True, True, hT_, hY, b.free)
                            s1 = V.cp(vv[0:32, :, e, :], b.t[0:32, 0:256].rearrange("p (a v) -> p a v", a=4), m)
                            s2 = A.cp(vv[64:96, :, e, :], b.t[64:96, 0:256].rearrange("p (a v) -> p a v", a=4), m)
                            b.free = [s1, s2]
                            hs_ += b.free
                        s1 = s2 = hs_
                        if s == 0:
                            b = bank()
                            for h_ in range(16):
                                a, o = h_ // 2, 64 * (h_ % 2)
                                dst = b.t[o:o + 64, a * 32:a * 32 + 32]
                                T.mm(dst, Z[d][o:o + 64, a, :], ARv[o:o + 64, a, c, 1, :], True, False, b.free, h_z)
                                m = T.mm(dst, vs_[o:o + 64, a, :], GTv[o:o + 64, c, a, 32:64], False, True, s1, s2)
                            t0 = bt * 128 + c * 32
                            b.free = [A.cp(Y[:, :, t0:t0 + 32], b.t[:, 0:256].rearrange("p (a t) -> p a t", a=8), m, ready)]
                        b = bank()
                        for h_ in range(16):
                            a, o = h_ // 2, 64 * (h_ % 2)
                            m = T.mm(b.t[o:o + 64, a * 64:a * 64 + 64], bkt[o:o + 64, a, :], vs_[o:o + 64, a, :],
                                     True, True, b.free, s1, s2, hb_)
                        rows[i] = m
                        V.tt(Z[d], Z[d], b.t[:, :].rearrange("p (a v) -> p a v", a=8), ALU.add, m)
                        b.free = [V.last]
                        h_z = V.tt(Z[d], Z[d], bc(pcv[:, :, c], 2, 64), ALU.mult)
                return [V.last, A.last, T.last]

            scanm = ones_period
            fr = features(1, start)
            e0 = scan(1, 0, [fr, everyone()], None)
            e1 = scan(1, 1, [e0, everyone()], None)
            fr = features(0, [e1, everyone()])
            ar.o = base
            Ys = [v8(ar.take(2048)) for _ in range(2)]
            e0 = scan(0, 0, [fr, everyone()], Ys[0])
            e1 = scan(0, 1, [e0, everyone()], Ys[1])
            after = [e1, everyone()]
            ar.o = base + 4096
            tq, Oh, bonus = (v8(ar.take(2048)) for _ in range(3))
            SG = [ar.take(256) for _ in range(2)]
            V.tt(bonus, r, k_, ALU.mult, after)
            for k in range(8):
                V.ts(bonus[:, k, :], bonus[:, k, :], vec("r_k")[:, k:k + 1], None, ALU.mult, None)
            head_sums(bonus, V.last, lambda q, t, m: V.tt(bonus[:, 2 * q:2 * q + 2, :],
                                                          vT[:, 2 * q:2 * q + 2, :], t, ALU.mult, m))
            hO = None
            for d in range(2):
                p1 = load(D["g1"][d])
                w = p1.ap[:, 0:1024].rearrange("p (k c) -> p k c", k=8)
                b = bank()
                m = T.group(b.t[:, 0:256], [(w[:, k, :], xg[:, k, :]) for k in range(8)], p1.h, b.free, after)
                p1.rel = m
                hs = A.act(SG[d], b.t[:, 0:256], ACT.Sigmoid, m, after)
                b.free = [hs]
                Yd = Ys[d]
                head_sums(Yd, after, lambda q, t, m: V.stt(Yd[:, 2 * q:2 * q + 2, :], t, -1.0 / 64, Yd[:, 2 * q:2 * q + 2, :],
                                                           ALU.mult, ALU.add, m))
                hq_ = A.act(tq, Yd, ACT.Square, V.last, hO)
                head_sums(tq, hq_, lambda q, t, m: A.act(tq[:, 2 * q:2 * q + 2, :], t, ACT.Sqrt, m, bias=epsg[:, 0:1],
                                                         scale=1.0 / 64))
                V.rcp(tq, tq, A.last)
                V.tt(Yd, Yd, tq, ALU.mult)
                for k in range(8):
                    V.ts(Yd[:, k, :], Yd[:, k, :], vec("gn_g")[:, k:k + 1], vec("gn_b")[:, k:k + 1], ALU.mult, ALU.add)
                V.tt(Yd, Yd, bonus, ALU.add)
                p2 = load(D["g2"][d])
                for q in range(4):
                    b = bank()
                    for c in range(2):
                        mt = 2 * q + c
                        m = T.mm(b.t[:, c * 256:c * 256 + 256], p2.ap[:, mt * 128:mt * 128 + 128], SG[d], True, True,
                                 p2.h, hs, b.free)
                    tv = b.t[:, :].rearrange("p (c t) -> p c t", c=2)
                    V.tt(Yd[:, 2 * q:2 * q + 2, :], Yd[:, 2 * q:2 * q + 2, :], tv, ALU.mult, m)
                    b.free = [V.last]
                p2.rel = m
                hO = V.last
            V.tt(Oh, Ys[0], Ys[1], ALU.add, after)
            hO = V.last
            for i in range(4):
                p = load(D["rw_o"][i])
                w = p.ap.rearrange("p (k c) -> p k c", k=8)
                for c in range(2):
                    b = bank()
                    m = T.group(b.t[:, 0:256], [(w[:, k, c * 128:c * 128 + 128], Oh[:, k, :]) for k in range(8)],
                                p.h, b.free, hO)
                    add_gated(1, 0, 2 * i + c, b, m, 1)
                p.rel = m
            return V.last

        ones_period = sb("ones_period", 128)[:, :]
        V.ms(ones_period, 1.0)
        h_scanm = V.ms(ones_period.rearrange("p (c t) -> p c t", c=4)[:, :, 0:1], 0.0)

        hx = fetch("x", XS[:, :].rearrange("p (t n) -> p t n", t=2),
                   (D["x0"] if "x0" in D else D["x"]).rearrange("(t p) n -> p t n", p=128))
        for l in range(2):
            if f"m{l}" in parts:
                hm = ada1(l, everyone())
                hx = mixer(l, [hx, hm], hm)
            if f"e{l}" in parts:
                hx = moe(l, hx)
        if "a" in parts or "b" in parts:
            hx = block2(hx)
        s_out = sem("s_out")
        S.add(lambda: nc.sync.dma_start(out.rearrange("(t p) n -> p t n", p=128),
                                        XS[:, :].rearrange("p (t n) -> p t n", t=2)).then_inc(s_out, 16) and None, [hx])
        S.add(lambda: None, [Landed(s_out, 16)])
        for q in (T, A, V, G, S):
            q.number()
        block = ctx.enter_context(nc.Block())

        @block.sync
        def _(eng):
            S.play(eng)

        @block.tensor
        def _(eng):
            T.play(eng)

        @block.scalar
        def _(eng):
            A.play(eng)

        @block.vector
        def _(eng):
            V.play(eng)

        @block.gpsimd
        def _(eng):
            G.play(eng)


def cols_i(w, n=256):
    N = w.shape[1]
    return np.ascontiguousarray(w.reshape(128, 8, N // n, n).transpose(2, 0, 1, 3)).reshape(N // n, 128, 8 * n)


def cols_s(w, n=256):
    K, N = w.shape[0] // 128, w.shape[1]
    return np.ascontiguousarray(w.reshape(K, 128, N // n, n).transpose(2, 1, 0, 3)).reshape(N // n, 128, K * n)


def vi(v):
    return np.asarray(v).reshape(128, -1)


def vs(v):
    return np.ascontiguousarray(np.asarray(v).reshape(-1, 128).T)


def both(a, f):
    return np.stack([f(a[l]) for l in range(a.shape[0])])


def layout(I):
    I = {k: np.asarray(v) for k, v in I.items()}
    A = {}
    A["x"] = I["x"].reshape(256, 1024)
    A["cond"] = np.concatenate([vi(I["c"][0]), vi(I["c_2"][0]), vi(I["c_ctx_2"]), vi(I["c_ctx_2"])], 1)
    cols, off, n = [], {}, 0

    def put(name, a):
        nonlocal n
        a = np.asarray(a, dtype=a.dtype)
        cols.append(a)
        off[name] = n
        n += a.shape[1]

    for l in range(2):
        b = I["b_ada"][l].reshape(6, 1024)
        put(f"b_ada{l}", np.concatenate([vi(b[i]) for i in (0, 1, 3, 4)], 1))
        put(f"b_sp{l}", np.ascontiguousarray(I["b_spatial"][l].T))
    b2 = I["ada_b_2"]
    for l in range(2):
        put(f"b2_{l}", np.concatenate([vs(b2[l].reshape(6, 1024)[i]) for i in range(6)], 1))
        put(f"n1g{l}", vs(I["norm1_g_2"][l]))
        put(f"n2g{l}", vs(I["norm2_g_2"][l]))
    for m in range(6):
        put(f"mu{m}", vs(I["rwkv_mu_2"][0, m]))
    put("w0_0", vs(I["rwkv_w0_2"][0, 0]))
    put("w0_1", vs(I["rwkv_w0_2"][0, 1]))
    put("a0", vs(I["rwkv_a0_2"][0]))
    put("k_k", vs(I["rwkv_k_k_2"][0]))
    put("k_a", vs(I["rwkv_k_a_2"][0]))
    put("r_k", vs(I["rwkv_r_k_2"][0].reshape(-1)))
    put("gn_g", vs(I["rwkv_gn_g_2"][0]))
    put("gn_b", vs(I["rwkv_gn_b_2"][0]))
    A["vecs"] = np.concatenate(cols, 1)

    def ada_one(w):
        w = w.reshape(1024, 6, 128, 8)
        outs = []
        for i in range(6):
            wi = w[:, i]
            wi = wi.reshape(1024, 1024) if i in (2, 5) else wi.transpose(0, 2, 1).reshape(1024, 1024)
            outs.append(cols_i(wi))
        return np.concatenate(outs, 0)

    A["w_ada"] = both(I["w_ada"], ada_one)
    A["b_gate"] = np.stack([np.concatenate([I["b_ada"][l].reshape(6, 1024)[2], I["b_ada"][l].reshape(6, 1024)[5]]) for l in range(2)])
    A["w_in"] = both(I["w_in"], cols_i)
    A["qk_gain"] = np.stack([np.concatenate([np.tile(I["q_scale"][l], 8), np.tile(I["k_scale"][l], 2)]) for l in range(2)])
    A["sgu_g"], A["sgu_b"] = I["sgu_ln_g"], I["sgu_ln_b"]
    A["ln1_g"], A["ln1_b"], A["ln2_g"], A["ln2_b"] = I["ln1_g"], I["ln1_b"], I["ln2_g"], I["ln2_b"]
    A["w_sp"] = both(I["w_spatial"], lambda w: np.ascontiguousarray(w.transpose(2, 0, 1)).reshape(128, 1024))
    A["w_ba"] = both(I["w_branch_a"], lambda w: cols_s(w, 512))
    A["w_bb"] = both(I["w_branch_b"], lambda w: cols_s(w, 512))
    A["w_out"] = both(I["w_out"], cols_s)
    A["router_w"] = I["router_w"].reshape(2, 128, 512)
    A["router_b"] = I["router_bias"]
    A["w_gate"] = I["w_gate"].reshape(2, 64, 128, 2048)
    A["w_up"] = I["w_up"].reshape(2, 64, 128, 2048)
    A["w_down"] = I["w_down"]
    A["ws_gate"] = I["ws_gate"].reshape(2, 128, 2048)
    A["ws_up"] = I["ws_up"].reshape(2, 128, 2048)
    A["ws_down"] = I["ws_down"]
    A["ltri"] = np.tril(np.ones((8, 8), np.float32), -1).reshape(64)
    t = np.arange(256)
    row, col = (t // 64 - 2).astype(np.float32), (t % 64 - 32).astype(np.float32)
    inv = (np.float32(10000.0) ** (-np.arange(16, dtype=np.float32) / np.float32(16))).astype(np.float32)
    ang = np.concatenate([row[:, None] * inv, col[:, None] * inv], -1)
    c, s = np.cos(ang).astype(np.float32), np.sin(ang).astype(np.float32)
    C = np.repeat(c, 2, 1)
    Sg = np.stack([-s, s], -1).reshape(256, 64)
    A["rope1"] = np.ascontiguousarray(np.stack([C, Sg]).reshape(2, 2, 128, 64).transpose(2, 0, 1, 3)).reshape(128, 256)
    A.update(layout2(I))
    return A, off


def layout2(I):
    A = {}
    A["ada2"] = both(I["ada_w_2"], cols_i)
    A["ctx"] = I["ctx_2"].reshape(256, 1024)
    A["wqkv"] = cols_s(I["att_w_qkv_2"][0])
    A["gain2"] = np.concatenate([np.tile(I["att_q_gain_2"][0], 16), np.tile(I["att_k_gain_2"][0], 4)])
    A["sink"] = I["att_sink_2"][0]
    A["w_o"] = cols_s(I["att_w_o_2"][0])
    A["mlp1"] = both(I["mlp_w1_2"], cols_s)
    A["mlp2"] = both(I["mlp_w2_2"], lambda w: np.ascontiguousarray(
        w.reshape(2, 16, 128, 8, 128).transpose(3, 0, 2, 1, 4)).reshape(8, 2, 128, 2048))
    A["w_rkv"] = both(I["rwkv_w_rkv_2"][0], cols_s)
    w1 = I["rwkv_w1_2"][0]
    A["w1"] = cols_s(np.concatenate([w1[0], w1[1]], 1), 128)[0]
    A["w2"] = I["rwkv_w2_2"][0].reshape(128, 1024)
    A["a1"] = cols_s(I["rwkv_a1_2"][0], 64)[0]
    A["a2"] = np.concatenate([I["rwkv_a2_2"][0], I["rwkv_a2_2"][0]], 0)
    A["g1"] = both(I["rwkv_g1_2"][0], lambda w: cols_s(w, 128)[0])
    A["g2"] = I["rwkv_g2_2"][0]
    A["rw_o"] = cols_s(I["rwkv_w_o_2"][0])
    t = np.arange(256)
    inv = (np.float32(10000.0) ** (-np.arange(16, dtype=np.float32) / np.float32(16))).astype(np.float32)
    ar, ac = (t // 64).astype(np.float32)[:, None] * inv, (t % 64).astype(np.float32)[:, None] * inv
    C = np.concatenate([np.cos(ar), np.cos(ar), np.cos(ac), np.cos(ac)], 1)
    Sg = np.concatenate([-np.sin(ar), np.sin(ar), -np.sin(ac), np.sin(ac)], 1)
    A["rope2"] = np.ascontiguousarray(
        np.stack([C, Sg]).astype(np.float32).reshape(2, 2, 128, 64).transpose(2, 0, 1, 3)).reshape(128, 256)
    m = np.where(np.abs(t[:, None] - t[None, :]) <= 128, 0.0, -1e30).astype(np.float32)
    A["mask"] = np.ascontiguousarray(m.reshape(2, 128, 256).transpose(1, 0, 2)).reshape(128, 512)
    A["blockones"] = np.kron(np.eye(2), np.ones((64, 64))).astype(np.float32)
    i = np.arange(32)
    up, inc = (i[:, None] < i[None, :]).astype(np.float32), (i[:, None] <= i[None, :]).astype(np.float32)

    def half(m_):
        same = i[:, None] // (2 * m_) == i[None, :] // (2 * m_)
        return (same & (i[:, None] % (2 * m_) < m_) & (i[None, :] % (2 * m_) >= m_)).astype(np.float32)

    parts = []
    for d in range(2):
        f = (lambda x: x) if d == 0 else (lambda x: x.T)
        g = np.concatenate([f(up), f(inc)], 1)
        parts.append(np.tile(g, (4, 1)))
        parts.append(np.tile(f(up), (4, 1)))
        parts.append(np.tile(f(up).T, (4, 1)))
        parts.append(np.tile(f(half(1)), (4, 1)))
        for lev in range(5):
            parts.append(np.tile(f(half(2 ** lev)).T, (4, 1)))
    parts.append(np.tile(np.eye(32, dtype=np.float32), (4, 1)))
    A["scan_c"] = np.ascontiguousarray(np.concatenate(parts, 1).astype(np.float32))
    return A


def kernel(**inputs):
    import concourse.bacc as bacc
    from concourse.bass_utils import run_bass_kernel_spmd

    arrays, off = layout(inputs)
    nc = bacc.Bacc("TRN2", target_bir_lowering=False, num_devices=1)
    D, given = {}, {}
    for name, a in arrays.items():
        if name in ("w_down", "ws_down"):
            t = nc.dram_tensor("in_" + name, a.shape, F32, kind="ExternalInput").ap()
            D[name] = t.rearrange("l e (j p) d -> l e p j d", p=128) if name == "w_down" else t.rearrange("l (j p) d -> l p j d", p=128)
        else:
            D[name] = nc.dram_tensor("in_" + name, a.shape, F32, kind="ExternalInput").ap()
        given["in_" + name] = np.ascontiguousarray(a)
    D["voff"] = off
    out = nc.dram_tensor("out_x", (256, 1024), F32, kind="ExternalOutput").ap()
    program(nc, D, out)
    r = run_bass_kernel_spmd(nc, [given], core_ids=[0])
    return r.results[0]["out_x"].reshape(1, 256, 1024)
```

```python
import math
from contextlib import ExitStack

import numpy as np

import concourse.bass as bass
from concourse import mybir
from concourse.alu_op_type import AluOpType as ALU

ACT = mybir.ActivationFunctionType
F32 = mybir.dt.float32
AX = mybir.AxisListType.X

ALPHA = 4.0 ** 0.25
NRING = 5
NEXTRA = 9
ARENA = 35300
EXPM05 = math.exp(-0.5)


class Mark:

    def __init__(self, queue):
        self.queue, self.value, self.needed = queue, None, False

    def where(self):
        return self.queue.sem, self.value


class Landed:

    def __init__(self, sem, value):
        self.sem, self.value, self.needed = sem, value, False

    def where(self):
        return self.sem, self.value


def flat(xs):
    for x in xs:
        if isinstance(x, (list, tuple)):
            yield from flat(x)
        elif x is not None:
            yield x


class Fork:

    def __init__(self, queue, flag, after):
        self.flag, self.after, self.ways, self.ends, self.join = flag, list(flat(after)), ([], []), None, Mark(queue)
        for m in self.after:
            m.needed = True


class Queue:

    def __init__(self, sem, linked):
        self.sem, self.linked, self.ops, self.last = sem, linked, [], None
        self.now = self.ops

    def add(self, fn, after):
        after = list(flat(after))
        if self.linked and self.last is not None:
            after.append(self.last)
        for m in after:
            m.needed = True
        mark = Mark(self)
        self.now.append((fn, after, mark))
        self.last = mark
        return mark

    def number(self, ops=None, n=0):
        for op in self.ops if ops is None else ops:
            if isinstance(op, Fork):
                op.ends = [self.number(way, n) for way in op.ways]
                n = op.join.value = max(op.ends)
            else:
                n += op[2].needed
                op[2].value = n
        return n

    def play(self, eng, ops=None, seen=None):
        seen = {} if seen is None else seen
        for op in self.ops if ops is None else ops:
            after = op.after if isinstance(op, Fork) else op[1]
            for m in after:
                sem, value = m.where()
                if seen.get(sem.num, 0) < value:
                    eng.wait_ge(sem, value)
                    seen[sem.num] = value
            if isinstance(op, Fork):
                flag = eng.value_load(op.flag, min_val=0, max_val=1)
                copies = [dict(seen), dict(seen)]
                with eng.If(flag):
                    self.way(eng, op, 1, copies[1])
                with eng.Else():
                    self.way(eng, op, 0, copies[0])
                seen.clear()
                seen.update({k: min(v, copies[1][k]) for k, v in copies[0].items() if k in copies[1]})
            else:
                ins = op[0]()
                if op[2].needed and ins is not None:
                    ins.then_inc(self.sem, 1)

    def way(self, eng, op, i, seen):
        self.play(eng, op.ways[i], seen)
        short = op.join.value - op.ends[i]
        if short:
            eng.wait_ge(self.sem, op.ends[i])
            eng.sem_inc(self.sem, short)


class Tensor(Queue):
    def __init__(self, nc, sem):
        super().__init__(sem, False)
        self.e = nc.tensor

    def mm(self, out, lhsT, rhs, start, stop, *after):
        return self.add(lambda: self.e.matmul(out, lhsT, rhs, start=start, stop=stop), after)

    def tr(self, out, in_, ident, *after):
        return self.add(lambda: self.e.transpose(out, in_, ident), after)

    def group(self, out, pairs, *after):
        n = len(pairs)
        m = None
        for i, p in enumerate(pairs):
            m = self.mm(out, p[0], p[1], i == 0, i == n - 1, after if i == 0 else (), *p[2:])
        return m


class Scalar(Queue):
    def __init__(self, nc, sem):
        super().__init__(sem, True)
        self.e = nc.scalar

    def act(self, out, in_, func, *after, bias=0.0, scale=1.0, accum=None):
        if accum is None:
            return self.add(lambda: self.e.activation(out, in_, func, bias=bias, scale=scale), after)
        return self.add(lambda: self.e.activation(out, in_, func, bias=bias, scale=scale, accum_out=accum), after)

    def cp(self, out, in_, *after):
        return self.act(out, in_, ACT.Copy, *after)

    def fma(self, out, in_, scale, bias, *after):
        return self.act(out, in_, ACT.Identity, *after, bias=bias, scale=scale)


class Vector(Queue):
    def __init__(self, nc, sem, e):
        super().__init__(sem, True)
        self.e = e

    def tt(self, out, a, b, op, *after):
        return self.add(lambda: self.e.tensor_tensor(out, a, b, op), after)

    def stt(self, out, a, s, b, op0, op1, *after):
        return self.add(lambda: self.e.scalar_tensor_tensor(out, a, s, b, op0, op1), after)

    def ts(self, out, a, s1, s2, op0, op1, *after):
        if op1 is None:
            return self.add(lambda: self.e.tensor_scalar(out, a, s1, None, op0), after)
        return self.add(lambda: self.e.tensor_scalar(out, a, s1, s2, op0, op1), after)

    def fma(self, out, in_, scale, bias, *after):
        return self.ts(out, in_, scale, bias, ALU.mult, ALU.add, *after)

    def red(self, out, a, op, *after, negate=False):
        if negate:
            return self.add(lambda: self.e.tensor_reduce(out, a, AX, op, negate=True), after)
        return self.add(lambda: self.e.tensor_reduce(out, a, AX, op), after)

    def rcp(self, out, a, *after):
        return self.add(lambda: self.e.reciprocal(out, a), after)

    def cp(self, out, a, *after):
        return self.add(lambda: self.e.tensor_copy(out, a), after)

    def ms(self, out, v, *after):
        return self.add(lambda: self.e.memset(out, v), after)

    def top8(self, out, a, *after):
        return self.add(lambda: self.e.max(out, a), after)

    def drop8(self, out, vals, a, imm, *after):
        return self.add(lambda: self.e.match_replace(out, vals, a, imm), after)

    def bns(self, out, a, *after):
        return self.add(lambda: self.e.bn_stats(out, a), after)

    def bna(self, out, a, *after):
        return self.add(lambda: self.e.bn_aggr(out, a), after)

    def scan(self, out, a, b, *after):
        return self.add(lambda: self.e.tensor_tensor_scan(out, a, b, 0.0, ALU.mult, ALU.add), after)

    def sel(self, out, pattern, op, fill, base, cm, *after):
        return self.add(lambda: self.e.affine_select(out=out, in_=out, compare_op=op, fill=fill, base=base,
                                                     pattern=pattern, channel_multiplier=cm), after)


def bc(a, dim, n):
    dims = [list(d) for d in a.ap]
    dims.insert(dim, [0, n])
    return bass.AP(a.tensor, a.offset, dims)


class Bank:
    def __init__(self, t):
        self.t, self.free = t, []


class Piece:
    def __init__(self, ap, landed):
        self.ap, self.h, self.rel = ap, landed, None


def program(nc, D, out, opts=None):
    opts = opts or {}
    parts = opts.get("parts", "m0 e0 m1 e1 a b")
    ctx = ExitStack()
    with ctx:
        def sb(name, n):
            return ctx.enter_context(nc.sbuf_tensor(name, [128, n], F32))

        def sem(name):
            return ctx.enter_context(nc.semaphore(name))

        ring = sb("ring", NRING * 2048)
        arena = sb("arena", ARENA)
        XS = sb("XS", 2048)
        ident = sb("ident", 128)
        ones = sb("ones", 128)
        eps5 = sb("eps5", 1)
        eps6 = sb("eps6", 1)
        epsg = sb("epsg", 1)
        cond = sb("cond", 8 * 4)
        condr = sb("condr", 8 * 64)
        mod1 = sb("mod1", 2 * 32)
        mod2 = sb("mod2", 2 * 96)
        vecs = sb("vecs", D["vecs"].shape[1])
        stage = sb("stage", 2 * 256)
        small = sb("small", 512)
        flags = ctx.enter_context(nc.sbuf_tensor("flags", [128, 64], mybir.dt.int32))
        banks = [Bank(ctx.enter_context(nc.psum_tensor(f"ps{i}", [128, 512], F32))) for i in range(8)]

        T = Tensor(nc, sem("s_pe"))
        A = Scalar(nc, sem("s_act"))
        V = Vector(nc, sem("s_dve"), nc.vector)
        G = Vector(nc, sem("s_pool"), nc.gpsimd)
        S = Queue(sem("s_sp"), False)
        engines = [T, A, V, G]

        def everyone():
            return [q.last for q in engines if q.last is not None]

        def barrier():
            return everyone()

        ring_sems = [sem(f"s_ring{i}") for i in range(NRING + NEXTRA)]
        slots = [ring[:, i * 2048:i * 2048 + 2048] for i in range(NRING)]
        slots += [arena[:, ARENA - (i + 1) * 2048:ARENA - i * 2048] for i in range(NEXTRA)]
        user, uses, at = [None] * len(slots), [0] * len(slots), [0]
        extra_after = [None]

        def load(src, shape=None, big=False):
            slot = at[0] % (NRING + NEXTRA if big else NRING)
            at[0] = slot + 1
            flat_ap = slots[slot]
            if shape is None:
                width = src.shape[1]
                dst = flat_ap[:, 0:width]
            else:
                dst = flat_ap.rearrange("p (a b) -> p a b", a=shape)
            prev = user[slot]
            s = ring_sems[slot]
            S.add(lambda: nc.sync.dma_start(dst, src).then_inc(s, 16) and None,
                  [prev.rel, prev.h] if prev else [], )
            if slot >= NRING:
                S.now[-1][1].extend(flat([extra_after[0]]))
                for m_ in flat([extra_after[0]]):
                    m_.needed = True
            uses[slot] += 1
            p = Piece(flat_ap, Landed(s, 16 * uses[slot]))
            user[slot] = p
            return p

        def fork(flag, after, sparse, dense):
            qs = (T, A, V)
            fs = [Fork(q, flag, after) for q in qs]
            lasts, nows, frees = [q.last for q in qs], [q.now for q in qs], [b.free for b in banks]
            for i, way in enumerate((sparse, dense)):
                for q, f, last in zip(qs, fs, lasts):
                    q.now, q.last = f.ways[i], last
                for b, fr in zip(banks, frees):
                    b.free = fr
                way()
                for q in qs:
                    q.last.needed = True
            for q, f, now in zip(qs, fs, nows):
                q.now, q.last = now, f.join
                now.append(f)
            return [f.join for f in fs]

        side = {}

        def fetch(name, dst, src, *after):
            if name not in side:
                side[name] = [sem("s_" + name), 0]
            s = side[name]
            s[1] += 16
            sm = s[0]
            S.add(lambda: nc.sync.dma_start(dst, src).then_inc(sm, 16) and None, after)
            return Landed(sm, s[1])

        turn = [0]

        def bank():
            b = banks[turn[0] % 8]
            turn[0] += 1
            return b

        flip = [0]

        def va():
            flip[0] += 1
            return V if flip[0] % 2 else A

        h_vec = fetch("c0", vecs[:, :], D["vecs"])
        h_cond = fetch("c1", cond[:, :], D["cond"])
        G.ms(ident[:, :], 0.0)
        h_id = G.sel(ident[:, :], [[-1, 128]], ALU.not_equal, 1.0, 0, 1)
        V.ms(ones[:, :], 1.0)
        V.ms(eps5[:, :], 1e-5)
        V.ms(eps6[:, :], 1e-6)
        h_one = V.ms(epsg[:, :], 64e-5)
        h = A.act(cond[:, :], cond[:, :], ACT.Silu, h_cond)
        cr = condr[:, :].rearrange("p (b k c) -> p b k c", b=2, k=8)
        V.cp(cr[:, 0, :, :], bc(cond[:, 0:8], 2, 32), h)
        V.cp(cr[:, 1, :, 0:16], bc(cond[:, 8:16], 2, 16))
        h_cr = V.cp(cr[:, 1, :, 16:32], bc(cond[:, 16:24], 2, 16))
        const = [h_vec, h_id, h_one]

        VO = D["voff"]

        def vec(name, n=8):
            o = VO[name]
            return vecs[:, o:o + n]

        stage_free = [None, None]
        stage_n = [0]

        def ada_rows(src, blk, waits=()):
            p = load(src)
            w = p.ap.rearrange("p (k c) -> p k c", k=8)
            b = bank()
            m = None
            for k in range(8):
                j = k % 4
                m = T.mm(b.t[32 * j:32 * j + 32, 0:256], cr[:, blk, k, :], w[:, k, :], k < 4, k >= 4,
                         p.h, h_cr, b.free, waits)
            p.rel = m
            n = stage_n[0] % 2
            stage_n[0] += 1
            st = stage[:, n * 256:n * 256 + 256]
            h = V.cp(st, b.t[:, 0:256], m, stage_free[n])
            b.free = [h]
            return st, n, h

        ones32 = sb("ones32", 128)
        h_o32 = V.ms(ones32[:, :], 1.0 / 32)

        def ada_cols(src, blk, dst, bias, after=()):
            st, n, h = ada_rows(src, blk)
            b = bank()
            m = None
            for c in range(2):
                m = T.tr(b.t[:, c * 128:c * 128 + 128], st[:, c * 128:c * 128 + 128], ident[:, :], h, b.free, h_id)
            stage_free[n] = m
            if blk == 0:
                view = b.t[:, 0:256].rearrange("p (c j r) -> p c j r", c=2, j=4)[:, :, :, 0]
                tmp = small[:, 0:2]
                V.red(tmp, view, ALU.add, m)
                b.free = [V.last]
                return V.tt(dst, tmp, bias, ALU.add, after, h_vec)
            view = b.t[:, 0:256].rearrange("p (c j s r) -> p c s j r", c=2, j=4, s=2)[:, :, :, :, 0]
            tmp = small[:, 0:4].rearrange("p (c s) -> p c s", c=2)
            V.red(tmp, view, ALU.add, m)
            b.free = [V.last]
            return V.tt(dst, tmp, bc(bias, 2, 2), ALU.add, after, h_vec)

        def ada_gate(src, dst, after=()):
            st, n, h = ada_rows(src, 0)
            b = bank()
            m = T.mm(b.t[:, 0:256], ones32[:, :], st, True, True, h, b.free, h_o32)
            stage_free[n] = m
            b.free = [V.tt(dst, b.t[:, 0:256], dst, ALU.add, m, after)]
            return b.free[0]

        gates = sb("gates", 2 * 1024)
        gate = [gates[:, 0:1024], gates[:, 1024:2048]]

        def ada1(l, after):
            hb = fetch("gb", gates[:, :], D["b_gate"][l].partition_broadcast(128), after)
            for v in range(6):
                for q in range(4):
                    src = D["w_ada"][l, v * 4 + q]
                    if v in (2, 5):
                        ada_gate(src, gate[v // 3][:, q * 256:q * 256 + 256], hb)
                    else:
                        vi = {0: 0, 1: 1, 3: 2, 4: 3}[v]
                        o = l * 32 + vi * 8 + 2 * q
                        bo = VO[f"b_ada{l}"] + vi * 8 + 2 * q
                        ada_cols(src, 0, mod1[:, o:o + 2], vecs[:, bo:bo + 2], after)
            for vi in (1, 3):
                o = l * 32 + vi * 8
                V.ts(mod1[:, o:o + 8], mod1[:, o:o + 8], 1.0, None, ALU.add, None)
            return V.last

        def transposed(dst, l, which, after):
            hs = []
            o = l * 32 + which * 16
            xk = XS[:, :].rearrange("p (t d k) -> p t k d", t=2, k=8)
            for k2 in range(4):
                b = bank()
                m = None
                for kk in range(2):
                    for t in range(2):
                        c = kk * 256 + t * 128
                        m = T.tr(b.t[:, c:c + 128], xk[:, t, 2 * k2 + kk, :], ident[:, :], b.free, h_id, after)
                fr = []
                for kk in range(2):
                    k = 2 * k2 + kk
                    e = A if k2 % 2 else V
                    fr.append(e.fma(dst[:, k * 256:k * 256 + 256], b.t[:, kk * 256:kk * 256 + 256],
                                    mod1[:, o + 8 + k:o + 9 + k], mod1[:, o + k:o + k + 1], m, after))
                b.free = fr
                hs += fr
            return hs

        def ln_tok(t, g, bvec, hv, dst, after):
            st = small[:, 16:16 + 24].rearrange("p (t s c) -> p t s c", t=2, s=2)
            mv = small[:, 48:52].rearrange("p (t c) -> p t c", t=2)
            tv = t.rearrange("p (t n) -> p t n", t=2)
            dv = dst.rearrange("p (t n) -> p t n", t=2)
            for i in range(2):
                for s in range(2):
                    V.bns(st[:, i, s, :], tv[:, i, s * 512:s * 512 + 512], after)
                V.bna(mv[:, i, :], st[:, i, :, :])
            h = V.last
            rs = small[:, 52:54]
            A.act(rs, mv[:, :, 1], ACT.Sqrt, h, h_one, bias=eps5[:, 0:1])
            V.rcp(rs, rs, A.last)
            for i in range(2):
                V.ts(tv[:, i, :], tv[:, i, :], mv[:, i, 0:1], rs[:, i:i + 1], ALU.subtract, ALU.mult)
            V.tt(tv, tv, bc(g, 1, 2), ALU.mult, hv)
            return V.tt(dv, tv, bc(bvec, 1, 2), ALU.add, after)

        def rms_rope(src, tmp, nt, nh, gain, hg, cs, sn, swap, hr, nrope):
            ss = small[:, 64:64 + nt * nh].rearrange("p (t h) -> p t h", t=nt)
            V.tt(tmp, src, src, ALU.mult, hg, hr)
            V.red(ss, tmp, ALU.add)
            h = A.act(ss, ss, ACT.Sqrt, V.last, h_one, bias=eps6[:, 0:1], scale=1.0 / 64)
            V.rcp(ss, ss, h)
            V.tt(src, src, bc(ss, 3, 64), ALU.mult)
            V.tt(src, src, bc(gain, 1, nt), ALU.mult)
            for t in range(nrope):
                s_, t_ = src[:, t], tmp[:, t]
                a0, a1 = swap(s_)
                b0, b1 = swap(t_)
                for dst_, x_, n_ in ((b0, a1, 0), (b1, a0, 1)):
                    tab = swap(sn[:, t])[n_]
                    V.tt(dst_, x_, bc(tab, 1, nh), ALU.mult)
                V.tt(s_, s_, bc(cs[:, t], 1, nh), ALU.mult)
                V.tt(s_, s_, t_, ALU.add)
            return V.last

        def softmax_pv(jobs):
            return None

        def mixer(l, x_ready, first):
            a0 = [0]

            def take(n):
                v = arena[:, a0[0]:a0[0] + n]
                a0[0] += n
                assert a0[0] <= ARENA, a0
                return v

            start = barrier() + [x_ready]
            hT, PQ, PQt, Z = take(2048), take(1536), take(1280), take(2048)
            GS, qT, kT, oaT, obT, yT = take(4096), take(1024), take(512), take(1024), take(1024), take(2048)
            PP, PT = take(4 * 256), take(2 * 512)
            gain, tabs = take(640), take(256)
            sg, sbv, lg, lb = take(512), take(512), take(1024), take(1024)
            ws = take(1024)
            TM = take(1536)
            hm = first
            hL = fetch("mx", gain, D["qk_gain"][l].partition_broadcast(128), start)
            hL = fetch("mx", tabs, D["rope1"], start)
            hL = fetch("mx", sg, D["sgu_g"][l].partition_broadcast(128), start)
            hL = fetch("mx", sbv, D["sgu_b"][l].partition_broadcast(128), start)
            hL = fetch("mx", lg, D["ln1_g"][l].partition_broadcast(128), start)
            hL = fetch("mx", lb, D["ln1_b"][l].partition_broadcast(128), start)
            hL = fetch("mx", ws, D["w_sp"][l], start)
            hh = transposed(hT, l, 0, start + [hm])
            hv = hT.rearrange("p (k t) -> p k t", k=8)
            PQv = PQ.rearrange("p (t n) -> p t n", t=2)
            Zv = Z.rearrange("p (t n) -> p t n", t=2)
            GSv = GS.rearrange("p (m t) -> p m t", m=16)
            hq, hz, hg = [], [], []
            for i in range(7):
                p = load(D["w_in"][l, i])
                w = p.ap.rearrange("p (k c) -> p k c", k=8)
                for t in range(2):
                    b = bank()
                    m = T.group(b.t[:, 0:256], [(hv[:, k, t * 128:t * 128 + 128], w[:, k, :]) for k in range(8)],
                                p.h, b.free, hh)
                    if i < 3:
                        b.free = [V.cp(PQv[:, t, i * 256:i * 256 + 256], b.t[:, 0:256], m, start)]
                        hq += b.free
                    else:
                        b.free = [A.act(Zv[:, t, (i - 3) * 256:(i - 3) * 256 + 256], b.t[:, 0:256], ACT.Gelu, m, start)]
                        hz += b.free
                p.rel = m
            q4 = PQv[:, :, 0:640].rearrange("p t (h d) -> p t h d", h=10)
            t4 = PQt.rearrange("p (t h d) -> p t h d", t=2, h=10)
            tb = tabs.rearrange("p (c t d) -> p c t d", c=2, t=2)

            def pairs(v):
                if len(v.shape) == 3:
                    w_ = v.rearrange("p h (j e) -> p h j e", e=2)
                    return w_[:, :, :, 0], w_[:, :, :, 1]
                w_ = v.rearrange("p (j e) -> p j e", e=2)
                return w_[:, :, 0], w_[:, :, 1]

            g3 = gain.rearrange("p (h d) -> p h d", h=10)
            hr = rms_rope(q4, t4, 2, 10, g3, hL, tb[:, 0], tb[:, 1], pairs, hq, 2)
            hk = V.cp(TM[:, 0:512].rearrange("p (t g r d) -> p t g r d", t=2, g=2, r=2),
                      bc(q4[:, :, 8:10, :], 3, 2), start)
            zs = small[:, 100:124].rearrange("p (t c) -> p t c", t=2)
            zm = small[:, 124:128].rearrange("p (t c) -> p t c", t=2)
            for t in range(2):
                V.bns(zs[:, t, 0:6], Zv[:, t, 512:1024], hz)
                V.bna(zm[:, t, :], zs[:, t, 0:6])
            rz = small[:, 128:130]
            h = A.act(rz, zm[:, :, 1], ACT.Sqrt, V.last, h_one, bias=eps5[:, 0:1])
            V.rcp(rz, rz, h)
            for t in range(2):
                V.ts(Zv[:, t, 512:1024], Zv[:, t, 512:1024], zm[:, t, 0:1], rz[:, t:t + 1], ALU.subtract, ALU.mult)
            V.tt(Zv[:, :, 512:1024], Zv[:, :, 512:1024], bc(sg, 1, 2), ALU.mult, hL)
            hvn = V.tt(Zv[:, :, 512:1024], Zv[:, :, 512:1024], bc(sbv, 1, 2), ALU.add, hL)
            for i in range(7, 15):
                p = load(D["w_in"][l, i])
                w = p.ap.rearrange("p (k c) -> p k c", k=8)
                for c in range(2):
                    b = bank()
                    m = T.group(b.t[:, 0:256], [(w[:, k, c * 128:c * 128 + 128], hv[:, k, :]) for k in range(8)],
                                p.h, b.free)
                    b.free = [A.act(GSv[:, 2 * (i - 7) + c, :], b.t[:, 0:256], ACT.Sigmoid, m, start)]
                    hg += b.free
                p.rel = m
            hqT = []
            qv = qT.rearrange("p (a t) -> p a t", a=4)
            kv = kT.rearrange("p (a t) -> p a t", a=2)
            for a in range(3):
                b = bank()
                m = None
                for s in range(2):
                    for t in range(2):
                        if a < 2:
                            src = q4[:, t, 4 * a + 2 * s:4 * a + 2 * s + 2, :]
                        else:
                            src = TM[:, t * 256 + s * 128:t * 256 + s * 128 + 128]
                        m = T.tr(b.t[:, s * 256 + t * 128:s * 256 + t * 128 + 128],
                                 src if a == 2 else src.rearrange("p h d -> p (h d)"), ident[:, :],
                                 b.free, hr, hk)
                dst = qT[:, a * 512:a * 512 + 512] if a < 2 else kT[:, 0:512]
                b.free = [va().cp(dst, b.t[:, 0:512], m, start)]
                hqT += b.free
            ho = attend(8, 2, lambda h_, t: qv[64 * (h_ % 2):64 * (h_ % 2) + 64, h_ // 2, t * 128:t * 128 + 128],
                        lambda h_: [(kv[64 * (h_ % 2):64 * (h_ % 2) + 64, h_ // 4, :], 0)],
                        lambda h_, c: PQv[:, c, 640 + 64 * (h_ // 4):704 + 64 * (h_ // 4)],
                        256, None, None, PP, PT, oaT.rearrange("p (a t) -> p a t", a=4), 0, hqT, start)
            wsv = ws.rearrange("p (g i) -> p g i", g=8)
            b = [bank(), bank()]
            m = None
            for g in range(8):
                bb = b[g // 4]
                o = (g % 4) * 128
                m = T.mm(bb.t[:, o:o + 128].rearrange("p (t d) -> p t d", t=2), wsv[:, g, :],
                         Zv[:, :, 512 + g * 64:576 + g * 64], True, True, bb.free, hvn, hL)
                if g % 4 == 3:
                    gg = g // 4
                    bs = vec(f"b_sp{l}")[:, 4 * gg:4 * gg + 4]
                    tmp = TM[:, 512 + gg * 512:1024 + gg * 512].rearrange("p (t g d) -> p t g d", t=2, g=4)
                    V.tt(tmp, bb.t[:, 0:512].rearrange("p (g t d) -> p t g d", g=4, t=2),
                         bc(bc(bs, 1, 2), 3, 64), ALU.add, m, start)
                    bb.free = [V.last]
                    uz = Zv[:, :, gg * 256:gg * 256 + 256].rearrange("p t (g d) -> p t g d", g=4)
                    V.tt(uz, uz, tmp, ALU.mult)
            hub = V.last
            obv = obT.rearrange("p (c t) -> p c t", c=4)
            hob = []
            for a in range(2):
                b = bank()
                for s in range(2):
                    for t in range(2):
                        m = T.tr(b.t[:, s * 256 + t * 128:s * 256 + t * 128 + 128],
                                 Zv[:, t, (2 * a + s) * 128:(2 * a + s) * 128 + 128], ident[:, :], b.free, hub)
                b.free = [va().cp(obT[:, a * 512:a * 512 + 512], b.t[:, 0:512], m, start)]
                hob += b.free
            yv = yT.rearrange("p (c t) -> p c t", c=8)
            oav = oaT.rearrange("p (a t) -> p a t", a=4)
            hy = []
            for hf in range(2):
                pa = load(D["w_ba"][l, hf])
                pb = load(D["w_bb"][l, hf])
                wa = pa.ap.rearrange("p (c n) -> p c n", c=4)
                wb = pb.ap.rearrange("p (c n) -> p c n", c=4)
                for c in range(4):
                    mt = hf * 4 + c
                    b = bank()
                    T.group(b.t[:, 0:256], [(wa[:, k, c * 128:c * 128 + 128], oav[:, k, :]) for k in range(4)],
                            pa.h, b.free, ho)
                    m = T.group(b.t[:, 256:512], [(wb[:, k, c * 128:c * 128 + 128], obv[:, k, :]) for k in range(4)],
                                pb.h, hob)
                    V.tt(yv[:, mt, :], GSv[:, mt, :], b.t[:, 0:256], ALU.mult, m, hg, start)
                    V.tt(GSv[:, 8 + mt, :], GSv[:, 8 + mt, :], b.t[:, 256:512], ALU.mult, hg)
                    b.free = [V.last]
                    V.tt(yv[:, mt, :], yv[:, mt, :], GSv[:, 8 + mt, :], ALU.add)
                pa.rel = pb.rel = m
            hy = V.last
            Tm = Z
            Tv = Zv
            for i in range(4):
                p = load(D["w_out"][l, i])
                w = p.ap.rearrange("p (k c) -> p k c", k=8)
                for t in range(2):
                    b = bank()
                    m = T.group(b.t[:, 0:256], [(yv[:, k, t * 128:t * 128 + 128], w[:, k, :]) for k in range(8)],
                                p.h, b.free, hy)
                    V.tt(Tv[:, t, i * 256:i * 256 + 256], b.t[:, 0:256], gate[0][:, i * 256:i * 256 + 256], ALU.mult, m, hob)
                    b.free = [V.last]
                p.rel = m
            V.stt(Tm, XS[:, :], ALPHA, Tm, ALU.mult, ALU.add)
            return ln_tok(Tm, lg, lb, hL, XS[:, :], hh)

        def attend(nh, nt, qf, kf, vf, nk, mask, sinks, PP, PT, oT, ocol, ready, start):
            nc_ = nk // 128
            done = []
            pfree = [None] * 4
            tfree = [None] * 2
            n = 0
            prev = None
            pv_open = {}
            st = small[:, 200:232]

            def scores(h_, t):
                nonlocal n
                i = n % 4
                n += 1
                b = bank()
                m = None
                for kk, off in kf(h_):
                    w_ = kk.shape[1]
                    m = T.mm(b.t[:, off:off + w_], qf(h_, t), kk, True, True, ready, b.free)
                P = PP[:, i * nk:i * nk + nk]
                s4 = st[:, i * 8:i * 8 + 8]
                waits = [m, pfree[i], start]
                if mask is None:
                    hm = V.red(s4[:, 0:1], b.t[:, 0:nk], ALU.max, waits)
                    src = b.t[:, 0:nk]
                else:
                    V.stt(P[:, 0:256], b.t[:, 0:256], 0.125, mask[:, t], ALU.mult, ALU.add, waits)
                    V.ts(P[:, 256:512], b.t[:, 256:512], 0.125, None, ALU.mult, None)
                    b.free = [V.last]
                    hm = V.red(s4[:, 0:1], P, ALU.max)
                    src = P
                sc = 0.125 if mask is None else 1.0
                if sinks is not None:
                    V.stt(s4[:, 1:2], s4[:, 0:1], sc, sinks[:, h_:h_ + 1], ALU.mult, ALU.max)
                    V.ts(s4[:, 1:2], s4[:, 1:2], -1.0, None, ALU.mult, None)
                else:
                    V.ts(s4[:, 1:2], s4[:, 0:1], -sc, None, ALU.mult, None)
                he = A.act(P, src, ACT.Exp, V.last, bias=s4[:, 1:2], scale=sc, accum=s4[:, 2:3])
                if mask is None:
                    b.free = [he]
                if sinks is not None:
                    he = A.act(s4[:, 3:4], sinks[:, h_:h_ + 1], ACT.Exp, bias=s4[:, 1:2])
                    V.tt(s4[:, 2:3], s4[:, 2:3], s4[:, 3:4], ALU.add, he)
                V.rcp(s4[:, 2:3], s4[:, 2:3], he)
                hp = V.ts(P, P, s4[:, 2:3], None, ALU.mult, None)
                return P, i, hp

            def finish(h_, parts_):
                for g in range(nc_ // 2):
                    ti = (h_ * (nc_ // 2) + g) % 2
                    b = bank()
                    m = None
                    for c in range(2):
                        for t, (P, i, hp) in enumerate(parts_):
                            o = c * nt * 128 + t * 128
                            m = T.tr(b.t[:, o:o + 128], P[:, (2 * g + c) * 128:(2 * g + c) * 128 + 128], ident[:, :],
                                     hp, b.free)
                    if g == nc_ // 2 - 1:
                        for P, i, hp in parts_:
                            pfree[i] = m
                    dst = PT[:, ti * 512:ti * 512 + 512]
                    he = va().cp(dst, b.t[:, 0:512], m, tfree[ti], start)
                    b.free = [he]
                    if g == 0:
                        if h_ % 2 == 0:
                            pv_open["b"] = bank()
                        ob = pv_open["b"]
                    for c in range(2):
                        first_, last_ = g == 0 and c == 0, g == nc_ // 2 - 1 and c == 1
                        m = T.mm(ob.t[64 * (h_ % 2):64 * (h_ % 2) + 64, 0:nt * 128], vf(h_, 2 * g + c),
                                 dst[:, c * nt * 128:c * nt * 128 + nt * 128], first_, last_, he, ob.free)
                    tfree[ti] = m
                if h_ % 2 == 1:
                    ob.free = [va().cp(oT[:, h_ // 2, ocol:ocol + nt * 128], ob.t[:, 0:nt * 128], m, start)]
                    done.append(ob.free[0])

            pend = None
            for h_ in range(nh):
                cur = [scores(h_, t) for t in range(nt)]
                if pend is not None:
                    finish(*pend)
                pend = (h_, cur)
            if pend is not None:
                finish(*pend)
            return done

        def moe(l, x_ready):
            a0 = [0]

            def take(n):
                v = arena[:, a0[0]:a0[0] + n]
                a0[0] += n
                assert a0[0] <= ARENA - NEXTRA * 2048, a0
                return v

            start = everyone() + [x_ready]
            extra_after[0] = start
            hT, lg, lb = take(2048), take(1024), take(1024)
            XE = [take(2048) for _ in range(2)]
            Y2, ST, HA, HX = take(1024), take(256), take(1024), take(1024)
            SelA, SelW = [take(512) for _ in range(2)], [take(512) for _ in range(2)]
            HP, HTT = HX[:, 0:256], HX[:, 256:512]
            rw = take(512)
            Gt = take(130)
            rb, sc, sl, mk = take(64), take(128), take(128), take(128)
            gt, gm, gs = take(256), take(16), take(128)
            ltri, tri = take(64), take(192)
            sid = take(128)
            hL = fetch("mo", lg, D["ln2_g"][l].partition_broadcast(128), start)
            hL = fetch("mo", lb, D["ln2_b"][l].partition_broadcast(128), start)
            hL = fetch("mo", rw, D["router_w"][l], start)
            hL = fetch("mo", rb, D["router_b"][l].partition_broadcast(128), start)
            hL = fetch("mo", ltri, D["ltri"].partition_broadcast(128), start)
            hL = fetch("mo", tri, D["tri"], start)
            hh = transposed(hT, l, 1, start)
            hv = hT.rearrange("p (k t) -> p k t", k=8)
            rv = rw.rearrange("p (k e) -> p k e", k=8)
            b = bank()
            for t in range(2):
                m = T.group(b.t[:, t * 64:t * 64 + 64], [(hv[:, k, t * 128:t * 128 + 128], rv[:, k, :]) for k in range(8)],
                            b.free, hh, hL)
            b.free = [A.act(sc, b.t[:, 0:128], ACT.Sigmoid, m, start)]
            V.tt(sl.rearrange("p (t e) -> p t e", t=2), sc.rearrange("p (t e) -> p t e", t=2), bc(rb, 1, 2), ALU.add,
                 b.free, start, hL)
            for t in range(2):
                for g in range(8):
                    V.top8(gs[:, t * 64 + g * 8:t * 64 + g * 8 + 8], sl[:, t * 64 + g * 8:t * 64 + g * 8 + 8])
            gv = gs.rearrange("p (t g c) -> p t g c", t=2, g=8)
            V.tt(gm.rearrange("p (t g) -> p t g", t=2), gv[:, :, :, 0], gv[:, :, :, 1], ALU.add)
            for t in range(2):
                me = gm[:, t * 8:t * 8 + 8]
                g1 = gt[:, 0:64].rearrange("p (i j) -> p i j", i=8)
                g2 = gt[:, 64:128].rearrange("p (i j) -> p i j", i=8)
                oth, own = bc(me, 1, 8), bc(me, 2, 8)
                V.tt(g1, oth, own, ALU.is_gt)
                V.tt(g2, oth, own, ALU.is_equal)
                V.tt(g2, g2, ltri.rearrange("p (i j) -> p i j", i=8), ALU.mult)
                V.tt(g1, g1, g2, ALU.add)
                V.red(gt[:, 128:136], g1, ALU.add)
                V.ts(gt[:, 136:144], gt[:, 128:136], 3.5, None, ALU.is_lt, None)
                V.ts(gt[:, 144:152], gt[:, 136:144], -1.0, 3e38, ALU.add, ALU.mult)
                st = sl[:, t * 64:t * 64 + 64].rearrange("p (g c) -> p g c", g=8)
                mt = mk[:, t * 64:t * 64 + 64].rearrange("p (g c) -> p g c", g=8)
                V.tt(mt, st, bc(gt[:, 136:144], 2, 8), ALU.mult)
                V.tt(mt, mt, bc(gt[:, 144:152], 2, 8), ALU.add)
                V.top8(gt[:, 160:168], mk[:, t * 64:t * 64 + 64])
                V.drop8(gs[:, t * 64:t * 64 + 64], gt[:, 160:168], mk[:, t * 64:t * 64 + 64], -3.3e38)
                V.tt(mk[:, t * 64:t * 64 + 64], mk[:, t * 64:t * 64 + 64], gs[:, t * 64:t * 64 + 64], ALU.not_equal)
                V.tt(sc[:, t * 64:t * 64 + 64], sc[:, t * 64:t * 64 + 64], mk[:, t * 64:t * 64 + 64], ALU.mult)
                V.red(gt[:, 170:171], sc[:, t * 64:t * 64 + 64], ALU.add)
                V.rcp(gt[:, 171:172], gt[:, 170:171])
                V.ts(Gt[:, t * 65:t * 65 + 64], sc[:, t * 64:t * 64 + 64], gt[:, 171:172], 2.5, ALU.mult, ALU.mult)
            hmk = V.last
            b = bank()
            T.mm(b.t[:, 0:64], tri[:, 0:128], mk[:, 0:64], True, True, hmk, b.free, hL)
            T.mm(b.t[:, 64:128], tri[:, 0:128], mk[:, 64:128], True, False)
            T.mm(b.t[:, 64:128], ones[:, :], mk[:, 0:64], False, True)
            T.mm(b.t[:, 128:192], ones[:, :], mk[:, 0:64], True, False)
            m = T.mm(b.t[:, 128:192], ones[:, :], mk[:, 64:128], False, True)
            V.tt(sid, b.t[:, 0:128], mk, ALU.mult, m)
            cnt = b.t[:, 128:192].rearrange("p (a e) -> p a e", e=2)
            V.red(gt[:, 0:32], cnt, ALU.max)
            b.free = [V.last]
            V.ts(sid, sid, -1.0, None, ALU.add, None)
            V.ts(gt[:, 32:64], gt[:, 0:32], 64.5, None, ALU.is_gt, None)
            h_flag = V.cp(flags[:, l * 32:l * 32 + 32], gt[:, 32:64])
            sv = sid.rearrange("p (t e) -> p t e", t=2)
            gtv = Gt.rearrange("p (t e) -> p t e", t=2)
            iota = tri[:, 128:192]
            work, acc = banks[0:4], banks[4:8]
            for bb in acc:
                T.add(lambda: None, [bb.free])
                bb.free = []
            ne = opts.get("experts", 64)

            def ff_dense(j, pw, after, wait_w=()):
                wg, wu = (p_.ap.rearrange("p (k f) -> p k f", k=8) for p_ in pw[:2])
                b = work[j]
                T.group(b.t[:, 0:256], [(wg[:, k, j * 128:j * 128 + 128], hv[:, k, :]) for k in range(8)],
                        pw[0].h, b.free, hh)
                m = T.group(b.t[:, 256:512], [(wu[:, k, j * 128:j * 128 + 128], hv[:, k, :]) for k in range(8)],
                            pw[1].h)
                h1 = A.act(HA[:, j * 256:j * 256 + 256], b.t[:, 0:256], ACT.Silu, m, after)
                h2 = V.tt(HX[:, j * 256:j * 256 + 256], HA[:, j * 256:j * 256 + 256], b.t[:, 256:512], ALU.mult,
                          h1, after)
                b.free = [h2]
                return h2

            def down_dense(pw, hx, first, last):
                wd = pw[2].ap.rearrange("p (j d) -> p j d", j=2)
                m = None
                for t in range(2):
                    for nh in range(2):
                        for j in range(2):
                            m = T.mm(acc[t * 2 + nh].t[:, :], HX[:, j * 256 + t * 128:j * 256 + t * 128 + 128],
                                     wd[:, j, nh * 512:nh * 512 + 512], first and j == 0, last and j == 1, hx, pw[2].h)
                return m

            def prep(Q, joins):
                q2 = Q % 2
                for t in range(2):
                    sa = SelA[q2][:, t * 256:t * 256 + 256].rearrange("p (e s) -> p e s", e=4)
                    sw = SelW[q2][:, t * 256:t * 256 + 256].rearrange("p (e s) -> p e s", e=4)
                    V.tt(sa, bc(iota, 1, 4), bc(sv[:, t, 4 * Q:4 * Q + 4], 2, 64), ALU.is_equal, joins, start)
                    V.tt(sw, sa, bc(gtv[:, t, 4 * Q:4 * Q + 4], 2, 64), ALU.mult)
                hsel = V.last
                xk = XS[:, :].rearrange("p (t d k) -> p t k d", t=2, k=8)
                o = l * 32 + 16
                done = []
                for k2 in range(4):
                    b = work[k2]
                    m = None
                    for kk in range(2):
                        m = T.group(b.t[:, kk * 256:kk * 256 + 256],
                                    [(xk[:, t, 2 * k2 + kk, :], SelA[q2][:, t * 256:t * 256 + 256]) for t in range(2)],
                                    hsel, b.free)
                    fr = []
                    for kk in range(2):
                        k = 2 * k2 + kk
                        e = A if k2 % 2 else V
                        fr.append(e.fma(XE[q2][:, k * 256:k * 256 + 256], b.t[:, kk * 256:kk * 256 + 256],
                                        mod1[:, o + 8 + k:o + 9 + k], mod1[:, o + k:o + k + 1], m, joins))
                    b.free = fr
                    done.append(fr)
                return done

            def pair(Q, pp, pa, pb, hxe, last):
                q2 = Q % 2
                xe = XE[q2].rearrange("p (k s) -> p k s", k=8)
                pws = (pa, pb)

                def sparse():
                    b = work[0]
                    m = None
                    for i_, off in ((0, 0), (1, 256)):
                        for k in range(8):
                            for ab in range(2):
                                w = pws[ab][i_]
                                m = T.mm(b.t[64 * ab:64 * ab + 64, off:off + 256],
                                         xe[:, k, pp * 128 + 64 * ab:pp * 128 + 64 * ab + 64],
                                         w.ap.rearrange("p (k f) -> p k f", k=8)[:, k, :], k == 0, k == 7,
                                         w.h, b.free, hxe[k // 2])
                    h1 = A.act(HA[:, 0:256], b.t[:, 0:256], ACT.Silu, m)
                    h2 = V.tt(HP, HA[:, 0:256], b.t[:, 256:512], ALU.mult, h1)
                    b1 = work[1]
                    for t in range(2):
                        m = T.tr(b1.t[:, t * 128:t * 128 + 128], SelW[q2][:, t * 256 + pp * 128:t * 256 + pp * 128 + 128],
                                 ident[:, :], b1.free)
                    hst = A.cp(ST, b1.t[:, 0:256], m)
                    for j in range(2):
                        m = T.tr(b.t[:, j * 128:j * 128 + 128], HP[:, j * 128:j * 128 + 128], ident[:, :], h2)
                    hht = V.cp(HTT, b.t[:, 0:256], m)
                    hy = []
                    for nh in range(2):
                        bb = work[2 + nh]
                        for j in range(2):
                            for ab in range(2):
                                w = pws[ab][2]
                                m = T.mm(bb.t[64 * ab:64 * ab + 64, :], HTT[:, j * 128 + 64 * ab:j * 128 + 64 * ab + 64],
                                         w.ap.rearrange("p (j d) -> p j d", j=2)[:, j, nh * 512:nh * 512 + 512],
                                         j == 0, j == 1, w.h, bb.free, hht)
                        hy.append((V if nh else A).cp(Y2[:, nh * 512:nh * 512 + 512], bb.t[:, :], m))
                    for nh in range(2):
                        for t in range(2):
                            T.mm(acc[t * 2 + nh].t[:, :], ST[:, t * 128:t * 128 + 128], Y2[:, nh * 512:nh * 512 + 512],
                                 False, last, hst, hy[nh])

                def dense():
                    for ab in range(2):
                        pw = pws[ab]
                        e = 4 * Q + 2 * pp + ab
                        prevm = T.last
                        hx = [ff_dense(j, pw, prevm) for j in range(2)]
                        b = work[2]
                        m = None
                        for t in range(2):
                            g1 = Gt[:, t * 65 + e:t * 65 + e + 1]
                            wide = bass.AP(g1.tensor, g1.offset, [list(g1.ap[0]), [0, 128]])
                            m = T.mm(b.t[:, t * 128:t * 128 + 128], wide, ident[:, :], True, True, b.free)
                        for j in range(2):
                            h = V.tt(HX[:, j * 256:j * 256 + 256], HX[:, j * 256:j * 256 + 256], b.t[:, 0:256], ALU.mult,
                                     m, hx)
                        b.free = [h]
                        down_dense(pw, h, False, last and ab == 1)

                joins = fork(flags[0:1, l * 32 + 2 * Q + pp:l * 32 + 2 * Q + pp + 1], [h_flag], sparse, dense)
                for pw in pws:
                    for p_ in pw:
                        p_.rel = joins[0]
                for bb in work:
                    bb.free = joins
                return joins

            pw = [load(D["ws_gate"][l], big=True), load(D["ws_up"][l], big=True), load(D["ws_down"][l], 2, big=True)]
            hx = [ff_dense(j, pw, start) for j in range(2)]
            m = down_dense(pw, hx, True, False)
            for p_ in pw:
                p_.rel = m
            nq = ne // 4
            joins = everyone()
            hxe = prep(0, joins)
            prev = [joins, joins]
            for Q in range(nq):
                for pp in range(2):
                    e = 4 * Q + 2 * pp
                    pa, pb = [None] * 3, [None] * 3
                    for i_, nm in enumerate(("w_gate", "w_up", "w_down")):
                        for ab, pw in ((0, pa), (1, pb)):
                            pw[i_] = load(D[nm][l, e + ab], 2 if i_ == 2 else None, big=True)
                    joins = pair(Q, pp, pa, pb, hxe, Q == nq - 1 and pp == 1)
                    if pp == 0 and Q + 1 < nq:
                        nxt = prep(Q + 1, [joins, prev])
                prev = joins
                hxe = nxt
            av = hT.rearrange("p (t n) -> p t n", t=2)
            for t in range(2):
                for nh in range(2):
                    bb = acc[t * 2 + nh]
                    V.tt(av[:, t, nh * 512:nh * 512 + 512], bb.t[:, :], gate[1][:, nh * 512:nh * 512 + 512], ALU.mult, joins)
                    bb.free = [V.last]
            V.stt(hT, XS[:, :], ALPHA, hT, ALU.mult, ALU.add)
            for bb in work:
                bb.free = joins
            return ln_tok(hT, lg, lb, hL, XS[:, :], hh)

        def ada2(l, after):
            for v in range(6):
                for q in range(4):
                    o = l * 96 + v * 16 + 4 * q
                    bo = VO[f"b2_{l}"] + v * 8 + 2 * q
                    ada_cols(D["ada2"][l, v * 4 + q], 1, mod2[:, o:o + 4].rearrange("p (c s) -> p c s", c=2),
                             vecs[:, bo:bo + 2], after)
            return V.last

        def block2(x_ready):
            XC = gates
            X = [XS[:, :].rearrange("p (k t) -> p k t", k=8), XC[:, :].rearrange("p (k t) -> p k t", k=8)]
            h_ada = [ada2(0, everyone()), ada2(1, ())]
            mv2 = mod2[:, :].rearrange("p (l v k s) -> p l v k s", l=2, v=6, k=8)

            class Arena:
                def __init__(self):
                    self.o = 0

                def take(self, n):
                    v = arena[:, self.o:self.o + n]
                    self.o += n
                    assert self.o <= ARENA, self.o
                    return v

            def norm_t(l, which, Xs, dst_of, sq, R, AB, after):
                outs = []
                gv = vec(f"n{which + 1}g{l}")
                for s, x in Xs:
                    ab = AB[:, s * 8:s * 8 + 8]
                    V.stt(ab, mv2[:, l, 3 * which + 1, :, s], 1.0, gv, ALU.add, ALU.mult, after, h_ada)
                    hs = A.act(sq, x, ACT.Square, after, outs)
                    b = bank()
                    m = T.group(b.t[:, 0:256], [(ones[:, :], sq[:, k, :]) for k in range(8)], hs, b.free, h_one)
                    h = A.act(R, b.t[:, 0:256], ACT.Sqrt, m, after, bias=eps6[:, 0:1], scale=1.0 / 1024)
                    b.free = [h]
                    V.rcp(R, R, h)
                    V.tt(sq, x, bc(R, 1, 8), ALU.mult, m)
                    hx_ = V.last
                    fr = []
                    for k in range(8):
                        e = A if k % 2 else V
                        fr.append(e.fma(dst_of(s, k), sq[:, k, :], ab[:, k:k + 1], mv2[:, l, 3 * which, k, s:s + 1],
                                        hx_, after))
                    outs += fr
                return outs

            def add_gated(l, which, mt, b, m, nseg, after=()):
                for s in range(nseg):
                    x = X[s][:, mt, :]
                    V.stt(x, b.t[:, s * 256:s * 256 + 256], mv2[:, l, 3 * which + 2, mt, s:s + 1], x, ALU.mult, ALU.add,
                          m, after)
                b.free = [V.last]

            def mlp(l, nseg, hx_):
                ar = Arena()
                start = everyone() + [hx_]
                W = nseg * 256
                hT = ar.take(8 * W).rearrange("p (k t) -> p k t", k=8)
                h1 = ar.take(32 * W).rearrange("p (k t) -> p k t", k=32)
                sq = ar.take(2048).rearrange("p (k t) -> p k t", k=8)
                R, AB = ar.take(256), ar.take(16)
                hh = norm_t(l, 1, [(s, X[s]) for s in range(nseg)],
                            lambda s, k: hT[:, k, s * 256:s * 256 + 256], sq, R, AB, start)
                hs = []
                for i in range(16):
                    p = load(D["mlp1"][l, i])
                    w = p.ap.rearrange("p (k c) -> p k c", k=8)
                    for c in range(2):
                        b = bank()
                        m = T.group(b.t[:, 0:W], [(w[:, k, c * 128:c * 128 + 128], hT[:, k, :]) for k in range(8)],
                                    p.h, b.free, hh)
                        dst = h1[:, 2 * i + c, :]
                        ha = A.act(dst, b.t[:, 0:W], ACT.Relu, m, start)
                        b.free = [ha]
                        hs.append(V.tt(dst, dst, dst, ALU.mult, ha))
                    p.rel = m
                for mt in range(8):
                    b = bank()
                    for hf in range(2):
                        p = load(D["mlp2"][l, mt, hf])
                        w = p.ap.rearrange("p (k c) -> p k c", k=16)
                        m = None
                        for k in range(16):
                            kk = hf * 16 + k
                            m = T.mm(b.t[:, 0:W], w[:, k, :], h1[:, kk, :], kk == 0, kk == 31, p.h, b.free, hs[kk])
                        p.rel = m
                    add_gated(l, 1, mt, b, m, nseg)
                return V.last

            ar = Arena()
            start = everyone() + [x_ready, h_ada]
            tmp = ar.take(2048)
            ctx_t = ar.take(2048)
            hc = fetch("cx", ctx_t.rearrange("p (t n) -> p t n", t=2), D["ctx"].rearrange("(t p) n -> p t n", p=128), start)
            xs_done = []
            for src, dst, hw in ((ctx_t, XC[:, :], hc), (XS[:, :], tmp, start)):
                sv = src.rearrange("p (t n) -> p t n", t=2)
                for k2 in range(4):
                    b = bank()
                    m = None
                    for kk in range(2):
                        for t in range(2):
                            k = 2 * k2 + kk
                            m = T.tr(b.t[:, kk * 256 + t * 128:kk * 256 + t * 128 + 128], sv[:, t, k * 128:k * 128 + 128],
                                     ident[:, :], hw, b.free, start)
                    b.free = [va().cp(dst[:, k2 * 512:k2 * 512 + 512], b.t[:, :], m, start)]
                    xs_done += b.free
            hx_ = V.cp(XS[:, :], tmp, xs_done)
            ar = Arena()
            start = everyone()
            hT = ar.take(4096)
            PQ = ar.take(6144)
            tm_ = ar.take(5120)
            qT, kT = ar.take(4096), ar.take(2048)
            PP, PT = ar.take(2048), ar.take(1024)
            oT = ar.take(4096)
            gain, tabs, mask, sk = ar.take(1280), ar.take(256), ar.take(512), ar.take(16)
            R, AB = ar.take(256), ar.take(16)
            TM = ar.take(2048)
            hL = fetch("at", gain, D["gain2"].partition_broadcast(128), start)
            hL = fetch("at", tabs, D["rope2"], start)
            hL = fetch("at", mask, D["mask"], start)
            hL = fetch("at", sk, D["sink"].partition_broadcast(128), start)
            sq = TM.rearrange("p (k t) -> p k t", k=8)
            hv = hT.rearrange("p (k t) -> p k t", k=8)
            hh = norm_t(0, 0, [(0, X[0]), (1, X[1])], lambda s, k: hv[:, k, s * 256:s * 256 + 256], sq, R, AB,
                        [start, hx_])
            PQv = PQ.rearrange("p (t n) -> p t n", t=4)
            hq = []
            for i in range(6):
                p = load(D["wqkv"][i])
                w = p.ap.rearrange("p (k c) -> p k c", k=8)
                for t in range(4):
                    b = bank()
                    m = T.group(b.t[:, 0:256], [(hv[:, k, t * 128:t * 128 + 128], w[:, k, :]) for k in range(8)],
                                p.h, b.free, hh)
                    b.free = [va().cp(PQv[:, t, i * 256:i * 256 + 256], b.t[:, 0:256], m, start)]
                    hq += b.free
                p.rel = m
            q4 = PQv[:, :, 0:1280].rearrange("p t (h d) -> p t h d", h=20)
            t4 = tm_.rearrange("p (t h d) -> p t h d", t=4, h=20)
            tb = tabs.rearrange("p (c t d) -> p c t d", c=2, t=2)

            def halves(v):
                if len(v.shape) == 3:
                    w_ = v.rearrange("p h (g e j) -> p h g e j", g=2, e=2)
                    return w_[:, :, :, 0, :], w_[:, :, :, 1, :]
                w_ = v.rearrange("p (g e j) -> p g e j", g=2, e=2)
                return w_[:, :, 0, :], w_[:, :, 1, :]

            hr = rms_rope(q4, t4, 4, 20, gain.rearrange("p (h d) -> p h d", h=20), [hL, hq], tb[:, 0], tb[:, 1],
                          halves, hL, 2)
            for t in range(4):
                hk = V.cp(TM[:, t * 512:t * 512 + 512].rearrange("p (g r d) -> p g r d", g=4, r=2),
                          bc(q4[:, t, 16:20, :], 2, 2), hh)
            qv = qT.rearrange("p (a t) -> p a t", a=8)
            kv = kT.rearrange("p (a t) -> p a t", a=4)
            hqT = []
            for a in range(12):
                b = bank()
                m = None
                for t in range(4):
                    if a < 8:
                        src = q4[:, t, 2 * a:2 * a + 2, :].rearrange("p h d -> p (h d)")
                    else:
                        src = TM[:, t * 512 + (a - 8) * 128:t * 512 + (a - 8) * 128 + 128]
                    m = T.tr(b.t[:, t * 128:t * 128 + 128], src, ident[:, :], b.free, hr, hk)
                dst = qv[:, a, :] if a < 8 else kv[:, a - 8, :]
                b.free = [va().cp(dst, b.t[:, 0:512], m, start)]
                hqT += b.free
            ov = oT.rearrange("p (a t) -> p a t", a=8)
            mk = mask.rearrange("p (t n) -> p t n", t=2)
            ho = attend(16, 2, lambda h_, t: qv[64 * (h_ % 2):64 * (h_ % 2) + 64, h_ // 2, t * 128:t * 128 + 128],
                        lambda h_: [(kv[64 * (h_ % 2):64 * (h_ % 2) + 64, h_ // 4, :], 0)],
                        lambda h_, c: PQv[:, c, 1280 + 64 * (h_ // 4):1344 + 64 * (h_ // 4)],
                        512, mk, sk, PP, PT, ov, 0, [hqT, hL], start)
            ho2 = attend(16, 2, lambda h_, t: qv[64 * (h_ % 2):64 * (h_ % 2) + 64, h_ // 2, 256 + t * 128:384 + t * 128],
                         lambda h_: [(kv[64 * (h_ % 2):64 * (h_ % 2) + 64, h_ // 4, 256:512], 0)],
                         lambda h_, c: PQv[:, 2 + c, 1280 + 64 * (h_ // 4):1344 + 64 * (h_ // 4)],
                         256, None, sk, PP, PT, ov, 256, [hqT, ho], [start, everyone()])
            for i in range(4):
                p = load(D["w_o"][i])
                w = p.ap.rearrange("p (k c) -> p k c", k=8)
                for c in range(2):
                    b = bank()
                    m = T.group(b.t[:, :], [(w[:, k, c * 128:c * 128 + 128], ov[:, k, :]) for k in range(8)],
                                p.h, b.free, ho, ho2)
                    add_gated(0, 0, 2 * i + c, b, m, 2)
                p.rel = m
            hx_ = mlp(0, 2, V.last)
            if "b" in parts:
                hx_ = rwkv(hx_, X, mv2, norm_t, add_gated, Arena, h_ada)
                hx_ = mlp(1, 1, hx_)
            ar = Arena()
            start = everyone() + [hx_]
            tmp = ar.take(2048).rearrange("p (t n) -> p t n", t=2)
            outs = []
            for k2 in range(4):
                b = bank()
                m = None
                for t in range(2):
                    for kk in range(2):
                        k = 2 * k2 + kk
                        m = T.tr(b.t[:, t * 256 + kk * 128:t * 256 + kk * 128 + 128], X[0][:, k, t * 128:t * 128 + 128],
                                 ident[:, :], start, b.free)
                b.free = [va().cp(tmp[:, :, k2 * 256:k2 * 256 + 256], b.t[:, :].rearrange("p (t c) -> p t c", t=2), m, start)]
                outs += b.free
            return V.cp(XS[:, :].rearrange("p (t n) -> p t n", t=2), tmp, outs)

        def rwkv(x_ready, X, mv2, norm_t, add_gated, Arena, h_ada):
            ar = Arena()
            start = everyone() + [x_ready]
            v8 = lambda a: a.rearrange("p (k t) -> p k t", k=8)
            r, k_, kk, b_ = (v8(ar.take(2048)) for _ in range(4))
            sg = [v8(ar.take(2048)) for _ in range(2)]
            vT = v8(ar.take(2048))
            xg = X[1]
            Z = [ar.take(512).rearrange("p (a v) -> p a v", a=8) for _ in range(2)]
            cs = ar.take(672)
            bo = ar.take(128)
            kvec = ar.take(8)
            base = ar.o
            hL = fetch("rw", cs, D["scan_c"], start)
            hL = fetch("rw", bo, D["blockones"], start)
            V.ts(kvec, vec("k_a"), -1.0, 1.0, ALU.mult, ALU.add, start, h_vec)
            for d in range(2):
                V.ms(Z[d], 0.0, start)
            hz = V.last

            def features(s, after):
                ar.o = base
                W = 256
                hp = ar.take(8 * 258).rearrange("p (k t) -> p k t", k=8)
                xx, aT, mixa, mixb = (v8(ar.take(2048)) for _ in range(4))
                low = [ar.take(256) for _ in range(2)]
                R, AB = ar.take(256), ar.take(16)
                V.ms(hp[:, :, 0:1], 0.0, after)
                V.ms(hp[:, :, 257:258], 0.0)
                hh = norm_t(1, 0, [(s, X[s])], lambda s_, k: hp[:, k, 1:257], mixa, R, AB, after)
                V.tt(xx, hp[:, :, 0:256], hp[:, :, 2:258], ALU.add, hh)
                hxx = V.stt(xx, xx, 0.5, hp[:, :, 1:257], ALU.mult, ALU.subtract)
                bufs, bfree, nb = [mixa, mixb], [None, None], [0]

                def mix(m_, dst=None):
                    i = nb[0] % 2
                    if dst is None:
                        nb[0] += 1
                    o = dst if dst is not None else bufs[i]
                    mu = vec(f"mu{m_}")
                    for k in range(8):
                        h = V.stt(o[:, k, :], xx[:, k, :], mu[:, k:k + 1], hp[:, k, 1:257], ALU.mult, ALU.add,
                                  bfree[i] if dst is None else None, after)
                    return o, h, i

                def wide(src, h, i, w_, evac):
                    for q in range(4):
                        p = load(w_[q])
                        w = p.ap.rearrange("p (k c) -> p k c", k=8)
                        b = bank()
                        m = None
                        for c in range(2):
                            m = T.group(b.t[:, c * 256:c * 256 + 256],
                                        [(w[:, k, c * 128:c * 128 + 128], src[:, k, :]) for k in range(8)],
                                        p.h, b.free, h)
                        p.rel = m
                        b.free = [evac(q, b.t[:, :].rearrange("p (c t) -> p c t", c=2), m)]
                    bfree[i] = m
                    return b.free[0]

                def lora(src, h, i, w1, n, func, dst, bias_of, w2, outs_, func2):
                    p = load(w1)
                    w = p.ap[:, 0:8 * n].rearrange("p (k c) -> p k c", k=8)
                    b = bank()
                    m = T.group(b.t[0:n, 0:256], [(w[:, k, :], src[:, k, :]) for k in range(8)], p.h, b.free, h)
                    p.rel = m
                    bfree[i] = m
                    ht = A.act(dst[0:n, :], b.t[0:n, 0:256], func, m, after)
                    b.free = [ht]
                    p = load(w2)
                    hs = []
                    for d, out_ in enumerate(outs_):
                        for q in range(4):
                            b = bank()
                            for c in range(2):
                                mt = 2 * q + c
                                m = T.mm(b.t[:, c * 256:c * 256 + 256], p.ap[64 * d:64 * d + 64, mt * 128:mt * 128 + 128],
                                         dst[64 * d:64 * d + 64, :], True, True, p.h, b.free, ht)
                            for c in range(2):
                                mt = 2 * q + c
                                hs.append(A.act(out_[:, mt, :], b.t[:, c * 256:c * 256 + 256], func2, m, after,
                                                bias=bias_of(d)[:, mt:mt + 1]))
                            b.free = [hs[-1]]
                    p.rel = m
                    return hs

                if s == 0:
                    o, h, i = mix(0)
                    wide(o, h, i, D["w_rkv"][0], lambda q, t, m: V.cp(r[:, 2 * q:2 * q + 2, :], t, m, after))
                o, h, i = mix(1)
                h_sg = lora(o, h, i, D["w1"], 128, ACT.Tanh, low[0], lambda d: vec(f"w0_{d}"), D["w2"], sg, ACT.Sigmoid)
                o, h, i = mix(2)
                wide(o, h, i, D["w_rkv"][1], lambda q, t, m: V.cp(k_[:, 2 * q:2 * q + 2, :], t, m, after))
                o, h, i = mix(3)
                h_v = wide(o, h, i, D["w_rkv"][2], lambda q, t, m: A.cp(vT[:, 2 * q:2 * q + 2, :], t, m, after))
                o, h, i = mix(4)
                h_a = lora(o, h, i, D["a1"], 64, ACT.Copy, low[1], lambda d: vec("a0"), D["a2"], [aT], ACT.Sigmoid)
                if s == 0:
                    o, h_g, i = mix(5, xg)
                for k in range(8):
                    V.ts(kk[:, k, :], k_[:, k, :], vec("k_k")[:, k:k + 1], None, ALU.mult, None, after)
                sq = xx
                hs = V.tt(sq, kk, kk, ALU.mult)
                head_sums(sq, hs, lambda q, t, m: A.act(sq[:, 2 * q:2 * q + 2, :], t, ACT.Sqrt, m))
                V.ts(sq, sq, 1e-12, None, ALU.max, None, A.last)
                V.rcp(sq, sq)
                V.tt(kk, kk, sq, ALU.mult)
                V.tt(b_, kk, aT, ALU.mult, h_a, after)
                for k in range(8):
                    V.ts(aT[:, k, :], aT[:, k, :], vec("k_a")[:, k:k + 1], kvec[:, k:k + 1], ALU.mult, ALU.add)
                V.tt(k_, k_, aT, ALU.mult)
                return [V.last, A.last]

            def head_sums(src, h, evac):
                for q in range(4):
                    b = bank()
                    m = None
                    for c in range(2):
                        m = T.mm(b.t[:, c * 256:c * 256 + 256], bo, src[:, 2 * q + c, :], True, True, h, b.free, hL)
                    b.free = [evac(q, b.t[:, :].rearrange("p (c t) -> p c t", c=2), m)]

            def scan(s, d, ready, Y):
                ar.o = base + (4096 if s == 0 else 0)
                after = ready
                C = v8(ar.take(1024))
                BK, AR, GT = (ar.take(2048) for _ in range(3))
                E1, E2 = v8(ar.take(1024)), v8(ar.take(1024))
                U, L, Yi, YTi, T1, BL = (ar.take(512) for _ in range(6))
                BKt, VS = [ar.take(512) for _ in range(2)], [ar.take(512) for _ in range(2)]
                Ts = ar.take(256)
                PC = ar.take(32)
                c0 = d * 320
                mG, mU, mL, mU1 = (cs[:, c0 + o:c0 + o + n] for o, n in ((0, 64), (64, 32), (96, 32), (128, 32)))
                mBL = [cs[:, c0 + 160 + 32 * i:c0 + 192 + 32 * i] for i in range(5)]
                I32 = cs[:, 640:672]
                cc = C.rearrange("p k (c t) -> p k c t", c=4)
                Sc = sg[d].rearrange("p k (c t) -> p k c t", c=8)
                BKv = BK.rearrange("p (a c e t) -> p a c e t", a=8, c=4, e=2)
                ARv = AR.rearrange("p (a c e t) -> p a c e t", a=8, c=4, e=2)
                GTv = GT.rearrange("p (c a n) -> p c a n", c=4, a=8)
                E1v = E1.rearrange("p k (c t) -> p k c t", c=4)
                E2v = E2.rearrange("p k (c t) -> p k c t", c=4)

                def q4(x):
                    return x.rearrange("p (c g n) -> p c g n", c=4, g=4)

                batch_order = (0, 1) if d == 0 else (1, 0)
                rows = [None, None]
                h_prev_batch = after
                h_z = hz
                for bt in batch_order:
                    h_b = [V.last, T.last, A.last]
                    for k in range(8):
                        V.scan(C[:, k, :], scanm, sg[d][:, k, bt * 128:bt * 128 + 128], after, h_scanm, h_b)
                    ss = Sc[:, :, 4 * bt:4 * bt + 4, :]

                    def seg_(x, off=0):
                        return x[:, :, off + bt * 128:off + bt * 128 + 128].rearrange("p k (c t) -> p k c t", c=4)

                    tot = cc[:, :, :, 31]
                    h_b = [V.last, T.last, A.last]
                    pcv = PC.rearrange("p (a c) -> p a c", a=8)
                    A.act(pcv, tot, ACT.Exp, h_b, h_prev_batch, scale=-EXPM05)
                    if d == 0:
                        V.tt(E2v, cc, ss, ALU.subtract, h_b, h_prev_batch)
                        incl = cc
                    else:
                        V.tt(E2v, bc(tot, 3, 32), cc, ALU.subtract, h_b, h_prev_batch)
                        V.tt(E1v, E2v, ss, ALU.add)
                        incl = E1v
                    hE2 = V.last
                    hx3 = A.act(E2v, E2v, ACT.Exp, hE2, scale=-EXPM05)
                    V.stt(ARv[:, :, :, 0, :], seg_(kk), -1.0, E2v, ALU.mult, ALU.mult, hx3)
                    if s == 0:
                        ha = A.act(E2v, incl, ACT.Exp, V.last, scale=-EXPM05)
                        V.tt(ARv[:, :, :, 1, :], seg_(r), E2v, ALU.mult, ha)
                    ha = A.act(E2v, incl, ACT.Exp, V.last, scale=EXPM05)
                    V.tt(BKv[:, :, :, 0, :], seg_(b_), E2v, ALU.mult, ha)
                    hbk = V.tt(BKv[:, :, :, 1, :], seg_(k_), E2v, ALU.mult)
                    ne_ = 2 if s == 0 else 1
                    for c in range(4):
                        b = bank()
                        m = None
                        for h_ in range(16):
                            a, o = h_ // 2, 64 * (h_ % 2)
                            m = T.mm(b.t[o:o + 64, a * 32 * ne_:(a + 1) * 32 * ne_],
                                     BKv[o:o + 64, a, c, :, :].rearrange("p e t -> p (e t)"),
                                     ARv[o:o + 64, a, c, 0:ne_, :].rearrange("p e t -> p (e t)"), True, True,
                                     hbk, b.free)
                        b.free = [V.tt(GTv[:, c, :, 0:32 * ne_], b.t[:, 0:256 * ne_].rearrange("p (a n) -> p a n", a=8),
                                       bc(mG[:, 0:32 * ne_], 1, 8), ALU.mult, m, hL)]
                    for dst, mask_, up in ((U, mU, True), (L, mL, False)):
                        b = bank()
                        m = None
                        for c in range(4):
                            for h_ in range(16):
                                a, o, g = h_ // 2, 64 * (h_ % 2), 32 * (h_ % 4)
                                x_, y_ = BKv[o:o + 64, a, c, 0, :], ARv[o:o + 64, a, c, 0, :]
                                if not up:
                                    x_, y_ = y_, x_
                                m = T.mm(b.t[g:g + 32, c * 128 + (h_ // 4) * 32:c * 128 + (h_ // 4) * 32 + 32], x_, y_,
                                         True, True, hbk, b.free)
                        b.free = [V.tt(q4(dst), b.t[:, :].rearrange("p (c g n) -> p c g n", c=4, g=4),
                                       bc(bc(mask_, 1, 4), 1, 4), ALU.mult, m, hL)]
                    iden = bc(bc(I32, 1, 4), 1, 4)
                    V.tt(q4(Yi), q4(U), bc(bc(mU1, 1, 4), 1, 4), ALU.mult)
                    V.tt(q4(Yi), q4(Yi), iden, ALU.add)
                    V.tt(q4(YTi), q4(L), bc(bc(mBL[0], 1, 4), 1, 4), ALU.mult)
                    V.tt(q4(YTi), q4(YTi), iden, ALU.add)
                    hY = V.last

                    def prods(b, lhs, rhs, *w):
                        m = None
                        for c in range(4):
                            for gf in range(4):
                                for g in range(4):
                                    o, f = 32 * g, c * 128 + gf * 32
                                    m = T.mm(b.t[o:o + 32, f:f + 32], lhs[o:o + 32, f:f + 32], rhs[o:o + 32, f:f + 32],
                                             True, True, w, b.free)
                        return m

                    for lev in range(1, 5):
                        hB = V.tt(q4(BL), q4(L), bc(bc(mBL[lev], 1, 4), 1, 4), ALU.mult, T.last)
                        b = bank()
                        m = prods(b, BL, Yi, hB, hY)
                        h1 = A.cp(T1, b.t[:, :], m)
                        b.free = [h1]
                        b = bank()
                        m = prods(b, YTi, T1, h1)
                        b2 = None
                        if lev < 4:
                            b2 = bank()
                            m2 = prods(b2, T1, YTi, h1)
                            V.tt(Yi, Yi, b.t[:, :], ALU.add, m)
                            b.free = [V.last]
                            V.tt(YTi, YTi, b2.t[:, :], ALU.add, m2)
                            b2.free = [V.last]
                        else:
                            V.tt(Yi, Yi, b.t[:, :], ALU.add, m)
                            b.free = [V.last]
                        hY = V.last
                    order = range(4) if d == 0 else range(3, -1, -1)
                    for n_, c in enumerate(order):
                        i = n_ % 2
                        hb_ = []
                        b = bank()
                        m = None
                        for h_ in range(16):
                            a, o = h_ // 2, 64 * (h_ % 2)
                            m = T.mm(b.t[o:o + 64, a * 64:a * 64 + 64],
                                     BKv[o:o + 64, a, c, :, :].rearrange("p e t -> p (e t)"),
                                     ident[o:o + 64, o:o + 64], True, True, hbk, b.free)
                        b.free = [V.cp(BKt[i], b.t[:, :], m, rows[i], h_b)]
                        hb_.append(V.last)
                        b = bank()
                        t0 = bt * 128 + c * 32
                        for h_ in range(16):
                            a, o = h_ // 2, 64 * (h_ % 2)
                            m = T.mm(b.t[o + 32:o + 64, a * 64:a * 64 + 64], vT[o:o + 64, a, t0:t0 + 32],
                                     ident[o:o + 64, o:o + 64], True, True, ready, b.free)
                        e1 = V.cp(VS[i][32:64, :], b.t[32:64, :], m, rows[i], h_b)
                        e2 = A.cp(VS[i][96:128, :], b.t[96:128, :], m, rows[i], h_b)
                        b.free = [e1, e2]
                        hb_ += [e1, e2]
                        bkt = BKt[i].rearrange("p (a v) -> p a v", a=8)
                        vs_ = VS[i].rearrange("p (a v) -> p a v", a=8)
                        b = bank()
                        m = None
                        for h_ in range(16):
                            a, o, g = h_ // 2, 64 * (h_ % 2), 32 * (h_ % 4)
                            dst = b.t[g:g + 32, (h_ // 4) * 64:(h_ // 4) * 64 + 64]
                            T.mm(dst, ARv[o:o + 64, a, c, 0, :], Z[d][o:o + 64, a, :], True, False, h_z, b.free, hbk)
                            m = T.mm(dst, GTv[o + 32:o + 64, c, a, 0:32], vs_[o + 32:o + 64, a, :], False, True, hb_)
                        hT_ = A.cp(Ts, b.t[:, 0:256], m, h_b)
                        b.free = [hT_]
                        hs_ = []
                        vv = VS[i].rearrange("p (a e v) -> p a e v", a=4, e=2)
                        for e in range(2):
                            b = bank()
                            for a2 in range(4):
                                for par in range(2):
                                    h_ = 4 * a2 + 2 * e + par
                                    o, g = 64 * par, 32 * (h_ % 4)
                                    f = c * 128 + a2 * 32
                                    m = T.mm(b.t[o:o + 32, a2 * 64:a2 * 64 + 64], Yi[g:g + 32, f:f + 32],
                                             Ts[g:g + 32, a2 * 64:a2 * 64 + 64], True, True, hT_, hY, b.free)
                            s1 = V.cp(vv[0:32, :, e, :], b.t[0:32, 0:256].rearrange("p (a v) -> p a v", a=4), m)
                            s2 = A.cp(vv[64:96, :, e, :], b.t[64:96, 0:256].rearrange("p (a v) -> p a v", a=4), m)
                            b.free = [s1, s2]
                            hs_ += b.free
                        s1 = s2 = hs_
                        if s == 0:
                            b = bank()
                            for h_ in range(16):
                                a, o = h_ // 2, 64 * (h_ % 2)
                                dst = b.t[o:o + 64, a * 32:a * 32 + 32]
                                T.mm(dst, Z[d][o:o + 64, a, :], ARv[o:o + 64, a, c, 1, :], True, False, b.free, h_z)
                                m = T.mm(dst, vs_[o:o + 64, a, :], GTv[o:o + 64, c, a, 32:64], False, True, s1, s2)
                            t0 = bt * 128 + c * 32
                            b.free = [A.cp(Y[:, :, t0:t0 + 32], b.t[:, 0:256].rearrange("p (a t) -> p a t", a=8), m, ready)]
                        b = bank()
                        for h_ in range(16):
                            a, o = h_ // 2, 64 * (h_ % 2)
                            m = T.mm(b.t[o:o + 64, a * 64:a * 64 + 64], bkt[o:o + 64, a, :], vs_[o:o + 64, a, :],
                                     True, True, b.free, s1, s2, hb_)
                        rows[i] = m
                        V.tt(Z[d], Z[d], b.t[:, :].rearrange("p (a v) -> p a v", a=8), ALU.add, m)
                        b.free = [V.last]
                        h_z = V.tt(Z[d], Z[d], bc(pcv[:, :, c], 2, 64), ALU.mult)
                return [V.last, A.last, T.last]

            scanm = ones_period
            fr = features(1, start)
            e0 = scan(1, 0, [fr, everyone()], None)
            e1 = scan(1, 1, [e0, everyone()], None)
            fr = features(0, [e1, everyone()])
            ar.o = base
            Ys = [v8(ar.take(2048)) for _ in range(2)]
            e0 = scan(0, 0, [fr, everyone()], Ys[0])
            e1 = scan(0, 1, [e0, everyone()], Ys[1])
            after = [e1, everyone()]
            ar.o = base + 4096
            tq, Oh, bonus = (v8(ar.take(2048)) for _ in range(3))
            SG = [ar.take(256) for _ in range(2)]
            V.tt(bonus, r, k_, ALU.mult, after)
            for k in range(8):
                V.ts(bonus[:, k, :], bonus[:, k, :], vec("r_k")[:, k:k + 1], None, ALU.mult, None)
            head_sums(bonus, V.last, lambda q, t, m: V.tt(bonus[:, 2 * q:2 * q + 2, :],
                                                          vT[:, 2 * q:2 * q + 2, :], t, ALU.mult, m))
            hO = None
            for d in range(2):
                p1 = load(D["g1"][d])
                w = p1.ap[:, 0:1024].rearrange("p (k c) -> p k c", k=8)
                b = bank()
                m = T.group(b.t[:, 0:256], [(w[:, k, :], xg[:, k, :]) for k in range(8)], p1.h, b.free, after)
                p1.rel = m
                hs = A.act(SG[d], b.t[:, 0:256], ACT.Sigmoid, m, after)
                b.free = [hs]
                Yd = Ys[d]
                head_sums(Yd, after, lambda q, t, m: V.stt(Yd[:, 2 * q:2 * q + 2, :], t, -1.0 / 64, Yd[:, 2 * q:2 * q + 2, :],
                                                           ALU.mult, ALU.add, m))
                hq_ = A.act(tq, Yd, ACT.Square, V.last, hO)
                head_sums(tq, hq_, lambda q, t, m: A.act(tq[:, 2 * q:2 * q + 2, :], t, ACT.Sqrt, m, bias=epsg[:, 0:1],
                                                         scale=1.0 / 64))
                V.rcp(tq, tq, A.last)
                V.tt(Yd, Yd, tq, ALU.mult)
                for k in range(8):
                    V.ts(Yd[:, k, :], Yd[:, k, :], vec("gn_g")[:, k:k + 1], vec("gn_b")[:, k:k + 1], ALU.mult, ALU.add)
                V.tt(Yd, Yd, bonus, ALU.add)
                p2 = load(D["g2"][d])
                for q in range(4):
                    b = bank()
                    for c in range(2):
                        mt = 2 * q + c
                        m = T.mm(b.t[:, c * 256:c * 256 + 256], p2.ap[:, mt * 128:mt * 128 + 128], SG[d], True, True,
                                 p2.h, hs, b.free)
                    tv = b.t[:, :].rearrange("p (c t) -> p c t", c=2)
                    V.tt(Yd[:, 2 * q:2 * q + 2, :], Yd[:, 2 * q:2 * q + 2, :], tv, ALU.mult, m)
                    b.free = [V.last]
                p2.rel = m
                hO = V.last
            V.tt(Oh, Ys[0], Ys[1], ALU.add, after)
            hO = V.last
            for i in range(4):
                p = load(D["rw_o"][i])
                w = p.ap.rearrange("p (k c) -> p k c", k=8)
                for c in range(2):
                    b = bank()
                    m = T.group(b.t[:, 0:256], [(w[:, k, c * 128:c * 128 + 128], Oh[:, k, :]) for k in range(8)],
                                p.h, b.free, hO)
                    add_gated(1, 0, 2 * i + c, b, m, 1)
                p.rel = m
            return V.last

        ones_period = sb("ones_period", 128)[:, :]
        V.ms(ones_period, 1.0)
        h_scanm = V.ms(ones_period.rearrange("p (c t) -> p c t", c=4)[:, :, 0:1], 0.0)

        hx = fetch("x", XS[:, :].rearrange("p (t n) -> p t n", t=2),
                   (D["x0"] if "x0" in D else D["x"]).rearrange("(t p) n -> p t n", p=128))
        for l in range(2):
            if f"m{l}" in parts:
                hm = ada1(l, everyone())
                hx = mixer(l, [hx, hm], hm)
            if f"e{l}" in parts:
                hx = moe(l, hx)
        if "a" in parts or "b" in parts:
            hx = block2(hx)
        s_out = sem("s_out")
        S.add(lambda: nc.sync.dma_start(out.rearrange("(t p) n -> p t n", p=128),
                                        XS[:, :].rearrange("p (t n) -> p t n", t=2)).then_inc(s_out, 16) and None, [hx])
        S.add(lambda: None, [Landed(s_out, 16)])
        for q in (T, A, V, G, S):
            q.number()
        block = ctx.enter_context(nc.Block())

        @block.sync
        def _(eng):
            S.play(eng)

        @block.tensor
        def _(eng):
            T.play(eng)

        @block.scalar
        def _(eng):
            A.play(eng)

        @block.vector
        def _(eng):
            V.play(eng)

        @block.gpsimd
        def _(eng):
            G.play(eng)


def cols_i(w, n=256):
    N = w.shape[1]
    return np.ascontiguousarray(w.reshape(128, 8, N // n, n).transpose(2, 0, 1, 3)).reshape(N // n, 128, 8 * n)


def cols_s(w, n=256):
    K, N = w.shape[0] // 128, w.shape[1]
    return np.ascontiguousarray(w.reshape(K, 128, N // n, n).transpose(2, 1, 0, 3)).reshape(N // n, 128, K * n)


def vi(v):
    return np.asarray(v).reshape(128, -1)


def vs(v):
    return np.ascontiguousarray(np.asarray(v).reshape(-1, 128).T)


def both(a, f):
    return np.stack([f(a[l]) for l in range(a.shape[0])])


def layout(I):
    I = {k: np.asarray(v) for k, v in I.items()}
    A = {}
    A["x"] = I["x"].reshape(256, 1024)
    A["cond"] = np.concatenate([vi(I["c"][0]), vi(I["c_2"][0]), vi(I["c_ctx_2"]), vi(I["c_ctx_2"])], 1)
    cols, off, n = [], {}, 0

    def put(name, a):
        nonlocal n
        a = np.asarray(a, dtype=a.dtype)
        cols.append(a)
        off[name] = n
        n += a.shape[1]

    for l in range(2):
        b = I["b_ada"][l].reshape(6, 1024)
        put(f"b_ada{l}", np.concatenate([vi(b[i]) for i in (0, 1, 3, 4)], 1))
        put(f"b_sp{l}", np.ascontiguousarray(I["b_spatial"][l].T))
    b2 = I["ada_b_2"]
    for l in range(2):
        put(f"b2_{l}", np.concatenate([vs(b2[l].reshape(6, 1024)[i]) for i in range(6)], 1))
        put(f"n1g{l}", vs(I["norm1_g_2"][l]))
        put(f"n2g{l}", vs(I["norm2_g_2"][l]))
    for m in range(6):
        put(f"mu{m}", vs(I["rwkv_mu_2"][0, m]))
    put("w0_0", vs(I["rwkv_w0_2"][0, 0]))
    put("w0_1", vs(I["rwkv_w0_2"][0, 1]))
    put("a0", vs(I["rwkv_a0_2"][0]))
    put("k_k", vs(I["rwkv_k_k_2"][0]))
    put("k_a", vs(I["rwkv_k_a_2"][0]))
    put("r_k", vs(I["rwkv_r_k_2"][0].reshape(-1)))
    put("gn_g", vs(I["rwkv_gn_g_2"][0]))
    put("gn_b", vs(I["rwkv_gn_b_2"][0]))
    A["vecs"] = np.concatenate(cols, 1)

    def ada_one(w):
        w = w.reshape(1024, 6, 128, 8)
        outs = []
        for i in range(6):
            wi = w[:, i]
            wi = wi.reshape(1024, 1024) if i in (2, 5) else wi.transpose(0, 2, 1).reshape(1024, 1024)
            outs.append(cols_i(wi))
        return np.concatenate(outs, 0)

    A["w_ada"] = both(I["w_ada"], ada_one)
    A["b_gate"] = np.stack([np.concatenate([I["b_ada"][l].reshape(6, 1024)[2], I["b_ada"][l].reshape(6, 1024)[5]]) for l in range(2)])
    A["w_in"] = both(I["w_in"], cols_i)
    A["qk_gain"] = np.stack([np.concatenate([np.tile(I["q_scale"][l], 8), np.tile(I["k_scale"][l], 2)]) for l in range(2)])
    A["sgu_g"], A["sgu_b"] = I["sgu_ln_g"], I["sgu_ln_b"]
    A["ln1_g"], A["ln1_b"], A["ln2_g"], A["ln2_b"] = I["ln1_g"], I["ln1_b"], I["ln2_g"], I["ln2_b"]
    A["w_sp"] = both(I["w_spatial"], lambda w: np.ascontiguousarray(w.transpose(2, 0, 1)).reshape(128, 1024))
    A["w_ba"] = both(I["w_branch_a"], lambda w: cols_s(w, 512))
    A["w_bb"] = both(I["w_branch_b"], lambda w: cols_s(w, 512))
    A["w_out"] = both(I["w_out"], cols_s)
    A["router_w"] = I["router_w"].reshape(2, 128, 512)
    A["router_b"] = I["router_bias"]
    A["w_gate"] = I["w_gate"].reshape(2, 64, 128, 2048)
    A["w_up"] = I["w_up"].reshape(2, 64, 128, 2048)
    A["w_down"] = I["w_down"]
    A["ws_gate"] = I["ws_gate"].reshape(2, 128, 2048)
    A["ws_up"] = I["ws_up"].reshape(2, 128, 2048)
    A["ws_down"] = I["ws_down"]
    A["ltri"] = np.tril(np.ones((8, 8), np.float32), -1).reshape(64)
    A["tri"] = np.concatenate([np.triu(np.ones((128, 128))), np.tile(np.arange(64.0), (128, 1))], 1).astype(np.float32)
    t = np.arange(256)
    row, col = (t // 64 - 2).astype(np.float32), (t % 64 - 32).astype(np.float32)
    inv = (np.float32(10000.0) ** (-np.arange(16, dtype=np.float32) / np.float32(16))).astype(np.float32)
    ang = np.concatenate([row[:, None] * inv, col[:, None] * inv], -1)
    c, s = np.cos(ang).astype(np.float32), np.sin(ang).astype(np.float32)
    C = np.repeat(c, 2, 1)
    Sg = np.stack([-s, s], -1).reshape(256, 64)
    A["rope1"] = np.ascontiguousarray(np.stack([C, Sg]).reshape(2, 2, 128, 64).transpose(2, 0, 1, 3)).reshape(128, 256)
    A.update(layout2(I))
    return A, off


def layout2(I):
    A = {}
    A["ada2"] = both(I["ada_w_2"], cols_i)
    A["ctx"] = I["ctx_2"].reshape(256, 1024)
    A["wqkv"] = cols_s(I["att_w_qkv_2"][0])
    A["gain2"] = np.concatenate([np.tile(I["att_q_gain_2"][0], 16), np.tile(I["att_k_gain_2"][0], 4)])
    A["sink"] = I["att_sink_2"][0]
    A["w_o"] = cols_s(I["att_w_o_2"][0])
    A["mlp1"] = both(I["mlp_w1_2"], cols_s)
    A["mlp2"] = both(I["mlp_w2_2"], lambda w: np.ascontiguousarray(
        w.reshape(2, 16, 128, 8, 128).transpose(3, 0, 2, 1, 4)).reshape(8, 2, 128, 2048))
    A["w_rkv"] = both(I["rwkv_w_rkv_2"][0], cols_s)
    w1 = I["rwkv_w1_2"][0]
    A["w1"] = cols_s(np.concatenate([w1[0], w1[1]], 1), 128)[0]
    A["w2"] = I["rwkv_w2_2"][0].reshape(128, 1024)
    A["a1"] = cols_s(I["rwkv_a1_2"][0], 64)[0]
    A["a2"] = np.concatenate([I["rwkv_a2_2"][0], I["rwkv_a2_2"][0]], 0)
    A["g1"] = both(I["rwkv_g1_2"][0], lambda w: cols_s(w, 128)[0])
    A["g2"] = I["rwkv_g2_2"][0]
    A["rw_o"] = cols_s(I["rwkv_w_o_2"][0])
    t = np.arange(256)
    inv = (np.float32(10000.0) ** (-np.arange(16, dtype=np.float32) / np.float32(16))).astype(np.float32)
    ar, ac = (t // 64).astype(np.float32)[:, None] * inv, (t % 64).astype(np.float32)[:, None] * inv
    C = np.concatenate([np.cos(ar), np.cos(ar), np.cos(ac), np.cos(ac)], 1)
    Sg = np.concatenate([-np.sin(ar), np.sin(ar), -np.sin(ac), np.sin(ac)], 1)
    A["rope2"] = np.ascontiguousarray(
        np.stack([C, Sg]).astype(np.float32).reshape(2, 2, 128, 64).transpose(2, 0, 1, 3)).reshape(128, 256)
    m = np.where(np.abs(t[:, None] - t[None, :]) <= 128, 0.0, -1e30).astype(np.float32)
    A["mask"] = np.ascontiguousarray(m.reshape(2, 128, 256).transpose(1, 0, 2)).reshape(128, 512)
    A["blockones"] = np.kron(np.eye(2), np.ones((64, 64))).astype(np.float32)
    i = np.arange(32)
    up, inc = (i[:, None] < i[None, :]).astype(np.float32), (i[:, None] <= i[None, :]).astype(np.float32)

    def half(m_):
        same = i[:, None] // (2 * m_) == i[None, :] // (2 * m_)
        return (same & (i[:, None] % (2 * m_) < m_) & (i[None, :] % (2 * m_) >= m_)).astype(np.float32)

    parts = []
    for d in range(2):
        f = (lambda x: x) if d == 0 else (lambda x: x.T)
        g = np.concatenate([f(up), f(inc)], 1)
        parts.append(np.tile(g, (4, 1)))
        parts.append(np.tile(f(up), (4, 1)))
        parts.append(np.tile(f(up).T, (4, 1)))
        parts.append(np.tile(f(half(1)), (4, 1)))
        for lev in range(5):
            parts.append(np.tile(f(half(2 ** lev)).T, (4, 1)))
    parts.append(np.tile(np.eye(32, dtype=np.float32), (4, 1)))
    A["scan_c"] = np.ascontiguousarray(np.concatenate(parts, 1).astype(np.float32))
    return A


def kernel(**inputs):
    import concourse.bacc as bacc
    from concourse.bass_utils import run_bass_kernel_spmd

    arrays, off = layout(inputs)
    nc = bacc.Bacc("TRN2", target_bir_lowering=False, num_devices=1)
    D, given = {}, {}
    for name, a in arrays.items():
        if name in ("w_down", "ws_down"):
            t = nc.dram_tensor("in_" + name, a.shape, F32, kind="ExternalInput").ap()
            D[name] = t.rearrange("l e (j p) d -> l e p j d", p=128) if name == "w_down" else t.rearrange("l (j p) d -> l p j d", p=128)
        else:
            D[name] = nc.dram_tensor("in_" + name, a.shape, F32, kind="ExternalInput").ap()
        given["in_" + name] = np.ascontiguousarray(a)
    D["voff"] = off
    out = nc.dram_tensor("out_x", (256, 1024), F32, kind="ExternalOutput").ap()
    program(nc, D, out)
    r = run_bass_kernel_spmd(nc, [given], core_ids=[0])
    return r.results[0]["out_x"].reshape(1, 256, 1024)
```

```python
import math
from contextlib import ExitStack

import numpy as np

import concourse.bass as bass
from concourse import mybir
from concourse.alu_op_type import AluOpType as ALU

ACT = mybir.ActivationFunctionType
F32 = mybir.dt.float32
F32R = mybir.dt.float32r
AX = mybir.AxisListType.X

ALPHA = 4.0 ** 0.25
NRING = 5
NEXTRA = 7
NROUND = 7424
NPUMP = (12, 8)
ARENA = 35144
EXPM05 = math.exp(-0.5)


class Mark:

    def __init__(self, queue):
        self.queue, self.value, self.needed = queue, None, False

    def where(self):
        return self.queue.sem, self.value


class Landed:

    def __init__(self, sem, value):
        self.sem, self.value, self.needed = sem, value, False

    def where(self):
        return self.sem, self.value


def flat(xs):
    for x in xs:
        if isinstance(x, (list, tuple)):
            yield from flat(x)
        elif x is not None:
            yield x


class Fork:

    def __init__(self, queue, flag, after):
        self.flag, self.after, self.ways, self.ends, self.join = flag, list(flat(after)), ([], []), None, Mark(queue)
        for m in self.after:
            m.needed = True


class Queue:

    def __init__(self, sem, linked):
        self.sem, self.linked, self.ops, self.last = sem, linked, [], None
        self.now = self.ops

    def add(self, fn, after):
        after = list(flat(after))
        if self.linked and self.last is not None:
            after.append(self.last)
        for m in after:
            m.needed = True
        mark = Mark(self)
        self.now.append((fn, after, mark))
        self.last = mark
        return mark

    def number(self, ops=None, n=0):
        for op in self.ops if ops is None else ops:
            if isinstance(op, Fork):
                op.ends = [self.number(way, n) for way in op.ways]
                n = op.join.value = max(op.ends)
            else:
                n += op[2].needed
                op[2].value = n
        return n

    def play(self, eng, ops=None, seen=None):
        seen = {} if seen is None else seen
        for op in self.ops if ops is None else ops:
            after = op.after if isinstance(op, Fork) else op[1]
            for m in after:
                sem, value = m.where()
                if seen.get(sem.num, 0) < value:
                    eng.wait_ge(sem, value)
                    seen[sem.num] = value
            if isinstance(op, Fork):
                flag = eng.value_load(op.flag, min_val=0, max_val=1)
                copies = [dict(seen), dict(seen)]
                with eng.If(flag):
                    self.way(eng, op, 1, copies[1])
                with eng.Else():
                    self.way(eng, op, 0, copies[0])
                seen.clear()
                seen.update({k: min(v, copies[1][k]) for k, v in copies[0].items() if k in copies[1]})
            else:
                ins = op[0]()
                if op[2].needed and ins is not None:
                    ins.then_inc(self.sem, 1)

    def way(self, eng, op, i, seen):
        self.play(eng, op.ways[i], seen)
        short = op.join.value - op.ends[i]
        if short:
            eng.wait_ge(self.sem, op.ends[i])
            eng.sem_inc(self.sem, short)


class Tensor(Queue):
    def __init__(self, nc, sem):
        super().__init__(sem, False)
        self.e = nc.tensor

    def mm(self, out, lhsT, rhs, start, stop, *after):
        return self.add(lambda: self.e.matmul(out, lhsT, rhs, start=start, stop=stop), after)

    def tr(self, out, in_, ident, *after):
        return self.add(lambda: self.e.transpose(out, in_, ident), after)

    def group(self, out, pairs, *after):
        n = len(pairs)
        m = None
        for i, p in enumerate(pairs):
            m = self.mm(out, p[0], p[1], i == 0, i == n - 1, after if i == 0 else (), *p[2:])
        return m


class Scalar(Queue):
    def __init__(self, nc, sem):
        super().__init__(sem, True)
        self.e = nc.scalar

    def act(self, out, in_, func, *after, bias=0.0, scale=1.0, accum=None):
        if accum is None:
            return self.add(lambda: self.e.activation(out, in_, func, bias=bias, scale=scale), after)
        return self.add(lambda: self.e.activation(out, in_, func, bias=bias, scale=scale, accum_out=accum), after)

    def cp(self, out, in_, *after):
        return self.act(out, in_, ACT.Copy, *after)

    def fma(self, out, in_, scale, bias, *after):
        return self.act(out, in_, ACT.Identity, *after, bias=bias, scale=scale)


class Vector(Queue):
    def __init__(self, nc, sem, e):
        super().__init__(sem, True)
        self.e = e

    def tt(self, out, a, b, op, *after):
        return self.add(lambda: self.e.tensor_tensor(out, a, b, op), after)

    def stt(self, out, a, s, b, op0, op1, *after):
        return self.add(lambda: self.e.scalar_tensor_tensor(out, a, s, b, op0, op1), after)

    def ts(self, out, a, s1, s2, op0, op1, *after):
        if op1 is None:
            return self.add(lambda: self.e.tensor_scalar(out, a, s1, None, op0), after)
        return self.add(lambda: self.e.tensor_scalar(out, a, s1, s2, op0, op1), after)

    def fma(self, out, in_, scale, bias, *after):
        return self.ts(out, in_, scale, bias, ALU.mult, ALU.add, *after)

    def red(self, out, a, op, *after, negate=False):
        if negate:
            return self.add(lambda: self.e.tensor_reduce(out, a, AX, op, negate=True), after)
        return self.add(lambda: self.e.tensor_reduce(out, a, AX, op), after)

    def rcp(self, out, a, *after):
        return self.add(lambda: self.e.reciprocal(out, a), after)

    def cp(self, out, a, *after):
        return self.add(lambda: self.e.tensor_copy(out, a), after)

    def ms(self, out, v, *after):
        return self.add(lambda: self.e.memset(out, v), after)

    def top8(self, out, a, *after):
        return self.add(lambda: self.e.max(out, a), after)

    def drop8(self, out, vals, a, imm, *after):
        return self.add(lambda: self.e.match_replace(out, vals, a, imm), after)

    def bns(self, out, a, *after):
        return self.add(lambda: self.e.bn_stats(out, a), after)

    def bna(self, out, a, *after):
        return self.add(lambda: self.e.bn_aggr(out, a), after)

    def scan(self, out, a, b, *after):
        return self.add(lambda: self.e.tensor_tensor_scan(out, a, b, 0.0, ALU.mult, ALU.add), after)

    def sel(self, out, pattern, op, fill, base, cm, *after):
        return self.add(lambda: self.e.affine_select(out=out, in_=out, compare_op=op, fill=fill, base=base,
                                                     pattern=pattern, channel_multiplier=cm), after)


def bc(a, dim, n):
    dims = [list(d) for d in a.ap]
    dims.insert(dim, [0, n])
    return bass.AP(a.tensor, a.offset, dims)


def f32(a):
    return a.bitcast(F32)


class Bank:
    def __init__(self, t):
        self.t, self.free = t, []


class Piece:
    def __init__(self, ap, landed):
        self.ap, self.h, self.rel = ap, landed, None


def program(nc, D, out, opts=None):
    opts = opts or {}
    parts = opts.get("parts", "m0 e0 m1 e1 a b")
    ctx = ExitStack()
    with ctx:
        def sb(name, n):
            return ctx.enter_context(nc.sbuf_tensor(name, [128, n], F32))

        def sem(name):
            return ctx.enter_context(nc.semaphore(name))

        ring = sb("ring", NRING * 2048)
        with nc.sbuf_tensor("rounded", [128, NROUND], F32R) as rounded:
            pass
        arena = sb("arena", ARENA)
        XS = sb("XS", 2048)
        ident = sb("ident", 128)
        ones = sb("ones", 128)
        eps5 = sb("eps5", 1)
        eps6 = sb("eps6", 1)
        epsg = sb("epsg", 1)
        cond = sb("cond", 8 * 4)
        condr = sb("condr", 8 * 64)
        mod1 = sb("mod1", 2 * 32)
        mod2 = sb("mod2", 2 * 96)
        vecs = sb("vecs", D["vecs"].shape[1])
        stage = sb("stage", 2 * 256)
        small = sb("small", 512)
        flags = ctx.enter_context(nc.sbuf_tensor("flags", [128, 64], mybir.dt.int32))
        banks = [Bank(ctx.enter_context(nc.psum_tensor(f"ps{i}", [128, 512], F32))) for i in range(8)]

        T = Tensor(nc, sem("s_pe"))
        A = Scalar(nc, sem("s_act"))
        V = Vector(nc, sem("s_dve"), nc.vector)
        G = Vector(nc, sem("s_pool"), nc.gpsimd)
        G.linked = False
        S = Queue(sem("s_sp"), False)
        engines = [T, A, V]

        def everyone():
            return [q.last for q in engines if q.last is not None]

        def barrier():
            return everyone()

        ring_sems = [sem(f"s_ring{i}") for i in range(NRING + NEXTRA)]
        slots = [ring[:, i * 2048:i * 2048 + 2048] for i in range(NRING)]
        slots += [arena[:, ARENA - (i + 1) * 2048:ARENA - i * 2048] for i in range(NEXTRA)]
        user, uses, at = [None] * len(slots), [0] * len(slots), [0]
        extra_after = [None]

        big_ring = [False]

        def load(src, shape=None):
            big = big_ring[0]
            slot = at[0] % (NRING + NEXTRA if big else NRING)
            at[0] = slot + 1
            flat_ap = slots[slot]
            if shape is None:
                width = src.shape[1]
                dst = flat_ap[:, 0:width]
            else:
                dst = flat_ap.rearrange("p (a b) -> p a b", a=shape)
            prev = user[slot]
            s = ring_sems[slot]
            S.add(lambda: nc.sync.dma_start(dst, src).then_inc(s, 16) and None,
                  [prev.rel, prev.h] if prev else [], )
            if slot >= NRING:
                S.now[-1][1].extend(flat([extra_after[0]]))
                for m_ in flat([extra_after[0]]):
                    m_.needed = True
            uses[slot] += 1
            p = Piece(flat_ap, Landed(s, 16 * uses[slot]))
            user[slot] = p
            return p

        def fork(flag, after, sparse, dense):
            qs = (T, A, V)
            fs = [Fork(q, flag, after) for q in qs]
            lasts, nows, frees = [q.last for q in qs], [q.now for q in qs], [b.free for b in banks]
            for i, way in enumerate((sparse, dense)):
                for q, f, last in zip(qs, fs, lasts):
                    q.now, q.last = f.ways[i], last
                for b, fr in zip(banks, frees):
                    b.free = fr
                way()
                for q in qs:
                    q.last.needed = True
            for q, f, now in zip(qs, fs, nows):
                q.now, q.last = now, f.join
                now.append(f)
            return [f.join for f in fs]

        side = {}

        def fetch(name, dst, src, *after, hw=False):
            if name not in side:
                side[name] = [sem("s_" + name), 0]
            s = side[name]
            s[1] += 16
            sm = s[0]
            if hw:
                S.add(lambda: nc.sync.dma_start(dst, src).then_inc(sm, 16) and None, after)
            else:
                G.add(lambda: nc.gpsimd.dma_start(dst, src).then_inc(sm, 16) and None, after)
            return Landed(sm, s[1])

        turn = [0]

        rotating = [banks]

        def bank():
            b = rotating[0][turn[0] % len(rotating[0])]
            turn[0] += 1
            return b

        flip = [0]

        def va():
            flip[0] += 1
            return V if flip[0] % 2 else A

        h_vec = fetch("c0", vecs[:, :], D["vecs"], hw=True)
        h_cond = fetch("c1", cond[:, :], D["cond"], hw=True)
        h_id = G.sel(ident[:, :], [[-1, 128]], ALU.not_equal, 1.0, 0, 1, G.ms(ident[:, :], 0.0))
        V.ms(ones[:, :], 1.0)
        V.ms(eps5[:, :], 1e-5)
        V.ms(eps6[:, :], 1e-6)
        h_one = V.ms(epsg[:, :], 64e-5)
        h = A.act(cond[:, :], cond[:, :], ACT.Silu, h_cond)
        cr = condr[:, :].rearrange("p (b k c) -> p b k c", b=2, k=8)
        V.cp(cr[:, 0, :, :], bc(cond[:, 0:8], 2, 32), h)
        V.cp(cr[:, 1, :, 0:16], bc(cond[:, 8:16], 2, 16))
        h_cr = V.cp(cr[:, 1, :, 16:32], bc(cond[:, 16:24], 2, 16))
        const = [h_vec, h_id, h_one]

        VO = D["voff"]

        def vec(name, n=8):
            o = VO[name]
            return vecs[:, o:o + n]

        stage_free = [None, None]
        stage_n = [0]

        def ada_rows(src, blk, waits=()):
            p = load(src)
            w = p.ap.rearrange("p (k c) -> p k c", k=8)
            b = bank()
            m = None
            for k in range(8):
                j = k % 4
                m = T.mm(b.t[32 * j:32 * j + 32, 0:256], cr[:, blk, k, :], w[:, k, :], k < 4, k >= 4,
                         p.h, h_cr, b.free, waits)
            p.rel = m
            n = stage_n[0] % 2
            stage_n[0] += 1
            st = stage[:, n * 256:n * 256 + 256]
            h = V.cp(st, b.t[:, 0:256], m, stage_free[n])
            b.free = [h]
            return st, n, h

        ones32 = sb("ones32", 128)
        routing = sb("routing", 832)
        rw, rb, ltri, tri = (routing[:, i:j] for i, j in ((0, 512), (512, 576), (576, 640), (640, 832)))
        h_router = {}
        h_tri = fetch("tri", ltri, D["ltri"].partition_broadcast(128))
        h_tri = fetch("tri", tri, D["tri"])
        h_o32 = V.ms(ones32[:, :], 1.0 / 32)

        h_mod = {}
        gates = sb("gates", 2 * 1024)
        gate = [gates[:, 0:1024], gates[:, 1024:2048]]
        waiting, open_piece, h_bias = [], [None], {}

        def ada_piece(blk, l, v, q):
            tag = (blk, l, v)
            kept = []

            def first():
                src = D["w_ada" if blk == 0 else "ada2"][l, v * 4 + q]
                if blk == 0 and v in (2, 5) and q == 0:
                    h_bias[tag] = fetch("gb", gate[v // 3], D["b_gate"][l][(v // 3) * 1024:(v // 3) * 1024 + 1024]
                                        .partition_broadcast(128), everyone())
                kept.append(ada_rows(src, blk))

            def second():
                st, n, h = kept[0]
                b = bank()
                if blk == 0 and v in (2, 5):
                    dst = gate[v // 3][:, q * 256:q * 256 + 256]
                    m = T.mm(b.t[:, 0:256], ones32[:, :], st, True, True, h, b.free, h_o32)
                    stage_free[n] = m
                    r = V.tt(dst, b.t[:, 0:256], dst, ALU.add, m, h_bias[tag])
                    b.free = [r]
                else:
                    m = None
                    for c in range(2):
                        m = T.tr(b.t[:, c * 128:c * 128 + 128], st[:, c * 128:c * 128 + 128], ident[:, :], h, b.free,
                                 h_id)
                    stage_free[n] = m
                    if blk == 0:
                        vi_ = {0: 0, 1: 1, 3: 2, 4: 3}[v]
                        view = b.t[:, 0:256].rearrange("p (c j r) -> p c j r", c=2, j=4)[:, :, :, 0]
                        tmp = small[:, 0:2]
                        o = l * 32 + vi_ * 8 + 2 * q
                        bo = VO[f"b_ada{l}"] + vi_ * 8 + 2 * q
                        dst, bias = mod1[:, o:o + 2], vecs[:, bo:bo + 2]
                    else:
                        view = b.t[:, 0:256].rearrange("p (c j s r) -> p c s j r", c=2, j=4, s=2)[:, :, :, :, 0]
                        tmp = small[:, 0:4].rearrange("p (c s) -> p c s", c=2)
                        o = l * 96 + v * 16 + 4 * q
                        bo = VO[f"b2_{l}"] + v * 8 + 2 * q
                        dst, bias = mod2[:, o:o + 4].rearrange("p (c s) -> p c s", c=2), bc(vecs[:, bo:bo + 2], 2, 2)
                    b.free = [V.red(tmp, view, ALU.add, m)]
                    one = 1.0 if blk == 0 and v in (1, 4) else 0.0
                    r = V.stt(dst, tmp, one, bias, ALU.add, ALU.add, h_vec)
                h_mod.setdefault(tag, []).append(r)

            return tag, first, second

        def pump():
            if open_piece[0] is not None:
                open_piece[0][2]()
                open_piece[0] = None
            if waiting:
                open_piece[0] = waiting.pop(0)
                open_piece[0][1]()

        def modulation(blk, l, *vs_):
            tags = [(blk, l, v) for v in vs_]
            while any(p[0] in tags for p in waiting + [open_piece[0]] if p is not None):
                pump()
            return [h_mod[t] for t in tags]

        def transposed(dst, l, which, after):
            hs = []
            o = l * 32 + which * 16
            xk = XS[:, :].rearrange("p (t d k) -> p t k d", t=2, k=8)
            for k2 in range(4):
                b = bank()
                m = None
                for kk in range(2):
                    for t in range(2):
                        c = kk * 256 + t * 128
                        m = T.tr(b.t[:, c:c + 128], xk[:, t, 2 * k2 + kk, :], ident[:, :], b.free, h_id, after)
                fr = []
                for kk in range(2):
                    k = 2 * k2 + kk
                    e = A if k2 % 2 else V
                    fr.append(e.fma(dst[:, k * 256:k * 256 + 256], b.t[:, kk * 256:kk * 256 + 256],
                                    mod1[:, o + 8 + k:o + 9 + k], mod1[:, o + k:o + k + 1], m, after))
                b.free = fr
                hs += fr
            return hs

        def ln_tok(t, g, bvec, hv, dst, after):
            st = small[:, 16:16 + 24].rearrange("p (t s c) -> p t s c", t=2, s=2)
            mv = small[:, 48:52].rearrange("p (t c) -> p t c", t=2)
            tv = t.rearrange("p (t n) -> p t n", t=2)
            dv = dst.rearrange("p (t n) -> p t n", t=2)
            for i in range(2):
                for s in range(2):
                    V.bns(st[:, i, s, :], tv[:, i, s * 512:s * 512 + 512], after)
                V.bna(mv[:, i, :], st[:, i, :, :])
            h = V.last
            rs = small[:, 52:54]
            A.act(rs, mv[:, :, 1], ACT.Sqrt, h, h_one, bias=eps5[:, 0:1])
            V.rcp(rs, rs, A.last)
            for i in range(2):
                V.ts(tv[:, i, :], tv[:, i, :], mv[:, i, 0:1], rs[:, i:i + 1], ALU.subtract, ALU.mult)
            V.tt(tv, tv, bc(g, 1, 2), ALU.mult, hv)
            return V.tt(dv, tv, bc(bvec, 1, 2), ALU.add, after)

        def rms_rope(src, tmp, nt, nh, gain, hg, cs, sn, swap, hr, nrope):
            ss = small[:, 64:64 + nt * nh].rearrange("p (t h) -> p t h", t=nt)
            V.tt(tmp, src, src, ALU.mult, hg, hr)
            V.red(ss, tmp, ALU.add)
            h = A.act(ss, ss, ACT.Sqrt, V.last, h_one, bias=eps6[:, 0:1], scale=1.0 / 64)
            V.rcp(ss, ss, h)
            V.tt(src, src, bc(ss, 3, 64), ALU.mult)
            V.tt(src, src, bc(gain, 1, nt), ALU.mult)
            for t in range(nrope):
                s_, t_ = src[:, t], tmp[:, t]
                a0, a1 = swap(s_)
                b0, b1 = swap(t_)
                for dst_, x_, n_ in ((b0, a1, 0), (b1, a0, 1)):
                    tab = swap(sn[:, t])[n_]
                    V.tt(dst_, x_, bc(tab, 1, nh), ALU.mult)
                V.tt(s_, s_, bc(cs[:, t], 1, nh), ALU.mult)
                V.tt(s_, s_, t_, ALU.add)
            return V.last

        def softmax_pv(jobs):
            return None

        def mixer(l, x_ready):
            h_router[l] = fetch("mo", rw, D["router_w"][l], everyone())
            h_router[l] = fetch("mo", rb, D["router_b"][l].partition_broadcast(128), everyone())
            a0 = [0]

            def take(n):
                v = arena[:, a0[0]:a0[0] + n]
                a0[0] += n
                assert a0[0] <= ARENA, a0
                return v

            start = barrier() + [x_ready]
            hT, PQ, PQt, Z = take(2048), take(1536), take(1280), take(2048)
            GS, qT, kT, oaT, obT, yT = take(4096), take(1024), take(512), take(1024), take(1024), take(2048)
            PP, PT = take(8 * 256), take(2 * 512)
            gain, tabs = take(640), take(256)
            sg, sbv, lg, lb = take(512), take(512), take(1024), take(1024)
            ws = take(1024)
            TM = take(1536)
            hL = fetch("mx", gain, D["qk_gain"][l].partition_broadcast(128), start)
            hL = fetch("mx", tabs, D["rope1"], start)
            hL = fetch("mx", sg, D["sgu_g"][l].partition_broadcast(128), start)
            hL = fetch("mx", sbv, D["sgu_b"][l].partition_broadcast(128), start)
            hL = fetch("mx", lg, D["ln1_g"][l].partition_broadcast(128), start)
            hL = fetch("mx", lb, D["ln1_b"][l].partition_broadcast(128), start)
            hL = fetch("mx", ws, D["w_sp"][l], start)
            hh = transposed(hT, l, 0, start + modulation(0, l, 0, 1))
            hv = hT.rearrange("p (k t) -> p k t", k=8)
            PQv = PQ.rearrange("p (t n) -> p t n", t=2)
            Zv = Z.rearrange("p (t n) -> p t n", t=2)
            GSv = GS.rearrange("p (m t) -> p m t", m=16)
            hq, hz, hg = [], [], []
            for i in range(7):
                p = load(D["w_in"][l, i])
                w = p.ap.rearrange("p (k c) -> p k c", k=8)
                for t in range(2):
                    b = bank()
                    m = T.group(b.t[:, 0:256], [(hv[:, k, t * 128:t * 128 + 128], w[:, k, :]) for k in range(8)],
                                p.h, b.free, hh)
                    if i < 3:
                        b.free = [V.cp(PQv[:, t, i * 256:i * 256 + 256], b.t[:, 0:256], m, start)]
                        hq += b.free
                    else:
                        b.free = [A.act(Zv[:, t, (i - 3) * 256:(i - 3) * 256 + 256], b.t[:, 0:256], ACT.Gelu, m, start)]
                        hz += b.free
                p.rel = m
            q4 = PQv[:, :, 0:640].rearrange("p t (h d) -> p t h d", h=10)
            t4 = PQt.rearrange("p (t h d) -> p t h d", t=2, h=10)
            tb = tabs.rearrange("p (c t d) -> p c t d", c=2, t=2)

            def pairs(v):
                if len(v.shape) == 3:
                    w_ = v.rearrange("p h (j e) -> p h j e", e=2)
                    return w_[:, :, :, 0], w_[:, :, :, 1]
                w_ = v.rearrange("p (j e) -> p j e", e=2)
                return w_[:, :, 0], w_[:, :, 1]

            g3 = gain.rearrange("p (h d) -> p h d", h=10)
            hr = rms_rope(q4, t4, 2, 10, g3, hL, tb[:, 0], tb[:, 1], pairs, hq, 2)
            hk = V.cp(TM[:, 0:512].rearrange("p (t g r d) -> p t g r d", t=2, g=2, r=2),
                      bc(q4[:, :, 8:10, :], 3, 2), start)
            zs = small[:, 100:124].rearrange("p (t c) -> p t c", t=2)
            zm = small[:, 124:128].rearrange("p (t c) -> p t c", t=2)
            for t in range(2):
                V.bns(zs[:, t, 0:6], Zv[:, t, 512:1024], hz)
                V.bna(zm[:, t, :], zs[:, t, 0:6])
            rz = small[:, 128:130]
            h = A.act(rz, zm[:, :, 1], ACT.Sqrt, V.last, h_one, bias=eps5[:, 0:1])
            V.rcp(rz, rz, h)
            for t in range(2):
                V.ts(Zv[:, t, 512:1024], Zv[:, t, 512:1024], zm[:, t, 0:1], rz[:, t:t + 1], ALU.subtract, ALU.mult)
            V.tt(Zv[:, :, 512:1024], Zv[:, :, 512:1024], bc(sg, 1, 2), ALU.mult, hL)
            hvn = V.tt(Zv[:, :, 512:1024], Zv[:, :, 512:1024], bc(sbv, 1, 2), ALU.add, hL)
            for i in range(7, 15):
                p = load(D["w_in"][l, i])
                w = p.ap.rearrange("p (k c) -> p k c", k=8)
                for c in range(2):
                    b = bank()
                    m = T.group(b.t[:, 0:256], [(w[:, k, c * 128:c * 128 + 128], hv[:, k, :]) for k in range(8)],
                                p.h, b.free)
                    b.free = [A.act(GSv[:, 2 * (i - 7) + c, :], b.t[:, 0:256], ACT.Sigmoid, m, start)]
                    hg += b.free
                p.rel = m
            hqT = []
            qv = qT.rearrange("p (a t) -> p a t", a=4)
            kv = kT.rearrange("p (a t) -> p a t", a=2)
            for a in range(3):
                b = bank()
                m = None
                for s in range(2):
                    for t in range(2):
                        if a < 2:
                            src = q4[:, t, 4 * a + 2 * s:4 * a + 2 * s + 2, :]
                        else:
                            src = TM[:, t * 256 + s * 128:t * 256 + s * 128 + 128]
                        m = T.tr(b.t[:, s * 256 + t * 128:s * 256 + t * 128 + 128],
                                 src if a == 2 else src.rearrange("p h d -> p (h d)"), ident[:, :],
                                 b.free, hr, hk)
                dst = qT[:, a * 512:a * 512 + 512] if a < 2 else kT[:, 0:512]
                b.free = [va().cp(dst, b.t[:, 0:512], m, start)]
                hqT += b.free
            ho = attend(8, 2, lambda h_, t: qv[64 * (h_ % 2):64 * (h_ % 2) + 64, h_ // 2, t * 128:t * 128 + 128],
                        lambda h_: [(kv[64 * (h_ % 2):64 * (h_ % 2) + 64, h_ // 4, :], 0)],
                        lambda h_, c: PQv[:, c, 640 + 64 * (h_ // 4):704 + 64 * (h_ // 4)],
                        256, None, None, PP, PT, oaT.rearrange("p (a t) -> p a t", a=4), 0, hqT, start)
            wsv = ws.rearrange("p (g i) -> p g i", g=8)
            b = [bank(), bank()]
            m = None
            for g in range(8):
                bb = b[g // 4]
                o = (g % 4) * 128
                m = T.mm(bb.t[:, o:o + 128].rearrange("p (t d) -> p t d", t=2), wsv[:, g, :],
                         Zv[:, :, 512 + g * 64:576 + g * 64], True, True, bb.free, hvn, hL)
                if g % 4 == 3:
                    gg = g // 4
                    bs = vec(f"b_sp{l}")[:, 4 * gg:4 * gg + 4]
                    tmp = TM[:, 512 + gg * 512:1024 + gg * 512].rearrange("p (t g d) -> p t g d", t=2, g=4)
                    V.tt(tmp, bb.t[:, 0:512].rearrange("p (g t d) -> p t g d", g=4, t=2),
                         bc(bc(bs, 1, 2), 3, 64), ALU.add, m, start)
                    bb.free = [V.last]
                    uz = Zv[:, :, gg * 256:gg * 256 + 256].rearrange("p t (g d) -> p t g d", g=4)
                    V.tt(uz, uz, tmp, ALU.mult)
            hub = V.last
            obv = obT.rearrange("p (c t) -> p c t", c=4)
            hob = []
            for a in range(2):
                b = bank()
                for s in range(2):
                    for t in range(2):
                        m = T.tr(b.t[:, s * 256 + t * 128:s * 256 + t * 128 + 128],
                                 Zv[:, t, (2 * a + s) * 128:(2 * a + s) * 128 + 128], ident[:, :], b.free, hub)
                b.free = [va().cp(obT[:, a * 512:a * 512 + 512], b.t[:, 0:512], m, start)]
                hob += b.free
            yv = yT.rearrange("p (c t) -> p c t", c=8)
            oav = oaT.rearrange("p (a t) -> p a t", a=4)
            hy = []
            for hf in range(2):
                pa = load(D["w_ba"][l, hf])
                pb = load(D["w_bb"][l, hf])
                wa = pa.ap.rearrange("p (c n) -> p c n", c=4)
                wb = pb.ap.rearrange("p (c n) -> p c n", c=4)
                for c in range(4):
                    mt = hf * 4 + c
                    b = bank()
                    T.group(b.t[:, 0:256], [(wa[:, k, c * 128:c * 128 + 128], oav[:, k, :]) for k in range(4)],
                            pa.h, b.free, ho)
                    m = T.group(b.t[:, 256:512], [(wb[:, k, c * 128:c * 128 + 128], obv[:, k, :]) for k in range(4)],
                                pb.h, hob)
                    V.tt(yv[:, mt, :], GSv[:, mt, :], b.t[:, 0:256], ALU.mult, m, hg, start)
                    V.tt(GSv[:, 8 + mt, :], GSv[:, 8 + mt, :], b.t[:, 256:512], ALU.mult, hg)
                    b.free = [V.last]
                    V.tt(yv[:, mt, :], yv[:, mt, :], GSv[:, 8 + mt, :], ALU.add)
                pa.rel = pb.rel = m
            hy = V.last
            hgt = modulation(0, l, 2)
            Tm = Z
            Tv = Zv
            for i in range(4):
                p = load(D["w_out"][l, i])
                w = p.ap.rearrange("p (k c) -> p k c", k=8)
                for t in range(2):
                    b = bank()
                    m = T.group(b.t[:, 0:256], [(yv[:, k, t * 128:t * 128 + 128], w[:, k, :]) for k in range(8)],
                                p.h, b.free, hy)
                    V.tt(Tv[:, t, i * 256:i * 256 + 256], b.t[:, 0:256], gate[0][:, i * 256:i * 256 + 256], ALU.mult, m, hob, hgt)
                    b.free = [V.last]
                p.rel = m
            V.stt(Tm, XS[:, :], ALPHA, Tm, ALU.mult, ALU.add)
            return ln_tok(Tm, lg, lb, hL, XS[:, :], hh)

        def attend(nh, nt, qf, kf, vf, nk, mask, sinks, PP, PT, oT, ocol, ready, start):
            nc_ = nk // 128
            done = []
            pfree = [None] * 8
            tfree = [None] * 2
            n = 0
            prev = None
            pv_open = {}
            st = small[:, 200:264]

            def scores(h_, t):
                nonlocal n
                i = n % 8
                n += 1
                b = bank()
                m = None
                for kk, off in kf(h_):
                    w_ = kk.shape[1]
                    m = T.mm(b.t[:, off:off + w_], qf(h_, t), kk, True, True, ready, b.free)
                P = PP[:, i * nk:i * nk + nk]
                s4 = st[:, i * 8:i * 8 + 8]
                waits = [m, pfree[i], start]
                if mask is None:
                    hm = V.red(s4[:, 0:1], b.t[:, 0:nk], ALU.max, waits)
                    src = b.t[:, 0:nk]
                else:
                    V.stt(P[:, 0:256], b.t[:, 0:256], 0.125, mask[:, t], ALU.mult, ALU.add, waits)
                    V.ts(P[:, 256:512], b.t[:, 256:512], 0.125, None, ALU.mult, None)
                    b.free = [V.last]
                    hm = V.red(s4[:, 0:1], P, ALU.max)
                    src = P
                sc = 0.125 if mask is None else 1.0
                if sinks is not None:
                    V.stt(s4[:, 1:2], s4[:, 0:1], sc, sinks[:, h_:h_ + 1], ALU.mult, ALU.max)
                    V.ts(s4[:, 1:2], s4[:, 1:2], -1.0, None, ALU.mult, None)
                else:
                    V.ts(s4[:, 1:2], s4[:, 0:1], -sc, None, ALU.mult, None)
                he = A.act(P, src, ACT.Exp, V.last, bias=s4[:, 1:2], scale=sc, accum=s4[:, 2:3])
                if mask is None:
                    b.free = [he]
                hk = A.act(s4[:, 3:4], sinks[:, h_:h_ + 1], ACT.Exp, bias=s4[:, 1:2]) if sinks is not None else None
                return P, i, s4, he, hk

            def normalise(P, i, s4, he, hk):
                if hk is not None:
                    he = hk
                    V.tt(s4[:, 2:3], s4[:, 2:3], s4[:, 3:4], ALU.add, he)
                V.rcp(s4[:, 2:3], s4[:, 2:3], he)
                hp = V.ts(P, P, s4[:, 2:3], None, ALU.mult, None)
                return P, i, hp

            def finish(h_, parts_):
                for g in range(nc_ // 2):
                    ti = (h_ * (nc_ // 2) + g) % 2
                    b = bank()
                    m = None
                    if g == 0 and h_ % 2 == 0:
                        pv_open["b"] = banks[6 + h_ // 2 % 2]
                    ob = pv_open["b"]
                    for c in range(2):
                        for t, (P, i, hp) in enumerate(parts_):
                            o = c * nt * 128 + t * 128
                            m = T.tr(b.t[:, o:o + 128], P[:, (2 * g + c) * 128:(2 * g + c) * 128 + 128], ident[:, :],
                                     hp, b.free)
                    if g == nc_ // 2 - 1:
                        for P, i, hp in parts_:
                            pfree[i] = m
                    dst = PT[:, ti * 512:ti * 512 + 512]
                    he = va().cp(dst, b.t[:, 0:512], m, tfree[ti], start)
                    b.free = [he]
                    late.append((h_, g, ti, dst, he, ob))
                    if len(late) > 1:
                        values(*late.pop(0))

            def values(h_, g, ti, dst, he, ob):
                for c in range(2):
                    first_, last_ = g == 0 and c == 0, g == nc_ // 2 - 1 and c == 1
                    m = T.mm(ob.t[64 * (h_ % 2):64 * (h_ % 2) + 64, 0:nt * 128], vf(h_, 2 * g + c),
                             dst[:, c * nt * 128:c * nt * 128 + nt * 128], first_, last_, he, ob.free)
                tfree[ti] = m
                if h_ % 2 == 1 and g == nc_ // 2 - 1:
                    ob.free = [va().cp(oT[:, h_ // 2, ocol:ocol + nt * 128], ob.t[:, 0:nt * 128], m, start)]
                    done.append(ob.free[0])

            pend, late, open_ = [], [], None
            rotating[0] = banks[0:6]
            for h_ in range(nh):
                cur = [scores(h_, t) for t in range(nt)]
                if open_ is not None:
                    pend.append((h_ - 1, [normalise(*p_) for p_ in open_]))
                open_ = cur
                pump()
                if nh == 8:
                    pump()
                if len(pend) > 1:
                    finish(*pend.pop(0))
            pend.append((nh - 1, [normalise(*p_) for p_ in open_]))
            for p_ in pend:
                finish(*p_)
            for p_ in late:
                values(*p_)
            rotating[0] = banks
            return done

        def moe(l, x_ready):
            a0 = [NROUND]

            def take(n):
                v = arena[:, a0[0]:a0[0] + n]
                a0[0] += n
                assert a0[0] <= ARENA - NEXTRA * 2048, a0
                return v

            start = everyone() + [x_ready]
            extra_after[0] = start
            big_ring[0] = True
            hT, lg, lb = take(2048), take(1024), take(1024)
            XE = [take(2048) for _ in range(2)]
            HA, HX = take(1024), take(1024)
            XH, XL, YH, YL, ST = (rounded[:, i:j] for i, j in
                                  ((0, 2048), (2048, 4096), (4096, 5120), (5120, 6144), (6144, 6400)))
            SelA, SelW = [rounded[:, 6400 + i * 512:6912 + i * 512] for i in range(2)], [take(512) for _ in range(2)]
            HP, HTT = HX[:, 0:256], HX[:, 256:512]
            Gt = take(130)
            sc, sl, mk = take(128), take(128), take(128)
            gt, gm, gs = take(256), take(16), take(128)
            sid = take(128)
            hL = fetch("mo", lg, D["ln2_g"][l].partition_broadcast(128), start)
            hL = fetch("mo", lb, D["ln2_b"][l].partition_broadcast(128), start)
            hR = h_router[l]
            hh = transposed(hT, l, 1, start + modulation(0, l, 3, 4))
            hv = hT.rearrange("p (k t) -> p k t", k=8)
            rv = rw.rearrange("p (k e) -> p k e", k=8)
            work, acc = banks[0:4], banks[4:8]
            def ff_dense(j, pw, after):
                return multiply(j, *ff_products(j, pw, after))

            def ff_products(j, pw, after):
                wg, wu = (p_.ap.rearrange("p (k f) -> p k f", k=8) for p_ in pw[:2])
                b = work[j]
                T.group(b.t[:, 0:256], [(wg[:, k, j * 128:j * 128 + 128], hv[:, k, :]) for k in range(8)],
                        pw[0].h, b.free, hh)
                m = T.group(b.t[:, 256:512], [(wu[:, k, j * 128:j * 128 + 128], hv[:, k, :]) for k in range(8)],
                            pw[1].h)
                return b, A.act(HA[:, j * 256:j * 256 + 256], b.t[:, 0:256], ACT.Silu, m, after), after

            def multiply(j, b, h1, after):
                h2 = V.tt(HX[:, j * 256:j * 256 + 256], HA[:, j * 256:j * 256 + 256], b.t[:, 256:512], ALU.mult,
                          h1, after)
                b.free = [h2]
                return h2

            b = acc[0]
            for t in range(2):
                m = T.group(b.t[:, t * 64:t * 64 + 64], [(hv[:, k, t * 128:t * 128 + 128], rv[:, k, :]) for k in range(8)],
                            b.free, hh, hR)
            b.free = [A.act(sc, b.t[:, 0:128], ACT.Sigmoid, m, start)]
            pw = [load(D["ws_gate"][l]), load(D["ws_up"][l]), load(D["ws_down"][l], 2)]
            shared = [ff_products(j, pw, start) for j in range(2)]
            V.tt(sl.rearrange("p (t e) -> p t e", t=2), sc.rearrange("p (t e) -> p t e", t=2), bc(rb, 1, 2), ALU.add,
                 b.free, start, hR)
            for t in range(2):
                for g in range(8):
                    V.top8(gs[:, t * 64 + g * 8:t * 64 + g * 8 + 8], sl[:, t * 64 + g * 8:t * 64 + g * 8 + 8])
            gv = gs.rearrange("p (t g c) -> p t g c", t=2, g=8)
            V.tt(gm.rearrange("p (t g) -> p t g", t=2), gv[:, :, :, 0], gv[:, :, :, 1], ALU.add)
            for t in range(2):
                me = gm[:, t * 8:t * 8 + 8]
                g1 = gt[:, 0:64].rearrange("p (i j) -> p i j", i=8)
                g2 = gt[:, 64:128].rearrange("p (i j) -> p i j", i=8)
                oth, own = bc(me, 1, 8), bc(me, 2, 8)
                V.tt(g1, oth, own, ALU.is_gt)
                V.tt(g2, oth, own, ALU.is_equal)
                V.tt(g2, g2, ltri.rearrange("p (i j) -> p i j", i=8), ALU.mult)
                V.tt(g1, g1, g2, ALU.add)
                V.red(gt[:, 128:136], g1, ALU.add)
                V.ts(gt[:, 136:144], gt[:, 128:136], 3.5, None, ALU.is_lt, None)
                V.ts(gt[:, 144:152], gt[:, 136:144], -1.0, 3e38, ALU.add, ALU.mult)
                st = sl[:, t * 64:t * 64 + 64].rearrange("p (g c) -> p g c", g=8)
                mt = mk[:, t * 64:t * 64 + 64].rearrange("p (g c) -> p g c", g=8)
                V.tt(mt, st, bc(gt[:, 136:144], 2, 8), ALU.mult)
                V.tt(mt, mt, bc(gt[:, 144:152], 2, 8), ALU.add)
                V.top8(gt[:, 160:168], mk[:, t * 64:t * 64 + 64])
                V.drop8(gs[:, t * 64:t * 64 + 64], gt[:, 160:168], mk[:, t * 64:t * 64 + 64], -3.3e38)
                V.tt(mk[:, t * 64:t * 64 + 64], mk[:, t * 64:t * 64 + 64], gs[:, t * 64:t * 64 + 64], ALU.not_equal)
                V.tt(sc[:, t * 64:t * 64 + 64], sc[:, t * 64:t * 64 + 64], mk[:, t * 64:t * 64 + 64], ALU.mult)
                V.red(gt[:, 170:171], sc[:, t * 64:t * 64 + 64], ALU.add)
                V.rcp(gt[:, 171:172], gt[:, 170:171])
                V.ts(Gt[:, t * 65:t * 65 + 64], sc[:, t * 64:t * 64 + 64], gt[:, 171:172], 2.5, ALU.mult, ALU.mult)
            hmk = V.last
            hx = [multiply(j, *shared[j]) for j in range(2)]
            b = work[2]
            T.mm(b.t[:, 0:64], tri[:, 0:128], mk[:, 0:64], True, True, hmk, b.free, h_tri)
            T.mm(b.t[:, 64:128], tri[:, 0:128], mk[:, 64:128], True, False)
            T.mm(b.t[:, 64:128], ones[:, :], mk[:, 0:64], False, True)
            T.mm(b.t[:, 128:192], ones[:, :], mk[:, 0:64], True, False)
            m = T.mm(b.t[:, 128:192], ones[:, :], mk[:, 64:128], False, True)
            V.tt(sid, b.t[:, 0:128], mk, ALU.mult, m)
            cnt = b.t[:, 128:192].rearrange("p (a e) -> p a e", e=2)
            V.red(gt[:, 0:32], cnt, ALU.max)
            b.free = [V.last]
            V.ts(sid, sid, -1.0, None, ALU.add, None)
            V.ts(gt[:, 32:64], gt[:, 0:32], 64.5, None, ALU.is_gt, None)
            h_flag = V.cp(flags[:, l * 32:l * 32 + 32], gt[:, 32:64])
            sv = sid.rearrange("p (t e) -> p t e", t=2)
            gtv = Gt.rearrange("p (t e) -> p t e", t=2)
            iota = tri[:, 128:192]
            V.cp(XH, XS[:, :], start)
            hxs = V.tt(XL, XS[:, :], f32(XH), ALU.subtract)
            rotating[0] = work[2:4]
            for bb in acc:
                T.add(lambda: None, [bb.free])
                bb.free = []
            ne = opts.get("experts", 64)

            def down_dense(pw, hx, first, last):
                wd = pw[2].ap.rearrange("p (j d) -> p j d", j=2)
                m = None
                for t in range(2):
                    for nh in range(2):
                        for j in range(2):
                            m = T.mm(acc[t * 2 + nh].t[:, :], HX[:, j * 256 + t * 128:j * 256 + t * 128 + 128],
                                     wd[:, j, nh * 512:nh * 512 + 512], first and j == 0, last and j == 1, hx, pw[2].h)
                return m

            def choose(Q, joins):
                q2 = Q % 2
                for t in range(2):
                    sa = SelA[q2][:, t * 256:t * 256 + 256].rearrange("p (e s) -> p e s", e=4)
                    sw = SelW[q2][:, t * 256:t * 256 + 256].rearrange("p (e s) -> p e s", e=4)
                    V.tt(sa, bc(iota, 1, 4), bc(sv[:, t, 4 * Q:4 * Q + 4], 2, 64), ALU.is_equal, joins, start)
                    V.tt(sw, f32(sa), bc(gtv[:, t, 4 * Q:4 * Q + 4], 2, 64), ALU.mult)
                return V.last

            def gather(Q, k, b, h_sel):
                q2 = Q % 2
                o = l * 32 + 16
                at = b.t[:, k % 2 * 256:k % 2 * 256 + 256]
                m = T.group(at, [(x_.rearrange("p (t d k) -> p t k d", t=2, k=8)[:, t, k, :],
                                  SelA[q2][:, t * 256:t * 256 + 256]) for x_ in (XH, XL) for t in range(2)],
                            h_sel, hxs, b.free)
                b.free = [(V if k % 2 else A).fma(XE[q2][:, k * 256:k * 256 + 256], at,
                                                  mod1[:, o + 8 + k:o + 9 + k], mod1[:, o + k:o + k + 1], m)]
                return b.free

            def pair(Q, pp, pa, pb, hxe, last, hsel):
                q2 = Q % 2
                xe = XE[q2].rearrange("p (k s) -> p k s", k=8)
                pws = (pa, pb)

                def sparse():
                    b1 = work[1]
                    for t in range(2):
                        m = T.tr(b1.t[:, t * 128:t * 128 + 128], SelW[q2][:, t * 256 + pp * 128:t * 256 + pp * 128 + 128],
                                 ident[:, :], b1.free)
                    ws = gt[:, 200:201]
                    V.red(ws, b1.t[:, 0:256], ALU.add, m)
                    hst = V.ts(ST, b1.t[:, 0:256], 0.0, None, ALU.not_equal, None)
                    b1.free = [hst]
                    b = work[0]
                    for i_, off in ((0, 0), (1, 256)):
                        for k in range(8):
                            for ab in range(2):
                                w = pws[ab][i_]
                                m = T.mm(b.t[64 * ab:64 * ab + 64, off:off + 256],
                                         xe[:, k, pp * 128 + 64 * ab:pp * 128 + 64 * ab + 64],
                                         w.ap.rearrange("p (k f) -> p k f", k=8)[:, k, :], k == 0, k == 7,
                                         w.h, b.free, hxe)
                    h1 = A.act(HA[:, 0:256], b.t[:, 0:256], ACT.Silu, m)
                    h2 = V.tt(HP, HA[:, 0:256], b.t[:, 256:512], ALU.mult, h1)
                    if hsel is not None:
                        gather(Q + 1, 4 * pp, work[2], hsel)
                        gather(Q + 1, 4 * pp + 1, work[3], hsel)
                    for j in range(2):
                        m = T.tr(b.t[:, j * 128:j * 128 + 128], HP[:, j * 128:j * 128 + 128], ident[:, :], h2)
                    hht = V.cp(HTT, b.t[:, 0:256], m)
                    if hsel is not None:
                        gather(Q + 1, 4 * pp + 2, b1, hsel)
                    hy = []
                    for nh in range(2):
                        bb = work[2 + nh]
                        for j in range(2):
                            for ab in range(2):
                                w = pws[ab][2]
                                m = T.mm(bb.t[64 * ab:64 * ab + 64, :], HTT[:, j * 128 + 64 * ab:j * 128 + 64 * ab + 64],
                                         w.ap.rearrange("p (j d) -> p j d", j=2)[:, j, nh * 512:nh * 512 + 512],
                                         j == 0, j == 1, w.h, bb.free, hht)
                        y = slice(nh * 512, nh * 512 + 512)
                        h1 = A.act(YH[:, y], bb.t[:, :], ACT.Copy, m, hst, scale=ws)
                        hy.append(V.stt(YL[:, y], bb.t[:, :], ws, f32(YH[:, y]), ALU.mult, ALU.subtract, h1))
                    for nh in range(2):
                        if nh == 1 and hsel is not None:
                            gather(Q + 1, 4 * pp + 3, b1, hsel)
                        for t in range(2):
                            for y_ in (YH, YL):
                                T.mm(acc[t * 2 + nh].t[:, :], ST[:, t * 128:t * 128 + 128],
                                     y_[:, nh * 512:nh * 512 + 512], False, last and y_ is YL, hst, hy[nh])

                def dense():
                    if hsel is not None:
                        for k in range(4):
                            gather(Q + 1, 4 * pp + k, work[k], hsel)
                    for ab in range(2):
                        pw = pws[ab]
                        e = 4 * Q + 2 * pp + ab
                        prevm = T.last
                        hx = [ff_dense(j, pw, prevm) for j in range(2)]
                        b = work[2]
                        m = None
                        for t in range(2):
                            g1 = Gt[:, t * 65 + e:t * 65 + e + 1]
                            wide = bass.AP(g1.tensor, g1.offset, [list(g1.ap[0]), [0, 128]])
                            m = T.mm(b.t[:, t * 128:t * 128 + 128], wide, ident[:, :], True, True, b.free)
                        for j in range(2):
                            h = V.tt(HX[:, j * 256:j * 256 + 256], HX[:, j * 256:j * 256 + 256], b.t[:, 0:256], ALU.mult,
                                     m, hx)
                        b.free = [h]
                        down_dense(pw, h, False, last and ab == 1)

                joins = fork(flags[0:1, l * 32 + 2 * Q + pp:l * 32 + 2 * Q + pp + 1], [h_flag], sparse, dense)
                for pw in pws:
                    for p_ in pw:
                        p_.rel = joins[0]
                for bb in work:
                    bb.free = joins
                return joins

            m = down_dense(pw, hx, True, False)
            for p_ in pw:
                p_.rel = m
            nq = ne // 4
            joins = everyone()
            hsel = choose(0, joins)
            hxe = [gather(0, k, work[k % 4], hsel) for k in range(8)]
            for Q in range(nq):
                hsel = choose(Q + 1, joins) if Q + 1 < nq else None
                for pp in range(2):
                    e = 4 * Q + 2 * pp
                    pa, pb = [None] * 3, [None] * 3
                    for i_, nm in enumerate(("w_gate", "w_up", "w_down")):
                        for ab, pw in ((0, pa), (1, pb)):
                            pw[i_] = load(D[nm][l, e + ab], 2 if i_ == 2 else None)
                    joins = pair(Q, pp, pa, pb, hxe, Q == nq - 1 and pp == 1, hsel)
                    i_ = 2 * Q + pp
                    for _ in range((i_ + 1) * NPUMP[l] // 32 - i_ * NPUMP[l] // 32):
                        pump()
                hxe = joins
            hgt = modulation(0, l, 5)
            rotating[0] = banks
            big_ring[0] = False
            av = hT.rearrange("p (t n) -> p t n", t=2)
            for t in range(2):
                for nh in range(2):
                    bb = acc[t * 2 + nh]
                    V.tt(av[:, t, nh * 512:nh * 512 + 512], bb.t[:, :], gate[1][:, nh * 512:nh * 512 + 512], ALU.mult, joins, hgt)
                    bb.free = [V.last]
            V.stt(hT, XS[:, :], ALPHA, hT, ALU.mult, ALU.add)
            return ln_tok(hT, lg, lb, hL, XS[:, :], hh)

        def block2(x_ready):
            XC = gates
            X = [XS[:, :].rearrange("p (k t) -> p k t", k=8), XC[:, :].rearrange("p (k t) -> p k t", k=8)]
            mv2 = mod2[:, :].rearrange("p (l v k s) -> p l v k s", l=2, v=6, k=8)

            class Arena:
                def __init__(self):
                    self.o = 0

                def take(self, n):
                    v = arena[:, self.o:self.o + n]
                    self.o += n
                    assert self.o <= ARENA, self.o
                    return v

            def norm_t(l, which, Xs, dst_of, sq, R, AB, after):
                outs = []
                h_ada = modulation(1, l, 3 * which, 3 * which + 1, 3 * which + 2)
                gv = vec(f"n{which + 1}g{l}")
                for s, x in Xs:
                    ab = AB[:, s * 8:s * 8 + 8]
                    V.stt(ab, mv2[:, l, 3 * which + 1, :, s], 1.0, gv, ALU.add, ALU.mult, after, h_ada)
                    hs = A.act(sq, x, ACT.Square, after, outs)
                    b = bank()
                    m = T.group(b.t[:, 0:256], [(ones[:, :], sq[:, k, :]) for k in range(8)], hs, b.free, h_one)
                    h = A.act(R, b.t[:, 0:256], ACT.Sqrt, m, after, bias=eps6[:, 0:1], scale=1.0 / 1024)
                    b.free = [h]
                    V.rcp(R, R, h)
                    V.tt(sq, x, bc(R, 1, 8), ALU.mult, m)
                    hx_ = V.last
                    fr = []
                    for k in range(8):
                        e = A if k % 2 else V
                        fr.append(e.fma(dst_of(s, k), sq[:, k, :], ab[:, k:k + 1], mv2[:, l, 3 * which, k, s:s + 1],
                                        hx_, after))
                    outs += fr
                return outs

            def add_gated(l, which, mt, b, m, nseg, after=()):
                for s in range(nseg):
                    x = X[s][:, mt, :]
                    V.stt(x, b.t[:, s * 256:s * 256 + 256], mv2[:, l, 3 * which + 2, mt, s:s + 1], x, ALU.mult, ALU.add,
                          m, after)
                b.free = [V.last]

            def mlp(l, nseg, hx_):
                ar = Arena()
                start = everyone() + [hx_]
                W = nseg * 256
                hT = ar.take(8 * W).rearrange("p (k t) -> p k t", k=8)
                h1 = ar.take(32 * W).rearrange("p (k t) -> p k t", k=32)
                sq = ar.take(2048).rearrange("p (k t) -> p k t", k=8)
                R, AB = ar.take(256), ar.take(16)
                hh = norm_t(l, 1, [(s, X[s]) for s in range(nseg)],
                            lambda s, k: hT[:, k, s * 256:s * 256 + 256], sq, R, AB, start)
                hs = []
                for i in range(16):
                    p = load(D["mlp1"][l, i])
                    w = p.ap.rearrange("p (k c) -> p k c", k=8)
                    for c in range(2):
                        b = bank()
                        m = T.group(b.t[:, 0:W], [(w[:, k, c * 128:c * 128 + 128], hT[:, k, :]) for k in range(8)],
                                    p.h, b.free, hh)
                        dst = h1[:, 2 * i + c, :]
                        ha = A.act(dst, b.t[:, 0:W], ACT.Relu, m, start)
                        b.free = [ha]
                        hs.append(V.tt(dst, dst, dst, ALU.mult, ha))
                    p.rel = m
                for mt in range(8):
                    b = bank()
                    for hf in range(2):
                        p = load(D["mlp2"][l, mt, hf])
                        w = p.ap.rearrange("p (k c) -> p k c", k=16)
                        m = None
                        for k in range(16):
                            kk = hf * 16 + k
                            m = T.mm(b.t[:, 0:W], w[:, k, :], h1[:, kk, :], kk == 0, kk == 31, p.h, b.free, hs[kk])
                        p.rel = m
                    add_gated(l, 1, mt, b, m, nseg)
                return V.last

            ar = Arena()
            start = everyone() + [x_ready]
            tmp = ar.take(2048)
            ctx_t = ar.take(2048)
            hc = fetch("cx", ctx_t.rearrange("p (t n) -> p t n", t=2), D["ctx"].rearrange("(t p) n -> p t n", p=128), start)
            xs_done = []
            for src, dst, hw in ((ctx_t, XC[:, :], hc), (XS[:, :], tmp, start)):
                sv = src.rearrange("p (t n) -> p t n", t=2)
                for k2 in range(4):
                    b = bank()
                    m = None
                    for kk in range(2):
                        for t in range(2):
                            k = 2 * k2 + kk
                            m = T.tr(b.t[:, kk * 256 + t * 128:kk * 256 + t * 128 + 128], sv[:, t, k * 128:k * 128 + 128],
                                     ident[:, :], hw, b.free, start, h_id)
                    b.free = [va().cp(dst[:, k2 * 512:k2 * 512 + 512], b.t[:, :], m, start)]
                    xs_done += b.free
            hx_ = V.cp(XS[:, :], tmp, xs_done)
            ar = Arena()
            start = everyone()
            hT = ar.take(4096)
            PQ = ar.take(6144)
            tm_ = ar.take(5120)
            qT, kT = ar.take(4096), ar.take(2048)
            PP, PT = ar.take(4096), ar.take(1024)
            oT = ar.take(4096)
            gain, tabs, mask, sk = ar.take(1280), ar.take(256), ar.take(512), ar.take(16)
            R, AB = ar.take(256), ar.take(16)
            TM = ar.take(2048)
            hL = fetch("at", gain, D["gain2"].partition_broadcast(128), start)
            hL = fetch("at", tabs, D["rope2"], start)
            hL = fetch("at", mask, D["mask"], start)
            hL = fetch("at", sk, D["sink"].partition_broadcast(128), start)
            sq = TM.rearrange("p (k t) -> p k t", k=8)
            hv = hT.rearrange("p (k t) -> p k t", k=8)
            hh = norm_t(0, 0, [(0, X[0]), (1, X[1])], lambda s, k: hv[:, k, s * 256:s * 256 + 256], sq, R, AB,
                        [start, hx_])
            PQv = PQ.rearrange("p (t n) -> p t n", t=4)
            hq = []
            for i in range(6):
                p = load(D["wqkv"][i])
                w = p.ap.rearrange("p (k c) -> p k c", k=8)
                for t in range(4):
                    b = bank()
                    m = T.group(b.t[:, 0:256], [(hv[:, k, t * 128:t * 128 + 128], w[:, k, :]) for k in range(8)],
                                p.h, b.free, hh)
                    b.free = [va().cp(PQv[:, t, i * 256:i * 256 + 256], b.t[:, 0:256], m, start)]
                    hq += b.free
                p.rel = m
            q4 = PQv[:, :, 0:1280].rearrange("p t (h d) -> p t h d", h=20)
            t4 = tm_.rearrange("p (t h d) -> p t h d", t=4, h=20)
            tb = tabs.rearrange("p (c t d) -> p c t d", c=2, t=2)

            def halves(v):
                if len(v.shape) == 3:
                    w_ = v.rearrange("p h (g e j) -> p h g e j", g=2, e=2)
                    return w_[:, :, :, 0, :], w_[:, :, :, 1, :]
                w_ = v.rearrange("p (g e j) -> p g e j", g=2, e=2)
                return w_[:, :, 0, :], w_[:, :, 1, :]

            hr = rms_rope(q4, t4, 4, 20, gain.rearrange("p (h d) -> p h d", h=20), [hL, hq], tb[:, 0], tb[:, 1],
                          halves, hL, 2)
            for t in range(4):
                hk = V.cp(TM[:, t * 512:t * 512 + 512].rearrange("p (g r d) -> p g r d", g=4, r=2),
                          bc(q4[:, t, 16:20, :], 2, 2), hh)
            qv = qT.rearrange("p (a t) -> p a t", a=8)
            kv = kT.rearrange("p (a t) -> p a t", a=4)
            hqT = []
            for a in range(12):
                b = bank()
                m = None
                for t in range(4):
                    if a < 8:
                        src = q4[:, t, 2 * a:2 * a + 2, :].rearrange("p h d -> p (h d)")
                    else:
                        src = TM[:, t * 512 + (a - 8) * 128:t * 512 + (a - 8) * 128 + 128]
                    m = T.tr(b.t[:, t * 128:t * 128 + 128], src, ident[:, :], b.free, hr, hk)
                dst = qv[:, a, :] if a < 8 else kv[:, a - 8, :]
                b.free = [va().cp(dst, b.t[:, 0:512], m, start)]
                hqT += b.free
            ov = oT.rearrange("p (a t) -> p a t", a=8)
            mk = mask.rearrange("p (t n) -> p t n", t=2)
            ho = attend(16, 2, lambda h_, t: qv[64 * (h_ % 2):64 * (h_ % 2) + 64, h_ // 2, t * 128:t * 128 + 128],
                        lambda h_: [(kv[64 * (h_ % 2):64 * (h_ % 2) + 64, h_ // 4, :], 0)],
                        lambda h_, c: PQv[:, c, 1280 + 64 * (h_ // 4):1344 + 64 * (h_ // 4)],
                        512, mk, sk, PP, PT, ov, 0, [hqT, hL], start)
            ho2 = attend(16, 2, lambda h_, t: qv[64 * (h_ % 2):64 * (h_ % 2) + 64, h_ // 2, 256 + t * 128:384 + t * 128],
                         lambda h_: [(kv[64 * (h_ % 2):64 * (h_ % 2) + 64, h_ // 4, 256:512], 0)],
                         lambda h_, c: PQv[:, 2 + c, 1280 + 64 * (h_ // 4):1344 + 64 * (h_ // 4)],
                         256, None, sk, PP, PT, ov, 256, [hqT, ho], [start, everyone()])
            for i in range(4):
                p = load(D["w_o"][i])
                w = p.ap.rearrange("p (k c) -> p k c", k=8)
                for c in range(2):
                    b = bank()
                    m = T.group(b.t[:, :], [(w[:, k, c * 128:c * 128 + 128], ov[:, k, :]) for k in range(8)],
                                p.h, b.free, ho, ho2)
                    add_gated(0, 0, 2 * i + c, b, m, 2)
                p.rel = m
            hx_ = mlp(0, 2, V.last)
            if "b" in parts:
                hx_ = rwkv(hx_, X, mv2, norm_t, add_gated, Arena)
                hx_ = mlp(1, 1, hx_)
            ar = Arena()
            start = everyone() + [hx_]
            tmp = ar.take(2048).rearrange("p (t n) -> p t n", t=2)
            outs = []
            for k2 in range(4):
                b = bank()
                m = None
                for t in range(2):
                    for kk in range(2):
                        k = 2 * k2 + kk
                        m = T.tr(b.t[:, t * 256 + kk * 128:t * 256 + kk * 128 + 128], X[0][:, k, t * 128:t * 128 + 128],
                                 ident[:, :], start, b.free)
                b.free = [va().cp(tmp[:, :, k2 * 256:k2 * 256 + 256], b.t[:, :].rearrange("p (t c) -> p t c", t=2), m, start)]
                outs += b.free
            return V.cp(XS[:, :].rearrange("p (t n) -> p t n", t=2), tmp, outs)

        def rwkv(x_ready, X, mv2, norm_t, add_gated, Arena):
            ar = Arena()
            start = everyone() + [x_ready]
            v8 = lambda a: a.rearrange("p (k t) -> p k t", k=8)
            r, k_, kk, b_ = (v8(ar.take(2048)) for _ in range(4))
            sg = [v8(ar.take(2048)) for _ in range(2)]
            vT = v8(ar.take(2048))
            xg = X[1]
            Z = [ar.take(512).rearrange("p (a v) -> p a v", a=8) for _ in range(2)]
            cs = ar.take(672)
            bo = ar.take(128)
            kvec = ar.take(8)
            base = ar.o
            hL = fetch("rw", cs, D["scan_c"], start)
            hL = fetch("rw", bo, D["blockones"], start)
            V.ts(kvec, vec("k_a"), -1.0, 1.0, ALU.mult, ALU.add, start, h_vec)
            for d in range(2):
                V.ms(Z[d], 0.0, start)
            hz = V.last

            def features(s, after):
                ar.o = base
                W = 256
                hp = ar.take(8 * 258).rearrange("p (k t) -> p k t", k=8)
                xx, aT, mixa, mixb = (v8(ar.take(2048)) for _ in range(4))
                low = [ar.take(256) for _ in range(2)]
                R, AB = ar.take(256), ar.take(16)
                V.ms(hp[:, :, 0:1], 0.0, after)
                V.ms(hp[:, :, 257:258], 0.0)
                hh = norm_t(1, 0, [(s, X[s])], lambda s_, k: hp[:, k, 1:257], mixa, R, AB, after)
                V.tt(xx, hp[:, :, 0:256], hp[:, :, 2:258], ALU.add, hh)
                hxx = V.stt(xx, xx, 0.5, hp[:, :, 1:257], ALU.mult, ALU.subtract)
                bufs, bfree, nb = [mixa, mixb], [None, None], [0]

                def mix(m_, dst=None):
                    i = nb[0] % 2
                    if dst is None:
                        nb[0] += 1
                    o = dst if dst is not None else bufs[i]
                    mu = vec(f"mu{m_}")
                    h = [V.stt(o[:, k, :], xx[:, k, :], mu[:, k:k + 1], hp[:, k, 1:257], ALU.mult, ALU.add,
                               bfree[i] if dst is None else None, after) for k in range(8)]
                    return o, h, i

                def wide(src, h, i, w_, evac, qs=range(4)):
                    for q in qs:
                        p = load(w_[q])
                        w = p.ap.rearrange("p (k c) -> p k c", k=8)
                        b = bank()
                        m = None
                        for c in range(2):
                            m = T.group(b.t[:, c * 256:c * 256 + 256],
                                        [(w[:, k, c * 128:c * 128 + 128], src[:, k, :], h[k]) for k in range(8)],
                                        p.h, b.free)
                        p.rel = m
                        b.free = [evac(q, b.t[:, :].rearrange("p (c t) -> p c t", c=2), m)]
                    bfree[i] = m
                    return b.free[0]

                def lora(src, h, i, w1, n, func, dst, bias_of, w2, outs_, func2):
                    p = load(w1)
                    w = p.ap[:, 0:8 * n].rearrange("p (k c) -> p k c", k=8)
                    b = bank()
                    m = T.group(b.t[0:n, 0:256], [(w[:, k, :], src[:, k, :], h[k]) for k in range(8)], p.h, b.free)
                    p.rel = m
                    bfree[i] = m
                    ht = A.act(dst[0:n, :], b.t[0:n, 0:256], func, m, after)
                    b.free = [ht]
                    p = load(w2)
                    hs = []
                    for d, out_ in enumerate(outs_):
                        for q in range(4):
                            b = bank()
                            for c in range(2):
                                mt = 2 * q + c
                                m = T.mm(b.t[:, c * 256:c * 256 + 256], p.ap[64 * d:64 * d + 64, mt * 128:mt * 128 + 128],
                                         dst[64 * d:64 * d + 64, :], True, True, p.h, b.free, ht)
                            for c in range(2):
                                mt = 2 * q + c
                                hs.append(A.act(out_[:, mt, :], b.t[:, c * 256:c * 256 + 256], func2, m, after,
                                                bias=bias_of(d)[:, mt:mt + 1]))
                            b.free = [hs[-1]]
                    p.rel = m
                    return hs

                if s == 0:
                    o, h, i = mix(0)
                    wide(o, h, i, D["w_rkv"][0], lambda q, t, m: A.cp(r[:, 2 * q:2 * q + 2, :], t, m, after))
                o, h, i = mix(1)
                h_sg = lora(o, h, i, D["w1"], 128, ACT.Tanh, low[0], lambda d: vec(f"w0_{d}"), D["w2"], sg, ACT.Sigmoid)
                o, h, i = mix(2)
                h_k = wide(o, h, i, D["w_rkv"][1], lambda q, t, m: A.cp(k_[:, 2 * q:2 * q + 2, :], t, m, after))
                o, h, i = mix(3)
                o4, h4, i4 = mix(4)
                if s == 0:
                    mix(5, xg)
                for k in range(8):
                    V.ts(kk[:, k, :], k_[:, k, :], vec("k_k")[:, k:k + 1], None, ALU.mult, None, h_k, after)
                sq = xx
                hs = V.tt(sq, kk, kk, ALU.mult)

                def evac(q, t, m):
                    return A.cp(vT[:, 2 * q:2 * q + 2, :], t, m, after)

                wide(o, h, i, D["w_rkv"][2], evac, range(2))
                head_sums(sq, hs, lambda q, t, m: A.act(sq[:, 2 * q:2 * q + 2, :], t, ACT.Sqrt, m))
                V.ts(sq, sq, 1e-12, None, ALU.max, None, A.last)
                V.rcp(sq, sq)
                V.tt(kk, kk, sq, ALU.mult)
                wide(o, h, i, D["w_rkv"][2], evac, range(2, 4))
                h_a = lora(o4, h4, i4, D["a1"], 64, ACT.Copy, low[1], lambda d: vec("a0"), D["a2"], [aT], ACT.Sigmoid)
                V.tt(b_, kk, aT, ALU.mult, h_a, after)
                for k in range(8):
                    V.ts(aT[:, k, :], aT[:, k, :], vec("k_a")[:, k:k + 1], kvec[:, k:k + 1], ALU.mult, ALU.add)
                V.tt(k_, k_, aT, ALU.mult, h_k)
                return [V.last, A.last]

            def head_sums(src, h, evac):
                for q in range(4):
                    b = bank()
                    m = None
                    for c in range(2):
                        m = T.mm(b.t[:, c * 256:c * 256 + 256], bo, src[:, 2 * q + c, :], True, True, h, b.free, hL)
                    b.free = [evac(q, b.t[:, :].rearrange("p (c t) -> p c t", c=2), m)]

            def scan(s, d, ready, Y):
                after = ready
                C = v8(ar.take(512))
                BK, AR, GT = (ar.take(1024) for _ in range(3))
                E1, E2 = v8(ar.take(512)), v8(ar.take(512))
                U, L, Yi, YTi, T1, BL = (ar.take(256) for _ in range(6))
                BKt, VS = ar.take(512), ar.take(512)
                Ts, PC = ar.take(256), ar.take(16)
                c0 = d * 320
                mG, mU, mL, mU1 = (cs[:, c0 + o:c0 + o + n] for o, n in ((0, 64), (64, 32), (96, 32), (128, 32)))
                mBL = [cs[:, c0 + 160 + 32 * i:c0 + 192 + 32 * i] for i in range(5)]
                I32 = cs[:, 640:672]
                cc = C.rearrange("p k (c t) -> p k c t", c=2)
                Sc = sg[d].rearrange("p k (c t) -> p k c t", c=8)
                BKv = BK.rearrange("p (a c e t) -> p a c e t", a=8, c=2, e=2)
                ARv = AR.rearrange("p (a c e t) -> p a c e t", a=8, c=2, e=2)
                GTv = GT.rearrange("p (c a n) -> p c a n", c=2, a=8)
                E1v = E1.rearrange("p k (c t) -> p k c t", c=2)
                E2v = E2.rearrange("p k (c t) -> p k c t", c=2)
                bkt = BKt.rearrange("p (a v) -> p a v", a=8)
                vs_ = VS.rearrange("p (a v) -> p a v", a=8)
                vv = VS.rearrange("p (a e v) -> p a e v", a=4, e=2)
                pcv = PC.rearrange("p (a c) -> p a c", a=8)
                ne_ = 2 if s == 0 else 1
                h_z = hz
                mT, mA = [None], [None]

                def own():
                    return [mT[0], mA[0], after]

                def q2(x):
                    return x.rearrange("p (c g n) -> p c g n", c=2, g=4)

                def rep(x):
                    return bc(bc(x, 1, 4), 1, 2)

                def prods(b, lhs, rhs, *w):
                    m = None
                    for c in range(2):
                        for gf in range(4):
                            for g in range(4):
                                o, f = 32 * g, c * 128 + gf * 32
                                m = T.mm(b.t[o:o + 32, f:f + 32], lhs[o:o + 32, f:f + 32], rhs[o:o + 32, f:f + 32],
                                         True, True, w, b.free)
                    mT[0] = m
                    return m

                for bt in (range(4) if d == 0 else range(3, -1, -1)):
                    ss = Sc[:, :, 2 * bt:2 * bt + 2, :]

                    def seg_(x):
                        return x[:, :, bt * 64:bt * 64 + 64].rearrange("p k (c t) -> p k c t", c=2)

                    for k in range(8):
                        V.scan(C[:, k, :], scanm, sg[d][:, k, bt * 64:bt * 64 + 64], own(), h_scanm)
                    tot = cc[:, :, :, 31]
                    hs_ = V.last
                    A.act(pcv, tot, ACT.Exp, hs_, own(), scale=-EXPM05)
                    if d == 0:
                        V.tt(E2v, cc, ss, ALU.subtract)
                        incl = cc
                    else:
                        V.tt(E2v, bc(tot, 3, 32), cc, ALU.subtract)
                        V.tt(E1v, E2v, ss, ALU.add)
                        incl = E1v
                    hx3 = A.act(E2v, E2v, ACT.Exp, V.last, scale=-EXPM05)
                    V.stt(ARv[:, :, :, 0, :], seg_(kk), -1.0, E2v, ALU.mult, ALU.mult, hx3)
                    if s == 0:
                        ha = A.act(E2v, incl, ACT.Exp, V.last, scale=-EXPM05)
                        V.tt(ARv[:, :, :, 1, :], seg_(r), E2v, ALU.mult, ha)
                    ha = A.act(E2v, incl, ACT.Exp, V.last, scale=EXPM05)
                    V.tt(BKv[:, :, :, 0, :], seg_(b_), E2v, ALU.mult, ha)
                    hbk = V.tt(BKv[:, :, :, 1, :], seg_(k_), E2v, ALU.mult)
                    yield
                    for dst, mask_, up in ((U, mU, True), (L, mL, False)):
                        b = bank()
                        m = None
                        for c in range(2):
                            for h_ in range(16):
                                a, o, g = h_ // 2, 64 * (h_ % 2), 32 * (h_ % 4)
                                x_, y_ = BKv[o:o + 64, a, c, 0, :], ARv[o:o + 64, a, c, 0, :]
                                if not up:
                                    x_, y_ = y_, x_
                                f = c * 128 + (h_ // 4) * 32
                                m = T.mm(b.t[g:g + 32, f:f + 32], x_, y_, True, True, hbk, b.free)
                        b.free = [V.tt(q2(dst), b.t[:, 0:256].rearrange("p (c g n) -> p c g n", c=2, g=4), rep(mask_),
                                       ALU.mult, m, own(), hL)]
                    for c in range(2):
                        b = bank()
                        m = None
                        for h_ in range(16):
                            a, o = h_ // 2, 64 * (h_ % 2)
                            m = T.mm(b.t[o:o + 64, a * 32 * ne_:(a + 1) * 32 * ne_],
                                     BKv[o:o + 64, a, c, :, :].rearrange("p e t -> p (e t)"),
                                     ARv[o:o + 64, a, c, 0:ne_, :].rearrange("p e t -> p (e t)"), True, True,
                                     hbk, b.free)
                        b.free = [V.tt(GTv[:, c, :, 0:32 * ne_], b.t[:, 0:256 * ne_].rearrange("p (a n) -> p a n", a=8),
                                       bc(mG[:, 0:32 * ne_], 1, 8), ALU.mult, m, own(), hL)]
                    mT[0] = m
                    hG = V.last
                    V.tt(q2(Yi), q2(U), rep(mU1), ALU.mult)
                    V.tt(q2(Yi), q2(Yi), rep(I32), ALU.add)
                    V.tt(q2(YTi), q2(L), rep(mBL[0]), ALU.mult)
                    V.tt(q2(YTi), q2(YTi), rep(I32), ALU.add)
                    hB = V.tt(q2(BL), q2(L), rep(mBL[1]), ALU.mult)
                    hY = hB
                    yield
                    for lev in range(1, 5):
                        b = bank()
                        m = prods(b, BL, Yi, hB, hY)
                        h1 = mA[0] = A.cp(T1, b.t[:, 0:256], m)
                        b.free = [h1]
                        yield
                        if lev < 4:
                            hB = V.tt(q2(BL), q2(L), rep(mBL[lev + 1]), ALU.mult, m)
                        b = bank()
                        m = prods(b, YTi, T1, h1, hY)
                        if lev < 4:
                            b2 = bank()
                            m2 = prods(b2, T1, YTi, h1)
                            V.tt(Yi, Yi, b.t[:, 0:256], ALU.add, m)
                            b.free = [V.last]
                            V.tt(YTi, YTi, b2.t[:, 0:256], ALU.add, m2)
                            b2.free = [V.last]
                        else:
                            V.tt(Yi, Yi, b.t[:, 0:256], ALU.add, m)
                            b.free = [V.last]
                        hY = V.last
                        yield
                    for c in (range(2) if d == 0 else (1, 0)):
                        b = bank()
                        m = None
                        for h_ in range(16):
                            a, o = h_ // 2, 64 * (h_ % 2)
                            m = T.mm(b.t[o:o + 64, a * 64:a * 64 + 64],
                                     BKv[o:o + 64, a, c, :, :].rearrange("p e t -> p (e t)"),
                                     ident[o:o + 64, o:o + 64], True, True, hbk, b.free)
                        b.free = [V.cp(BKt, b.t[:, :], m, own())]
                        hb_ = [V.last]
                        b = bank()
                        t0 = bt * 64 + c * 32
                        for h_ in range(16):
                            a, o = h_ // 2, 64 * (h_ % 2)
                            m = T.mm(b.t[o + 32:o + 64, a * 64:a * 64 + 64], vT[o:o + 64, a, t0:t0 + 32],
                                     ident[o:o + 64, o:o + 64], True, True, ready, b.free)
                        e1 = V.cp(VS[32:64, :], b.t[32:64, :], m, own())
                        e2 = A.cp(VS[96:128, :], b.t[96:128, :], m, own())
                        b.free = [e1, e2]
                        hb_ += [e1, e2]
                        b = bank()
                        for h_ in range(16):
                            a, o, g = h_ // 2, 64 * (h_ % 2), 32 * (h_ % 4)
                            dst = b.t[g:g + 32, (h_ // 4) * 64:(h_ // 4) * 64 + 64]
                            T.mm(dst, ARv[o:o + 64, a, c, 0, :], Z[d][o:o + 64, a, :], True, False, h_z, b.free, hbk)
                            m = T.mm(dst, GTv[o + 32:o + 64, c, a, 0:32], vs_[o + 32:o + 64, a, :], False, True, hb_, hG)
                        hT_ = A.cp(Ts, b.t[:, 0:256], m, own())
                        b.free = [hT_]
                        yield
                        hs_ = []
                        for e in range(2):
                            b = bank()
                            for a2 in range(4):
                                for par in range(2):
                                    h_ = 4 * a2 + 2 * e + par
                                    o, g = 64 * par, 32 * (h_ % 4)
                                    f = c * 128 + a2 * 32
                                    m = T.mm(b.t[o:o + 32, a2 * 64:a2 * 64 + 64], Yi[g:g + 32, f:f + 32],
                                             Ts[g:g + 32, a2 * 64:a2 * 64 + 64], True, True, hT_, hY, b.free)
                            s1 = V.cp(vv[0:32, :, e, :], b.t[0:32, 0:256].rearrange("p (a v) -> p a v", a=4), m)
                            s2 = A.cp(vv[64:96, :, e, :], b.t[64:96, 0:256].rearrange("p (a v) -> p a v", a=4), m)
                            b.free = [s1, s2]
                            hs_ += b.free
                        mA[0] = s2
                        yield
                        b = bank()
                        for h_ in range(16):
                            a, o = h_ // 2, 64 * (h_ % 2)
                            m = T.mm(b.t[o:o + 64, a * 64:a * 64 + 64], bkt[o:o + 64, a, :], vs_[o:o + 64, a, :],
                                     True, True, b.free, hs_, hb_)
                        mz = m
                        bz = b
                        if s == 0:
                            b = bank()
                            for h_ in range(16):
                                a, o = h_ // 2, 64 * (h_ % 2)
                                dst = b.t[o:o + 64, a * 32:a * 32 + 32]
                                T.mm(dst, Z[d][o:o + 64, a, :], ARv[o:o + 64, a, c, 1, :], True, False, b.free, h_z)
                                m = T.mm(dst, vs_[o:o + 64, a, :], GTv[o:o + 64, c, a, 32:64], False, True, hs_, hG)
                            mA[0] = A.cp(Y[:, :, t0:t0 + 32], b.t[:, 0:256].rearrange("p (a t) -> p a t", a=8), m, ready)
                            b.free = [mA[0]]
                        mT[0] = m
                        V.tt(Z[d], Z[d], bz.t[:, :].rearrange("p (a v) -> p a v", a=8), ALU.add, mz, m)
                        bz.free = [V.last]
                        h_z = V.tt(Z[d], Z[d], bc(pcv[:, :, c], 2, 64), ALU.mult)
                        yield

            def both_ways(s, ready, Y):
                ar.o = base + (4096 if s == 0 else 0)
                ways = [scan(s, d, ready, Y[d]) for d in range(2)]
                while ways:
                    for w in list(ways):
                        try:
                            next(w)
                        except StopIteration:
                            ways.remove(w)

            scanm = ones_period
            fr = features(1, start)
            both_ways(1, [fr, everyone()], [None, None])
            fr = features(0, everyone())
            ar.o = base
            Ys = [v8(ar.take(2048)) for _ in range(2)]
            both_ways(0, [fr, everyone()], Ys)
            after = everyone()
            ar.o = base + 4096
            tq, Oh, bonus = (v8(ar.take(2048)) for _ in range(3))
            SG = [ar.take(256) for _ in range(2)]
            V.tt(bonus, r, k_, ALU.mult, after)
            for k in range(8):
                V.ts(bonus[:, k, :], bonus[:, k, :], vec("r_k")[:, k:k + 1], None, ALU.mult, None)
            head_sums(bonus, V.last, lambda q, t, m: V.tt(bonus[:, 2 * q:2 * q + 2, :],
                                                          vT[:, 2 * q:2 * q + 2, :], t, ALU.mult, m))
            hO = None
            for d in range(2):
                p1 = load(D["g1"][d])
                w = p1.ap[:, 0:1024].rearrange("p (k c) -> p k c", k=8)
                b = bank()
                m = T.group(b.t[:, 0:256], [(w[:, k, :], xg[:, k, :]) for k in range(8)], p1.h, b.free, after)
                p1.rel = m
                hs = A.act(SG[d], b.t[:, 0:256], ACT.Sigmoid, m, after)
                b.free = [hs]
                Yd = Ys[d]
                head_sums(Yd, after, lambda q, t, m: V.stt(Yd[:, 2 * q:2 * q + 2, :], t, -1.0 / 64, Yd[:, 2 * q:2 * q + 2, :],
                                                           ALU.mult, ALU.add, m))
                hq_ = A.act(tq, Yd, ACT.Square, V.last, hO)
                head_sums(tq, hq_, lambda q, t, m: A.act(tq[:, 2 * q:2 * q + 2, :], t, ACT.Sqrt, m, bias=epsg[:, 0:1],
                                                         scale=1.0 / 64))
                V.rcp(tq, tq, A.last)
                V.tt(Yd, Yd, tq, ALU.mult)
                for k in range(8):
                    V.ts(Yd[:, k, :], Yd[:, k, :], vec("gn_g")[:, k:k + 1], vec("gn_b")[:, k:k + 1], ALU.mult, ALU.add)
                V.tt(Yd, Yd, bonus, ALU.add)
                p2 = load(D["g2"][d])
                for q in range(4):
                    b = bank()
                    for c in range(2):
                        mt = 2 * q + c
                        m = T.mm(b.t[:, c * 256:c * 256 + 256], p2.ap[:, mt * 128:mt * 128 + 128], SG[d], True, True,
                                 p2.h, hs, b.free)
                    tv = b.t[:, :].rearrange("p (c t) -> p c t", c=2)
                    V.tt(Yd[:, 2 * q:2 * q + 2, :], Yd[:, 2 * q:2 * q + 2, :], tv, ALU.mult, m)
                    b.free = [V.last]
                p2.rel = m
                hO = V.last
            V.tt(Oh, Ys[0], Ys[1], ALU.add, after)
            hO = V.last
            for i in range(4):
                p = load(D["rw_o"][i])
                w = p.ap.rearrange("p (k c) -> p k c", k=8)
                for c in range(2):
                    b = bank()
                    m = T.group(b.t[:, 0:256], [(w[:, k, c * 128:c * 128 + 128], Oh[:, k, :]) for k in range(8)],
                                p.h, b.free, hO)
                    add_gated(1, 0, 2 * i + c, b, m, 1)
                p.rel = m
            return V.last

        ones_period = sb("ones_period", 64)[:, :]
        V.ms(ones_period, 1.0)
        h_scanm = V.ms(ones_period.rearrange("p (c t) -> p c t", c=2)[:, :, 0:1], 0.0)

        hx = fetch("x", XS[:, :].rearrange("p (t n) -> p t n", t=2),
                   (D["x0"] if "x0" in D else D["x"]).rearrange("(t p) n -> p t n", p=128))
        def pieces_of(blk, l, *vs_):
            if (blk == 0 and f"m{l}" in parts) or (blk == 1 and "a" in parts):
                waiting.extend(ada_piece(blk, l, v, q) for v in vs_ for q in range(4))

        pieces_of(0, 0, 0, 1, 2, 3, 4, 5)
        for l in range(2):
            if l == 0:
                pieces_of(0, 1, 0, 1, 2, 3, 4)
            else:
                pieces_of(0, 1, 5)
                pieces_of(1, 0, 0, 1, 2, 3, 4, 5)
                pieces_of(1, 1, 0, 1, 2, 3, 4, 5)
            if f"m{l}" in parts:
                hx = mixer(l, [hx])
            if f"e{l}" in parts:
                hx = moe(l, hx)
        if "a" in parts or "b" in parts:
            hx = block2(hx)
        s_out = sem("s_out")
        S.add(lambda: nc.sync.dma_start(out.rearrange("(t p) n -> p t n", p=128),
                                        XS[:, :].rearrange("p (t n) -> p t n", t=2)).then_inc(s_out, 16) and None, [hx])
        S.add(lambda: None, [Landed(s_out, 16)])
        for q in (T, A, V, G, S):
            q.number()
        block = ctx.enter_context(nc.Block())

        @block.sync
        def _(eng):
            S.play(eng)

        @block.tensor
        def _(eng):
            T.play(eng)

        @block.scalar
        def _(eng):
            A.play(eng)

        @block.vector
        def _(eng):
            V.play(eng)

        @block.gpsimd
        def _(eng):
            G.play(eng)


def cols_i(w, n=256):
    N = w.shape[1]
    return np.ascontiguousarray(w.reshape(128, 8, N // n, n).transpose(2, 0, 1, 3)).reshape(N // n, 128, 8 * n)


def cols_s(w, n=256):
    K, N = w.shape[0] // 128, w.shape[1]
    return np.ascontiguousarray(w.reshape(K, 128, N // n, n).transpose(2, 1, 0, 3)).reshape(N // n, 128, K * n)


def vi(v):
    return np.asarray(v).reshape(128, -1)


def vs(v):
    return np.ascontiguousarray(np.asarray(v).reshape(-1, 128).T)


def both(a, f):
    return np.stack([f(a[l]) for l in range(a.shape[0])])


def layout(I):
    I = {k: np.asarray(v) for k, v in I.items()}
    A = {}
    A["x"] = I["x"].reshape(256, 1024)
    A["cond"] = np.concatenate([vi(I["c"][0]), vi(I["c_2"][0]), vi(I["c_ctx_2"]), vi(I["c_ctx_2"])], 1)
    cols, off, n = [], {}, 0

    def put(name, a):
        nonlocal n
        a = np.asarray(a, dtype=a.dtype)
        cols.append(a)
        off[name] = n
        n += a.shape[1]

    for l in range(2):
        b = I["b_ada"][l].reshape(6, 1024)
        put(f"b_ada{l}", np.concatenate([vi(b[i]) for i in (0, 1, 3, 4)], 1))
        put(f"b_sp{l}", np.ascontiguousarray(I["b_spatial"][l].T))
    b2 = I["ada_b_2"]
    for l in range(2):
        put(f"b2_{l}", np.concatenate([vs(b2[l].reshape(6, 1024)[i]) for i in range(6)], 1))
        put(f"n1g{l}", vs(I["norm1_g_2"][l]))
        put(f"n2g{l}", vs(I["norm2_g_2"][l]))
    for m in range(6):
        put(f"mu{m}", vs(I["rwkv_mu_2"][0, m]))
    put("w0_0", vs(I["rwkv_w0_2"][0, 0]))
    put("w0_1", vs(I["rwkv_w0_2"][0, 1]))
    put("a0", vs(I["rwkv_a0_2"][0]))
    put("k_k", vs(I["rwkv_k_k_2"][0]))
    put("k_a", vs(I["rwkv_k_a_2"][0]))
    put("r_k", vs(I["rwkv_r_k_2"][0].reshape(-1)))
    put("gn_g", vs(I["rwkv_gn_g_2"][0]))
    put("gn_b", vs(I["rwkv_gn_b_2"][0]))
    A["vecs"] = np.concatenate(cols, 1)

    def ada_one(w):
        w = w.reshape(1024, 6, 128, 8)
        outs = []
        for i in range(6):
            wi = w[:, i]
            wi = wi.reshape(1024, 1024) if i in (2, 5) else wi.transpose(0, 2, 1).reshape(1024, 1024)
            outs.append(cols_i(wi))
        return np.concatenate(outs, 0)

    A["w_ada"] = both(I["w_ada"], ada_one)
    A["b_gate"] = np.stack([np.concatenate([I["b_ada"][l].reshape(6, 1024)[2], I["b_ada"][l].reshape(6, 1024)[5]]) for l in range(2)])
    A["w_in"] = both(I["w_in"], cols_i)
    A["qk_gain"] = np.stack([np.concatenate([np.tile(I["q_scale"][l], 8), np.tile(I["k_scale"][l], 2)]) for l in range(2)])
    A["sgu_g"], A["sgu_b"] = I["sgu_ln_g"], I["sgu_ln_b"]
    A["ln1_g"], A["ln1_b"], A["ln2_g"], A["ln2_b"] = I["ln1_g"], I["ln1_b"], I["ln2_g"], I["ln2_b"]
    A["w_sp"] = both(I["w_spatial"], lambda w: np.ascontiguousarray(w.transpose(2, 0, 1)).reshape(128, 1024))
    A["w_ba"] = both(I["w_branch_a"], lambda w: cols_s(w, 512))
    A["w_bb"] = both(I["w_branch_b"], lambda w: cols_s(w, 512))
    A["w_out"] = both(I["w_out"], cols_s)
    A["router_w"] = I["router_w"].reshape(2, 128, 512)
    A["router_b"] = I["router_bias"]
    A["w_gate"] = I["w_gate"].reshape(2, 64, 128, 2048)
    A["w_up"] = I["w_up"].reshape(2, 64, 128, 2048)
    A["w_down"] = I["w_down"]
    A["ws_gate"] = I["ws_gate"].reshape(2, 128, 2048)
    A["ws_up"] = I["ws_up"].reshape(2, 128, 2048)
    A["ws_down"] = I["ws_down"]
    A["ltri"] = np.tril(np.ones((8, 8), np.float32), -1).reshape(64)
    A["tri"] = np.concatenate([np.triu(np.ones((128, 128))), np.tile(np.arange(64.0), (128, 1))], 1).astype(np.float32)
    t = np.arange(256)
    row, col = (t // 64 - 2).astype(np.float32), (t % 64 - 32).astype(np.float32)
    inv = (np.float32(10000.0) ** (-np.arange(16, dtype=np.float32) / np.float32(16))).astype(np.float32)
    ang = np.concatenate([row[:, None] * inv, col[:, None] * inv], -1)
    c, s = np.cos(ang).astype(np.float32), np.sin(ang).astype(np.float32)
    C = np.repeat(c, 2, 1)
    Sg = np.stack([-s, s], -1).reshape(256, 64)
    A["rope1"] = np.ascontiguousarray(np.stack([C, Sg]).reshape(2, 2, 128, 64).transpose(2, 0, 1, 3)).reshape(128, 256)
    A.update(layout2(I))
    return A, off


def layout2(I):
    A = {}
    A["ada2"] = both(I["ada_w_2"], cols_i)
    A["ctx"] = I["ctx_2"].reshape(256, 1024)
    A["wqkv"] = cols_s(I["att_w_qkv_2"][0])
    A["gain2"] = np.concatenate([np.tile(I["att_q_gain_2"][0], 16), np.tile(I["att_k_gain_2"][0], 4)])
    A["sink"] = I["att_sink_2"][0]
    A["w_o"] = cols_s(I["att_w_o_2"][0])
    A["mlp1"] = both(I["mlp_w1_2"], cols_s)
    A["mlp2"] = both(I["mlp_w2_2"], lambda w: np.ascontiguousarray(
        w.reshape(2, 16, 128, 8, 128).transpose(3, 0, 2, 1, 4)).reshape(8, 2, 128, 2048))
    A["w_rkv"] = both(I["rwkv_w_rkv_2"][0], cols_s)
    w1 = I["rwkv_w1_2"][0]
    A["w1"] = cols_s(np.concatenate([w1[0], w1[1]], 1), 128)[0]
    A["w2"] = I["rwkv_w2_2"][0].reshape(128, 1024)
    A["a1"] = cols_s(I["rwkv_a1_2"][0], 64)[0]
    A["a2"] = np.concatenate([I["rwkv_a2_2"][0], I["rwkv_a2_2"][0]], 0)
    A["g1"] = both(I["rwkv_g1_2"][0], lambda w: cols_s(w, 128)[0])
    A["g2"] = I["rwkv_g2_2"][0]
    A["rw_o"] = cols_s(I["rwkv_w_o_2"][0])
    t = np.arange(256)
    inv = (np.float32(10000.0) ** (-np.arange(16, dtype=np.float32) / np.float32(16))).astype(np.float32)
    ar, ac = (t // 64).astype(np.float32)[:, None] * inv, (t % 64).astype(np.float32)[:, None] * inv
    C = np.concatenate([np.cos(ar), np.cos(ar), np.cos(ac), np.cos(ac)], 1)
    Sg = np.concatenate([-np.sin(ar), np.sin(ar), -np.sin(ac), np.sin(ac)], 1)
    A["rope2"] = np.ascontiguousarray(
        np.stack([C, Sg]).astype(np.float32).reshape(2, 2, 128, 64).transpose(2, 0, 1, 3)).reshape(128, 256)
    m = np.where(np.abs(t[:, None] - t[None, :]) <= 128, 0.0, -1e30).astype(np.float32)
    A["mask"] = np.ascontiguousarray(m.reshape(2, 128, 256).transpose(1, 0, 2)).reshape(128, 512)
    A["blockones"] = np.kron(np.eye(2), np.ones((64, 64))).astype(np.float32)
    i = np.arange(32)
    up, inc = (i[:, None] < i[None, :]).astype(np.float32), (i[:, None] <= i[None, :]).astype(np.float32)

    def half(m_):
        same = i[:, None] // (2 * m_) == i[None, :] // (2 * m_)
        return (same & (i[:, None] % (2 * m_) < m_) & (i[None, :] % (2 * m_) >= m_)).astype(np.float32)

    parts = []
    for d in range(2):
        f = (lambda x: x) if d == 0 else (lambda x: x.T)
        g = np.concatenate([f(up), f(inc)], 1)
        parts.append(np.tile(g, (4, 1)))
        parts.append(np.tile(f(up), (4, 1)))
        parts.append(np.tile(f(up).T, (4, 1)))
        parts.append(np.tile(f(half(1)), (4, 1)))
        for lev in range(5):
            parts.append(np.tile(f(half(2 ** lev)).T, (4, 1)))
    parts.append(np.tile(np.eye(32, dtype=np.float32), (4, 1)))
    A["scan_c"] = np.ascontiguousarray(np.concatenate(parts, 1).astype(np.float32))
    return A


def kernel(**inputs):
    import concourse.bacc as bacc
    from concourse.bass_utils import run_bass_kernel_spmd

    arrays, off = layout(inputs)
    nc = bacc.Bacc("TRN2", target_bir_lowering=False, num_devices=1)
    D, given = {}, {}
    for name, a in arrays.items():
        if name in ("w_down", "ws_down"):
            t = nc.dram_tensor("in_" + name, a.shape, F32, kind="ExternalInput").ap()
            D[name] = t.rearrange("l e (j p) d -> l e p j d", p=128) if name == "w_down" else t.rearrange("l (j p) d -> l p j d", p=128)
        else:
            D[name] = nc.dram_tensor("in_" + name, a.shape, F32, kind="ExternalInput").ap()
        given["in_" + name] = np.ascontiguousarray(a)
    D["voff"] = off
    out = nc.dram_tensor("out_x", (256, 1024), F32, kind="ExternalOutput").ap()
    program(nc, D, out)
    r = run_bass_kernel_spmd(nc, [given], core_ids=[0])
    return r.results[0]["out_x"].reshape(1, 256, 1024)
```
